# Optimizing a Trainium2 kernel written in Bass

```python
import jax, jax.numpy as jnp
from jax import lax
import numpy as np

D_MODEL = 2048
BATCH = 1
SEQ = 512
DEPTH = 1

HEAD_DIM = 64
ATTN_GROUPS = ((128, 1), (512, 4), (2048, 16))
N_ATTN_GROUPS = len(ATTN_GROUPS)
ATTN_HEADS_PER_GROUP = 8
ATTN_HEADS = N_ATTN_GROUPS * ATTN_HEADS_PER_GROUP
ATTN_WIDTH = ATTN_HEADS * HEAD_DIM
ATTN_OUT_WIDTH = ATTN_HEADS_PER_GROUP * HEAD_DIM
ALIBI_MAX_BIAS = 8.0
RWKV_HEADS = 16
RWKV_WIDTH = RWKV_HEADS * HEAD_DIM
DECAY_LORA = 64
ICLR_LORA = 64
GATE_LORA = 160
N_DIRS = 2
N_BRANCHES = 2
RWKV_IN_WIDTH = 3 * RWKV_WIDTH + DECAY_LORA + ICLR_LORA + GATE_LORA
IN_WIDTH = 3 * ATTN_WIDTH + RWKV_IN_WIDTH + N_BRANCHES * D_MODEL
FFN_HIDDEN = -(-8 * D_MODEL // (3 * 256)) * 256
RMS_EPS = 1e-6
GN_EPS = 64e-5
L2_EPS = 1e-12
NEG_INF = -1e30

kernel_name = 'hybrid_dilated_attn_rwkv7_swiglu'

def rms_norm(t, w, eps=RMS_EPS):
    tf = t.astype(jnp.float32)
    return tf * lax.rsqrt(jnp.mean(tf * tf, axis=-1, keepdims=True) + eps) * w.astype(jnp.float32)

def dilated_band_attention(q, k, v, dilation, half, slopes):
    b, s, h, e = q.shape
    n = s // dilation
    nb = -(-n // half)
    n_pad = nb * half

    def to_residue(t):
        return t.reshape(b, n, dilation, h, e).transpose(0, 2, 3, 1, 4)

    def band(t):
        tp = jnp.pad(t, ((0, 0), (0, 0), (0, 0), (half, n_pad - n + half), (0, 0)))
        tp = tp.reshape(b, dilation, h, nb + 2, half, e)
        return jnp.concatenate([tp[:, :, :, :-2], tp[:, :, :, 1:-1], tp[:, :, :, 2:]], axis=-2)

    qb = jnp.pad(to_residue(q), ((0, 0), (0, 0), (0, 0), (0, n_pad - n), (0, 0)))
    qb = qb.reshape(b, dilation, h, nb, half, e)
    kb = band(to_residue(k))
    vb = band(to_residue(v))

    q_idx = jnp.arange(nb)[:, None] * half + jnp.arange(half)[None, :]
    k_idx = jnp.arange(nb)[:, None] * half - half + jnp.arange(3 * half)[None, :]
    rel = k_idx[:, None, :] - q_idx[:, :, None]
    valid = (jnp.abs(rel) <= half) & (k_idx[:, None, :] >= 0) & (k_idx[:, None, :] < n)
    dist = (jnp.abs(rel) * dilation).astype(jnp.float32)

    scores = jnp.einsum('bdhnqe,bdhnke->bdhnqk', qb, kb)
    scores = scores - slopes[None, None, :, None, None, None] * dist
    scores = jnp.where(valid, scores, NEG_INF)
    m = jnp.max(scores, axis=-1, keepdims=True)
    p = jnp.exp(scores - m)
    den = jnp.sum(p, axis=-1, keepdims=True)
    out = jnp.einsum('bdhnqk,bdhnke->bdhnqe', p, vb) / den
    lse = (m + jnp.log(den))[..., 0]
    out = out.reshape(b, dilation, h, n_pad, e)[:, :, :, :n].transpose(0, 3, 1, 2, 4).reshape(b, s, h, e)
    lse = lse.reshape(b, dilation, h, n_pad)[:, :, :, :n].transpose(0, 3, 1, 2).reshape(b, s, h)
    return out, lse

def token_shift_centred(z, mu_prev, mu_next):
    z_prev = jnp.pad(z, ((0, 0), (1, 0), (0, 0)))[:, :-1]
    z_next = jnp.pad(z, ((0, 0), (0, 1), (0, 0)))[:, 1:]
    return z + mu_prev * (z_prev - z) + mu_next * (z_next - z)

def dir_stack(fwd, bwd):
    return jnp.stack([fwd, jnp.flip(bwd, axis=1)])

def rwkv7_bidir_scan(r, w, k, v, kk, a):
    def step(state, inp):
        r_t, w_t, k_t, v_t, kk_t, a_t = inp
        sa = jnp.einsum('zbhvk,zbhk->zbhv', state, -kk_t)
        state = (state * w_t[..., None, :] + sa[..., :, None] * (kk_t * a_t)[..., None, :]
                 + v_t[..., :, None] * k_t[..., None, :])
        y = jnp.einsum('zbhvk,zbhk->zbhv', state, r_t)
        return state, y
    xs = tuple(jnp.moveaxis(t, 2, 0) for t in (r, w, k, v, kk, a))
    init = jnp.zeros(r.shape[:2] + (RWKV_HEADS, HEAD_DIM, HEAD_DIM), jnp.float32)
    _, y = lax.scan(step, init, xs)
    return jnp.moveaxis(y, 0, 2)

def to_heads(t):
    return t.reshape(t.shape[:-1] + (RWKV_HEADS, HEAD_DIM))

def setup_inputs(seed: int = 0) -> dict:
    key = jax.random.key(seed)
    ks = jax.random.split(key, 26)
    f32 = jnp.float32

    def nrm(k, shape, scale):
        return jax.random.normal(k, shape, f32) * scale

    L, C = DEPTH, RWKV_WIDTH
    ramp = jnp.linspace(-6.0, -1.0, C, dtype=f32)
    return {
        'x': nrm(ks[0], (BATCH, SEQ, D_MODEL), 1.0),
        'norm1_w': 1.0 + nrm(ks[1], (L, D_MODEL), 0.05),
        'w_in': nrm(ks[2], (L, D_MODEL, IN_WIDTH), D_MODEL ** -0.5),
        'b_gate': nrm(ks[3], (L, N_BRANCHES, D_MODEL), 0.1),
        'q_norm_w': 1.0 + nrm(ks[4], (L, HEAD_DIM), 0.05),
        'k_norm_w': 1.0 + nrm(ks[5], (L, HEAD_DIM), 0.05),
        'shift_mu_prev': jax.random.uniform(ks[6], (L, RWKV_IN_WIDTH), f32, 0.0, 0.5),
        'shift_mu_next': jax.random.uniform(ks[7], (L, RWKV_IN_WIDTH), f32, 0.0, 0.5),
        'decay_w0': ramp + nrm(ks[8], (L, N_DIRS, C), 0.1),
        'decay_w2': nrm(ks[9], (L, N_DIRS, DECAY_LORA, C), 0.5 * DECAY_LORA ** -0.5),
        'iclr_a0': nrm(ks[10], (L, N_DIRS, C), 0.1),
        'iclr_a2': nrm(ks[11], (L, N_DIRS, ICLR_LORA, C), 0.5 * ICLR_LORA ** -0.5),
        'gate_g2': nrm(ks[12], (L, GATE_LORA, C), GATE_LORA ** -0.5),
        'k_k': 0.85 + nrm(ks[13], (L, C), 0.05),
        'k_a': 1.0 + nrm(ks[14], (L, C), 0.05),
        'r_k': nrm(ks[15], (L, RWKV_HEADS, HEAD_DIM), 0.1),
        'ln_x_w': 1.0 + nrm(ks[16], (L, C), 0.05),
        'ln_x_b': nrm(ks[17], (L, C), 0.02),
        'w_branch_attn': nrm(ks[18], (L, ATTN_OUT_WIDTH, D_MODEL), ATTN_OUT_WIDTH ** -0.5),
        'w_branch_rwkv': nrm(ks[19], (L, C, D_MODEL), C ** -0.5),
        'w_out': nrm(ks[20], (L, D_MODEL, D_MODEL), D_MODEL ** -0.5),
        'norm2_w': 1.0 + nrm(ks[21], (L, D_MODEL), 0.05),
        'w_ffn_gate': nrm(ks[22], (L, D_MODEL, FFN_HIDDEN), D_MODEL ** -0.5),
        'w_ffn_up': nrm(ks[23], (L, D_MODEL, FFN_HIDDEN), D_MODEL ** -0.5),
        'w_ffn_down': nrm(ks[24], (L, FFN_HIDDEN, D_MODEL), FFN_HIDDEN ** -0.5),
    }

def reference(x, norm1_w, w_in, b_gate, q_norm_w, k_norm_w, shift_mu_prev, shift_mu_next,
              decay_w0, decay_w2, iclr_a0, iclr_a2, gate_g2, k_k, k_a, r_k, ln_x_w, ln_x_b,
              w_branch_attn, w_branch_rwkv, w_out, norm2_w, w_ffn_gate, w_ffn_up, w_ffn_down):
    f32 = jnp.float32
    b, s, _ = x.shape
    slopes = jnp.exp2(-ALIBI_MAX_BIAS * jnp.arange(1, ATTN_HEADS + 1, dtype=f32) / ATTN_HEADS)
    slopes = slopes.reshape(N_ATTN_GROUPS, ATTN_HEADS_PER_GROUP)
    cuts = np.cumsum([3 * ATTN_WIDTH, RWKV_IN_WIDTH]).tolist()
    rwkv_cuts = np.cumsum([RWKV_WIDTH, RWKV_WIDTH, RWKV_WIDTH, DECAY_LORA, ICLR_LORA]).tolist()
    for layer in range(DEPTH):
        h_in = rms_norm(x, norm1_w[layer]).astype(x.dtype)
        z = h_in @ w_in[layer]
        z_attn, z_rwkv, z_gate = jnp.split(z, cuts, axis=-1)

        qkv = z_attn.astype(f32).reshape(b, s, 3, N_ATTN_GROUPS, ATTN_HEADS_PER_GROUP, HEAD_DIM)
        q = rms_norm(qkv[:, :, 0], q_norm_w[layer]) * HEAD_DIM ** -0.5
        kq = rms_norm(qkv[:, :, 1], k_norm_w[layer])
        va = qkv[:, :, 2]
        outs, lses = [], []
        for g, (window, dilation) in enumerate(ATTN_GROUPS):
            o_g, lse_g = dilated_band_attention(q[:, :, g], kq[:, :, g], va[:, :, g],
                                                dilation, window // (2 * dilation), slopes[g])
            outs.append(o_g)
            lses.append(lse_g)
        alpha = jax.nn.softmax(jnp.stack(lses), axis=0)
        o_attn = jnp.sum(alpha[..., None] * jnp.stack(outs), axis=0).reshape(b, s, ATTN_OUT_WIDTH)

        zr = token_shift_centred(z_rwkv.astype(f32), shift_mu_prev[layer], shift_mu_next[layer])
        r, k_raw, v_raw, w_lo, a_lo, g_lo = jnp.split(zr, rwkv_cuts, axis=-1)
        w_log = -jax.nn.softplus(-(decay_w0[layer][:, None, None, :]
                                   + jnp.einsum('bsr,zrc->zbsc', jnp.tanh(w_lo), decay_w2[layer]))) - 0.5
        decay = jnp.exp(-jnp.exp(w_log))
        iclr = jax.nn.sigmoid(iclr_a0[layer][:, None, None, :]
                              + jnp.einsum('bsr,zrc->zbsc', a_lo, iclr_a2[layer]))
        gate = jax.nn.sigmoid(g_lo) @ gate_g2[layer]
        kk = to_heads(k_raw * k_k[layer])
        kk = kk / jnp.maximum(jnp.sqrt(jnp.sum(kk * kk, axis=-1, keepdims=True)), L2_EPS)
        k_dir = to_heads(k_raw[None] * (1.0 + (iclr - 1.0) * k_a[layer]))
        r_h, v_h = to_heads(r), to_heads(v_raw)
        decay_h, iclr_h = to_heads(decay), to_heads(iclr)
        wkv = rwkv7_bidir_scan(dir_stack(r_h, r_h), dir_stack(decay_h[0], decay_h[1]),
                               dir_stack(k_dir[0], k_dir[1]), dir_stack(v_h, v_h),
                               dir_stack(kk, kk), dir_stack(iclr_h[0], iclr_h[1]))
        wkv = wkv[0] + jnp.flip(wkv[1], axis=1)
        mu = jnp.mean(wkv, axis=-1, keepdims=True)
        var = jnp.mean(jnp.square(wkv - mu), axis=-1, keepdims=True)
        gn = ((wkv - mu) * lax.rsqrt(var + GN_EPS)).reshape(b, s, RWKV_WIDTH) * ln_x_w[layer] + ln_x_b[layer]
        bonus = jnp.sum(jnp.sum(r_h[None] * k_dir * r_k[layer], axis=-1, keepdims=True) * v_h[None], axis=0)
        o_rwkv = (gn + bonus.reshape(b, s, RWKV_WIDTH)) * gate

        gates = jax.nn.sigmoid(z_gate.astype(f32).reshape(b, s, N_BRANCHES, D_MODEL) + b_gate[layer])
        branch_a = o_attn.astype(x.dtype) @ w_branch_attn[layer]
        branch_b = o_rwkv.astype(x.dtype) @ w_branch_rwkv[layer]
        merged = gates[:, :, 0] * branch_a + gates[:, :, 1] * branch_b
        x = x + merged.astype(x.dtype) @ w_out[layer]

        h2 = rms_norm(x, norm2_w[layer]).astype(x.dtype)
        hid = jax.nn.silu(h2 @ w_ffn_gate[layer]) * (h2 @ w_ffn_up[layer])
        x = x + hid @ w_ffn_down[layer]
    return x


_drawn_inputs = setup_inputs


def setup_inputs(seed=0):
    import zlib

    import numpy as np

    out = dict(_drawn_inputs(seed))
    spreads = {}
    factors = {'b_gate': 4.112,
     'q_norm_w': 8.0,
     'k_norm_w': 8.0,
     'decay_w2': 4.689,
     'iclr_a0': 4.052,
     'k_k': 4.098,
     'k_a': 2.991,
     'ln_x_w': 3.573,
     'ln_x_b': 8.0}
    for name, (base, spread) in spreads.items():
        noise = np.random.default_rng([zlib.crc32(name.encode()), seed]).standard_normal(out[name].shape)
        drawn = base * np.exp(spread * noise) if base else spread * noise
        out[name] = __import__('jax').numpy.asarray(drawn.astype(out[name].dtype))
    for name, factor in factors.items():
        out[name] = (out[name] * factor).astype(out[name].dtype)
    return out
```

```python
from contextlib import ExitStack

import numpy as np

import concourse.bass as bass
from concourse import mybir

F32 = mybir.dt.float32
F32R = mybir.dt.float32r
ALU = mybir.AluOpType
ACT = mybir.ActivationFunctionType
AX = mybir.AxisListType

P = 128
SEQ, D_MODEL = 512, 2048
TT = SEQ // P
KD = D_MODEL // P
HEAD_DIM = 64
ATTN_GROUPS = ((128, 1), (512, 4), (2048, 16))
ATTN_HPG = 8
ATTN_HEADS = 24
ATTN_WIDTH = ATTN_HEADS * HEAD_DIM
RW = 1024
NPAIR = RW // P
DECAY_LORA = ICLR_LORA = 64
GATE_LORA = 160
FFN = 5632
KF = FFN // P
RMS_EPS, GN_EPS, L2_EPS = 1e-6, 64e-5, 1e-12
COL_RKV = 3 * ATTN_WIDTH
COL_LORA = COL_RKV + 3 * RW
COL_G = COL_LORA + DECAY_LORA + ICLR_LORA
COL_GATES = COL_G + GATE_LORA
ROW_ATTN, ROW_RKV = 0, 3 * ATTN_WIDTH
ROW_SW = ROW_RKV + 3 * RW
ROW_IC = ROW_SW + 2 * RW
ROW_GATE = ROW_IC + 2 * RW
ROW_MIX = ROW_GATE + RW
ROW_KK = ROW_MIX + 2 * D_MODEL
ROW_END = ROW_KK + RW

PARAMS = {}
_at = 0
for _name, _n in (("norm1", 16), ("norm2", 16), ("b_gate", 32), ("mu_prev", 27), ("mu_next", 27),
                  ("qn", 1), ("kn", 1),
                  ("w0", 16), ("a0", 16), ("k_k", 8), ("k_a", 8), ("r_k", 8), ("lnw", 8), ("lnb", 8),
                  ("c_self", 27)):
    PARAMS[_name] = (_at, _n)
    _at += _n
N_PARAM = _at
N_PARAM_A = PARAMS["w0"][0]
N_PARAM_B = PARAMS["c_self"][0] - N_PARAM_A


class Shared:
    pass


def two_faced(nc, ctx, name, shape):
    with nc.sbuf_tensor(name + "_rounded", shape, F32R) as rounded:
        pass
    return rounded, ctx.enter_context(nc.sbuf_tensor(name + "_plain", shape, F32))


def weight_stream(nc, ctx, g, tag=""):
    g.w_raw = [ctx.enter_context(nc.sbuf_tensor(f"w_raw{s}{tag}", [P, KD, P], F32)) for s in range(2)]
    g.w_hi = [ctx.enter_context(nc.sbuf_tensor(f"w_hi{s}{tag}", [P, KD, P], F32R)) for s in range(2)]
    g.w_lo = [ctx.enter_context(nc.sbuf_tensor(f"w_lo{s}{tag}", [P, KD, P], F32R)) for s in range(2)]
    g.w_landed = [nc.alloc_semaphore(f"w_landed{s}{tag}") for s in range(2)]
    g.w_hi_ready = nc.alloc_semaphore(f"w_hi_ready{tag}")
    g.w_lo_ready = nc.alloc_semaphore(f"w_lo_ready{tag}")
    g.w_used = nc.alloc_semaphore(f"w_used{tag}")
    g.out_ready = nc.alloc_semaphore(f"out_ready{tag}")
    g.out_stored = [nc.alloc_semaphore(f"out_stored{s}{tag}") for s in range(2)]


class Step:

    def __init__(self, c, it=0, per=0, outer=0, outer_per=0, loads=0):
        self.c, self.it, self.per, self.outer, self.outer_per = c, it, per, outer, outer_per
        self.slot, self.loads = c % 2, loads

    def count(self, back=0):
        return self.outer * self.outer_per + self.it * self.per + (self.c - back + 1)

    def slot_count(self, back=0):
        return (self.outer * (8 * self.outer_per) + self.it * (8 * self.per)
                + 16 * ((self.c - back) // 2 + 1 + self.loads))


def load_slab(sp, g, n, parts):
    if n.c >= 2:
        sp.wait_ge(g.w_lo_ready, n.count(2))
    at = 0
    for i, (k, view) in enumerate(parts):
        ins = sp.dma_start(g.w_raw[n.slot][:, at:at + k, :], view)
        ins.then_inc(g.w_landed[n.slot], 16)
        at += k


def split_hi(act, g, n, k, dmas=None):
    act.wait_ge(g.w_landed[n.slot], n.slot_count() if dmas is None else dmas)
    if n.c >= 2:
        act.wait_ge(g.w_used, n.count(2))
    act.copy(g.w_hi[n.slot][:, 0:k, :], g.w_raw[n.slot][:, 0:k, :]).then_inc(g.w_hi_ready, 1)


def split_lo(pool, g, n, k):
    pool.wait_ge(g.w_hi_ready, n.count())
    if n.c >= 2:
        pool.wait_ge(g.w_used, n.count(2))
    pool.tensor_tensor(g.w_lo[n.slot][:, 0:k, :], g.w_raw[n.slot][:, 0:k, :],
                       g.w_hi[n.slot][:, 0:k, :].bitcast(F32), ALU.subtract).then_inc(g.w_lo_ready, 1)


def products(pe, g, n, ks, bank, hi, lo, start=True, stop=True):
    ins = None
    for j, (kw, ka) in enumerate(ks):
        wh, wl = g.w_hi[n.slot][:, kw, :], g.w_lo[n.slot][:, kw, :]
        pe.matmul(bank, wl, hi[:, ka, :], start=start and j == 0, stop=False)
        pe.matmul(bank, wh, lo[:, ka, :], start=False, stop=False)
        ins = pe.matmul(bank, wh, hi[:, ka, :], start=False, stop=stop and j == len(ks) - 1)
    return ins


def param(g, name, i=0, n=1):
    at = PARAMS[name][0] + i
    return g.params[:, at:at + n]


def phase_setup(nc, g, a, xt):
    with ExitStack() as ctx:
        sb = lambda n, s, d=F32: ctx.enter_context(nc.sbuf_tensor(n, s, d))
        ps = lambda n, s: ctx.enter_context(nc.psum_tensor(n, s, F32))
        sem = nc.alloc_semaphore
        x_tok = sb("x_tok", [P, TT, D_MODEL])
        sq = sb("sq", [P, D_MODEL])
        x_t = sb("x_t", [P, 4, SEQ])
        diag = sb("diag", [P, TT, P])
        rstd_all = sb("rstd_all", [P, SEQ])
        h_f32 = sb("h_f32", [P, 2, SEQ])
        rows_a = sb("rows_a", [P, P])
        rows_b = sb("rows_b", [P, P])
        ssq = sb("ssq", [P, TT])
        ms = sb("ms", [P, TT])
        neg_half = sb("neg_half", [P, TT])
        rstd = sb("rstd", [P, TT])
        ps_t = [ps(f"ps_t{i}", [P, SEQ]) for i in range(2)]
        ps_p = ps("ps_p", [P, SEQ])
        ps_r = ps("ps_r", [P, SEQ])
        x_landed, rows_landed = sem("x_landed"), sem("rows_landed")
        zeroed, const_ready, ssq_ready, ms_ready = sem("zeroed"), sem("const_ready"), sem("ssq_ready"), sem("ms_ready")
        rstd_ready, xn_ready, tr_done, hf_ready, hh_ready, hl_ready = (sem(n) for n in (
            "rstd_ready", "xn_ready", "tr_done", "hf_ready", "hh_ready", "hl_ready"))
        par_t, par_ready, xt_ready, spread, rstd_kept = (sem(n) for n in ("par_t", "par_ready", "xt_ready", "spread", "rstd_kept"))
        xt_stored = [sem(f"xt_stored{i}") for i in range(4)]
        ra, rb = PARAMS, N_PARAM_A
        row_loads = []

        def rows(name, src, n, lo_row=0):
            at = PARAMS[name][0] + lo_row
            t, at = (rows_a, at) if at < N_PARAM_A else (rows_b, at - N_PARAM_A)
            row_loads.append((t[at:at + n, :], src))

        rows("norm1", a["norm1_w"].rearrange("l (k p) -> (l k) p", p=P), 16)
        rows("norm2", a["norm2_w"].rearrange("l (k p) -> (l k) p", p=P), 16)
        rows("b_gate", a["b_gate"].rearrange("l b (k p) -> (l b k) p", p=P), 32)
        for nm, key in (("mu_prev", "shift_mu_prev"), ("mu_next", "shift_mu_next")):
            rows(nm, a[key][:, 0:26 * P].rearrange("l (k p) -> (l k) p", p=P), 26)
            at = PARAMS[nm][0] + 26
            row_loads.append((rows_a[at:at + 1, 0:32], a[key][:, 26 * P:26 * P + 32]))
        for nm, key in (("qn", "q_norm_w"), ("kn", "k_norm_w")):
            at = PARAMS[nm][0]
            for h in range(2):
                row_loads.append((rows_a[at:at + 1, 64 * h:64 * h + 64], a[key]))
        rows("w0", a["decay_w0"].rearrange("l z (k p) -> (l z k) p", p=P), 16)
        rows("a0", a["iclr_a0"].rearrange("l z (k p) -> (l z k) p", p=P), 16)
        for nm, key in (("k_k", "k_k"), ("k_a", "k_a"), ("lnw", "ln_x_w"), ("lnb", "ln_x_b")):
            rows(nm, a[key].rearrange("l (k p) -> (l k) p", p=P), 8)
        rows("r_k", a["r_k"].rearrange("l (k a) e -> (l k) (a e)", a=2), 8)
        nrow = len(row_loads)

        with nc.Block() as block:
            @block.sync
            def _(sp):
                for t in range(TT):
                    sp.dma_start(x_tok[:, t, :], a["x"][0, t * P:(t + 1) * P, :]).then_inc(x_landed, 16)
                sp.wait_ge(zeroed, 2)
                for dst, src in row_loads:
                    sp.dma_start(dst, src).then_inc(rows_landed, 16)
                for k in range(KD):
                    sp.wait_ge(xt_ready, k + 1)
                    sp.dma_start(xt[k * P:(k + 1) * P, :], x_t[:, k % 4, :]).then_inc(xt_stored[k % 4], 16)
                for i in range(4):
                    sp.wait_ge(xt_stored[i], 16 * (KD // 4))

            @block.gpsimd
            def _(pool):
                pool.memset(g.ident[:, :], 0.0).then_inc(const_ready, 1)
                pool.memset(g.head_ones[:, :], 1.0).then_inc(const_ready, 1)
                pool.memset(neg_half[:, :], -0.5).then_inc(const_ready, 1)
                pool.memset(g.all_ones[:, :], 1.0).then_inc(const_ready, 1)
                pool.wait_ge(const_ready, 4)
                pool.affine_select(out=g.ident[:, :], in_=g.ident[:, :], compare_op=ALU.not_equal, fill=1.0,
                                   base=0, pattern=[[-1, P]], channel_multiplier=1).then_inc(const_ready, 1)
                pool.affine_select(out=g.head_ones[:, 0:64], in_=g.head_ones[:, 0:64], compare_op=ALU.is_ge,
                                   fill=0.0, base=63, pattern=[[0, 64]], channel_multiplier=-1).then_inc(const_ready, 1)
                pool.affine_select(out=g.head_ones[:, 64:128], in_=g.head_ones[:, 64:128], compare_op=ALU.is_ge,
                                   fill=0.0, base=-64, pattern=[[0, 64]], channel_multiplier=1).then_inc(const_ready, 1)
                pool.wait_ge(ms_ready, 1)
                pool.tensor_tensor(rstd[:, :], ms[:, :], neg_half[:, :], ALU.pow).then_inc(rstd_ready, 1)
                for k in range(KD):
                    pool.wait_ge(hh_ready, k + 1)
                    pool.tensor_tensor(g.h_lo[:, k, :], h_f32[:, k % 2, :], g.h_hi[:, k, :].bitcast(F32),
                                       ALU.subtract).then_inc(hl_ready, 1)

            @block.scalar
            def _(act):
                for t in range(TT):
                    act.wait_ge(x_landed, 16 * TT)
                    act.activation(sq[:, :], x_tok[:, t, :], ACT.Square, accum_out=ssq[:, t:t + 1]).then_inc(ssq_ready, 1)
                    act.wait_ge(ssq_ready, t + 1)

                def keep(k):
                    act.wait_ge(tr_done, k + 1)
                    if k >= 4:
                        act.wait_ge(xt_stored[k % 4], 16 * (k // 4))
                        act.wait_ge(hf_ready, k - 3)
                    act.copy(x_t[:, k % 4, :], ps_t[k % 2][:, :]).then_inc(xt_ready, 1)
                keep(0)
                keep(1)
                for k in range(KD):
                    if k + 2 < KD:
                        keep(k + 2)
                    act.wait_ge(hf_ready, k + 1)
                    act.copy(g.h_hi[:, k, :], h_f32[:, k % 2, :]).then_inc(hh_ready, 1)

            @block.tensor
            def _(pe):
                pe.wait_ge(const_ready, 5)
                pe.wait_ge(x_landed, 16 * TT)
                for k in range(KD):
                    if k == 2:
                        pe.wait_ge(rows_landed, 16 * nrow)
                        pe.transpose(ps_p[:, 0:P], rows_a[:, :], g.ident[:, :])
                        pe.transpose(ps_p[:, P:2 * P], rows_b[:, :], g.ident[:, :]).then_inc(par_t, 1)
                        pe.wait_ge(xn_ready, TT)
                        for t in range(TT):
                            ins = pe.matmul(ps_r[:, t * P:(t + 1) * P], g.all_ones[:, :], diag[:, t, :], start=True, stop=True)
                        ins.then_inc(spread, 1)
                    if k >= 2:
                        pe.wait_ge(xt_ready, k - 1)
                    for t in range(TT):
                        ins = pe.transpose(ps_t[k % 2][:, t * P:(t + 1) * P], x_tok[:, t, k * P:(k + 1) * P], g.ident[:, :])
                    ins.then_inc(tr_done, 1)

            @block.vector
            def _(dve):
                dve.memset(rows_a[:, :], 0.0).then_inc(zeroed, 1)
                dve.memset(rows_b[:, :], 0.0).then_inc(zeroed, 1)
                dve.wait_ge(ssq_ready, TT)
                dve.tensor_scalar(ms[:, :], ssq[:, :], 1.0 / D_MODEL, RMS_EPS, ALU.mult, ALU.add).then_inc(ms_ready, 1)
                dve.wait_ge(rstd_ready, 1)
                dve.wait_ge(const_ready, 5)
                for t in range(TT):
                    dve.tensor_scalar(diag[:, t, :], g.ident[:, :], rstd[:, t:t + 1], None, ALU.mult).then_inc(xn_ready, 1)
                dve.wait_ge(par_t, 1)
                dve.tensor_copy(g.params[:, 0:N_PARAM_A], ps_p[:, 0:N_PARAM_A]).then_inc(par_ready, 1)
                dve.tensor_copy(g.params[:, N_PARAM_A:N_PARAM_A + N_PARAM_B], ps_p[:, P:P + N_PARAM_B]).then_inc(par_ready, 1)
                dve.wait_ge(par_ready, 2)
                dve.tensor_tensor(param(g, "c_self", 0, 27), param(g, "mu_prev", 0, 27), param(g, "mu_next", 0, 27),
                                  ALU.add).then_inc(par_ready, 1)
                dve.wait_ge(par_ready, 3)
                dve.tensor_scalar(param(g, "c_self", 0, 27), param(g, "c_self", 0, 27), -1.0, 1.0, ALU.mult,
                                  ALU.add).then_inc(par_ready, 1)
                dve.wait_ge(spread, 1)
                dve.tensor_copy(rstd_all[:, :], ps_r[:, :]).then_inc(rstd_kept, 1)
                dve.wait_ge(rstd_kept, 1)
                for k in range(KD):
                    dve.wait_ge(xt_ready, k + 1)
                    if k >= 2:
                        dve.wait_ge(hl_ready, k - 1)
                    dve.scalar_tensor_tensor(out=h_f32[:, k % 2, :], in0=x_t[:, k % 4, :], scalar=param(g, "norm1", k),
                                             in1=rstd_all[:, :], op0=ALU.mult, op1=ALU.mult).then_inc(hf_ready, 1)


def phase_project(nc, g, a, zt):
    w_in = a["w_in"].rearrange("l (k p) n -> (l p) k n", p=P)
    C0 = 3
    NA, NB, ND = 36, 24, 32
    SA0, SB0, SD0, SEND = C0, C0 + NA, C0 + NA + NB, C0 + NA + NB + ND
    UN = 4
    with ExitStack() as ctx:
        sb = lambda n, s, d=F32: ctx.enter_context(nc.sbuf_tensor(n, s, d))
        ps = lambda n, s: ctx.enter_context(nc.psum_tensor(n, s, F32))
        sem = nc.alloc_semaphore
        bank = [ps(f"bank{i}", [P, SEQ]) for i in range(2)]
        lbank = [ps(f"lbank{i}", [P, SEQ]) for i in range(2)]
        out = [sb(f"out{i}", [P, SEQ]) for i in range(2)]
        lout = [sb(f"lout{i}", [P, SEQ]) for i in range(2)]
        lora = sb("lora", [P, 3, SEQ])
        w2 = sb("w2", [P, 2, RW])
        g2 = sb("g2", [P, 2, RW])
        mix_ready, w2_landed, sem_c, lora_ready, lora_act, l_done, l_ev = (sem(n) for n in (
            "mix_ready", "w2_landed", "shift_chain", "lora_ready", "lora_act", "l_done", "l_ev"))
        l_stored = [sem(f"l_stored{i}") for i in range(2)]
        shifted = [0]

        def cols(c0):
            return w_in[:, :, c0:c0 + P]

        lora_jobs = []
        for z in range(2):
            for p in range(NPAIR):
                lora_jobs.append((ROW_SW + z * RW + p * P, "w", z, p))
                lora_jobs.append((ROW_IC + z * RW + p * P, "a", z, p))
        for p in range(NPAIR):
            lora_jobs.append((ROW_GATE + p * P, "g", 0, p))

        with nc.Block() as block:
            @block.sync
            def _(sp):
                for z in range(2):
                    sp.dma_start(w2[0:64, z, :], a["decay_w2"][0, z]).then_inc(w2_landed, 16)
                    sp.dma_start(w2[64:128, z, :], a["iclr_a2"][0, z]).then_inc(w2_landed, 16)
                sp.dma_start(g2[:, 0, :], a["gate_g2"][0, 0:P, :]).then_inc(w2_landed, 16)
                sp.dma_start(g2[0:32, 1, :], a["gate_g2"][0, P:GATE_LORA, :]).then_inc(w2_landed, 16)
                for c, c0 in enumerate((COL_LORA, COL_G, COL_G + P)):
                    load_slab(sp, g, Step(c), [(KD, cols(c0))])
                load_slab(sp, g, Step(SA0), [(KD, cols(0))])
                load_slab(sp, g, Step(SA0 + 1), [(KD, cols(P))])
                for j, (row, _, _, _) in enumerate(lora_jobs):
                    sp.wait_ge(l_ev, j + 1)
                    sp.dma_start(zt[row:row + P, :], lout[j % 2][:, :]).then_inc(l_stored[j % 2], 16)

                def turn(base, i, col0, row0, freed, counted, ahead):
                    for j in range(UN):
                        st = Step(base + j, i, UN)
                        if ahead[j] is not None:
                            load_slab(sp, g, Step(base + j + 2, i, UN), [(KD, ahead[j])])
                        sp.wait_ge(freed, st.count() - counted)
                        sp.dma_start(zt[bass.ds(i * (UN * P) + (row0 + j * P), P), :],
                                     out[st.slot][:, :]).then_inc(g.out_stored[st.slot], 16)

                def section(base, n, col0, row0, freed, counted, then):
                    with sp.Fori(0, n // UN - 1) as i:
                        turn(base, i, col0, row0, freed, counted,
                             [w_in[:, :, bass.ds(i * (UN * P) + (col0 + (j + 2) * P), P)] for j in range(UN)])
                    m = n - UN
                    turn(base + m, 0, col0 + m * P, row0 + m * P, freed, counted,
                         [cols(col0 + (m + j + 2) * P) for j in range(UN - 2)] + then)

                section(SA0, NA, 0, ROW_ATTN, g.out_ready, C0, [cols(COL_RKV), cols(COL_RKV + P)])
                section(SB0, NB, COL_RKV, ROW_RKV, g.out_ready, C0, [cols(COL_GATES), cols(COL_GATES + P)])
                section(SD0, ND, COL_GATES, ROW_MIX, mix_ready, SD0, [None, None])
                for s in range(2):
                    sp.wait_ge(g.out_stored[s], 16 * ((SEND - C0) // 2))
                    sp.wait_ge(l_stored[s], 16 * (len(lora_jobs) // 2))

            @block.scalar
            def _(act):
                for c in range(C0):
                    split_hi(act, g, Step(c), KD)
                act.wait_ge(lora_ready, 3)
                act.activation(lora[0:64, 0, :], lora[0:64, 0, :], ACT.Tanh).then_inc(lora_act, 1)
                act.activation(lora[:, 1, :], lora[:, 1, :], ACT.Sigmoid).then_inc(lora_act, 1)
                act.activation(lora[0:32, 2, :], lora[0:32, 2, :], ACT.Sigmoid).then_inc(lora_act, 1)
                split_hi(act, g, Step(SA0), KD)
                for j, (row, kind, z, p) in enumerate(lora_jobs):
                    act.wait_ge(l_done, j + 1)
                    if j >= 2:
                        act.wait_ge(l_stored[j % 2], 16 * (j // 2))
                    if kind == "g":
                        ins = act.copy(lout[j % 2][:, :], lbank[j % 2][:, :])
                    else:
                        ins = act.activation(lout[j % 2][:, :], lbank[j % 2][:, :], ACT.Sigmoid,
                                             bias=param(g, "w0" if kind == "w" else "a0", z * 8 + p))
                    ins.then_inc(l_ev, 1)
                for base, n in ((SA0, NA), (SB0, NB)):
                    with act.Fori(0, n // UN) as i:
                        for j in range(UN):
                            split_hi(act, g, Step(base + j + 1, i, UN), KD)

                def mix(st, row_tile):
                    act.wait_ge(g.w_used, st.count())
                    act.wait_ge(g.out_stored[st.slot], st.slot_count(2) - 16 * (C0 // 2 + (0 if st.slot else 1)))
                    act.activation(out[st.slot][:, :], bank[st.slot][:, :], ACT.Sigmoid, bias=row_tile).then_inc(mix_ready, 1)
                with act.Fori(0, ND // UN - 1) as i:
                    for j in range(UN):
                        split_hi(act, g, Step(SD0 + j + 1, i, UN), KD)
                        mix(Step(SD0 + j, i, UN), g.params[:, bass.ds(i * UN + (PARAMS["b_gate"][0] + j), 1)])
                for j in range(ND - UN, ND):
                    if j + 1 < ND:
                        split_hi(act, g, Step(SD0 + j + 1), KD)
                    mix(Step(SD0 + j), param(g, "b_gate", j))

            @block.gpsimd
            def _(pool):
                for c in range(C0):
                    split_lo(pool, g, Step(c), KD)
                with pool.Fori(0, (SEND - C0) // UN) as i:
                    for j in range(UN):
                        split_lo(pool, g, Step(C0 + j, i, UN), KD)

            @block.tensor
            def _(pe):
                for c in range(C0):
                    pe.wait_ge(g.w_lo_ready, c + 1)
                    if c >= 2:
                        pe.wait_ge(lora_ready, c - 1)
                    products(pe, g, Step(c), [(k, k) for k in range(KD)], bank[c % 2][:, :], g.h_hi, g.h_lo).then_inc(g.w_used, 1)
                pe.wait_ge(w2_landed, 16 * 6)
                pe.wait_ge(lora_act, 3)
                for j, (row, kind, z, p) in enumerate(lora_jobs):
                    if j >= 2:
                        pe.wait_ge(l_ev, j - 1)
                    o, c = lbank[j % 2][:, :], slice(p * P, (p + 1) * P)
                    if kind == "g":
                        pe.matmul(o, g2[:, 0, c], lora[:, 1, :], start=True, stop=False)
                        ins = pe.matmul(o, g2[0:32, 1, c], lora[0:32, 2, :], start=False, stop=True)
                    else:
                        r = slice(0, 64) if kind == "w" else slice(64, 128)
                        ins = pe.matmul(o, w2[r, z, c], lora[r, 0, :], start=True, stop=True)
                    ins.then_inc(l_done, 1)

                def one(st, freed, base):
                    pe.wait_ge(g.w_lo_ready, st.count())
                    if freed is not None:
                        pe.wait_ge(freed, st.count(2) - base)
                    products(pe, g, st, [(k, k) for k in range(KD)], bank[st.slot][:, :], g.h_hi, g.h_lo).then_inc(g.w_used, 1)
                pe.wait_ge(lora_ready, 3)
                for j in range(UN):
                    one(Step(C0 + j), None if j < 2 else g.out_ready, C0)
                with pe.Fori(0, (SD0 - C0) // UN - 1) as i:
                    for j in range(UN):
                        one(Step(C0 + UN + j, i, UN), g.out_ready, C0)
                for j in range(UN):
                    one(Step(SD0 + j), *((g.out_ready, C0) if j < 2 else (mix_ready, SD0)))
                with pe.Fori(0, ND // UN - 1) as i:
                    for j in range(UN):
                        one(Step(SD0 + UN + j, i, UN), mix_ready, SD0)

            @block.vector
            def _(dve):
                def shift(src, dst, ti, rows=P, it=None):
                    def pr(name):
                        if it is None:
                            return param(g, name, ti)[0:rows, :]
                        return g.params[0:rows, bass.ds(it * UN + (PARAMS[name][0] + ti), 1)]
                    base = shifted[0]
                    s = src[0:rows, :]
                    dve.tensor_scalar(dst[0:rows, :], s, pr("c_self"), None, ALU.mult).then_inc(sem_c, 1)
                    cnt = (lambda k: base + k) if it is None else (lambda k: it * (2 * UN) + (base + k))
                    dve.wait_ge(sem_c, cnt(1))
                    dve.scalar_tensor_tensor(out=dst[0:rows, 1:SEQ], in0=src[0:rows, 0:SEQ - 1], scalar=pr("mu_prev"),
                                             in1=dst[0:rows, 1:SEQ], op0=ALU.mult, op1=ALU.add).then_inc(sem_c, 1)
                    dve.wait_ge(sem_c, cnt(2))
                    shifted[0] += 2
                    return dve.scalar_tensor_tensor(out=dst[0:rows, 0:SEQ - 1], in0=src[0:rows, 1:SEQ], scalar=pr("mu_next"),
                                                    in1=dst[0:rows, 0:SEQ - 1], op0=ALU.mult, op1=ALU.add)

                for c, rows in enumerate((P, P, 32)):
                    dve.wait_ge(g.w_used, c + 1)
                    shift(bank[c % 2], lora[:, c, :], 24 + c, rows).then_inc(lora_ready, 1)

                def slot_free(st):
                    dve.wait_ge(g.out_stored[st.slot], st.slot_count(2) - 16 * (C0 // 2 + (0 if st.slot else 1)))

                def plain(st, first=False):
                    dve.wait_ge(g.w_used, st.count())
                    if not first:
                        slot_free(st)
                    dve.tensor_copy(out[st.slot][:, :], bank[st.slot][:, :]).then_inc(g.out_ready, 1)
                for j in range(UN):
                    plain(Step(SA0 + j), first=j < 2)
                with dve.Fori(0, NA // UN - 1) as i:
                    for j in range(UN):
                        plain(Step(SA0 + UN + j, i, UN))
                with dve.Fori(0, NB // UN) as i:
                    for j in range(UN):
                        st = Step(SB0 + j, i, UN)
                        dve.wait_ge(g.w_used, st.count())
                        slot_free(st)
                        shift(bank[st.slot], out[st.slot], j, it=i).then_inc(g.out_ready, 1)
    g.next_step = SEND



CH = 64
NCH = SEQ // CH
NQ = 4
LEVELS = 5
DECAY_SCALE = float(np.exp(np.float64(-0.5)))

SCAN_STAGES = ([("ab0", 0, "dve"), ("ab1", 1, "dve"), ("ak0", 2, "dve"), ("ak1", 3, "dve"), ("mab", 0, "dve"),
                ("ta", 1, "act"), ("tb", 2, "act"), ("tk", 3, "act"), ("tv", 1, "act"), ("mkv", 2, "act")]
               + [s for l in range(1, LEVELS + 1) for s in
                  [(f"z{l}", 0, "act"), (f"u{l}", 3, "dve")] + ([(f"x{l}", 1, "act")] if l < LEVELS else [])]
               + [("pt", 1, "act"), ("sa", 2, "dve"), ("y", 3, "act"), ("tn", 0, "dve")])
SCAN_NAMES = [s[0] for s in SCAN_STAGES]
N_PE = len(SCAN_STAGES)
N_EV = {e: sum(s[2] == e for s in SCAN_STAGES) for e in ("dve", "act")}


def made(name):
    return SCAN_NAMES.index(name) + 1


def taken(name):
    e = SCAN_STAGES[SCAN_NAMES.index(name)][2]
    return e, sum(s[2] == e for s in SCAN_STAGES[:SCAN_NAMES.index(name) + 1])


def bank_before(name):
    i = SCAN_NAMES.index(name)
    prev = [s[0] for s in SCAN_STAGES[:i] if s[1] == SCAN_STAGES[i][1]]
    return prev[-1] if prev else None


def phase_scan(nc, g, zt, yt):
    with ExitStack() as ctx:
        sb = lambda n, s, d=F32: ctx.enter_context(nc.sbuf_tensor(n, s, d))
        sem = nc.alloc_semaphore
        S2, H2 = range(2), range(2)
        bank = [[ctx.enter_context(nc.psum_tensor(f"sbank{s}{b}", [P, NQ, P], F32)) for b in range(4)] for s in S2]
        r_in, k_in, kk_in, sw_in, ic_in = ([[sb(f"{n}{s}{h}", [P, NQ, CH]) for h in H2] for s in S2]
                                           for n in ("r_in", "k_in", "kk_in", "sw_in", "ic_in"))
        v_bd = [[sb(f"v_bd{s}{h}", [P, NQ, P]) for h in H2] for s in S2]
        ar_bd = [[sb(f"ar_bd{s}{h}", [P, NQ, 2 * P]) for h in H2] for s in S2]
        b_bd = [[sb(f"b_bd{s}{h}", [P, NQ, P]) for h in H2] for s in S2]
        k_bd = [[sb(f"k_bd{s}{h}", [P, NQ, P]) for h in H2] for s in S2]
        g_end = [[sb(f"g_end{s}{h}", [P, NQ]) for h in H2] for s in S2]
        state = [[sb(f"state{s}{h}", [P, NQ, P]) for h in H2] for s in S2]
        y_sb = [[sb(f"y_sb{s}{h}", [P, NQ, CH]) for h in H2] for s in S2]
        lw, cum, ex, e_in, e_inv, e_ex, kd, b0 = ([sb(f"{n}{s}", [P, NQ, CH]) for s in S2]
                                                  for n in ("lw", "cum", "ex", "e_in", "e_inv", "e_ex", "kd", "b0"))
        ab = [sb(f"ab{s}", [P, NQ, 2 * P]) for s in S2]
        ak = [sb(f"ak{s}", [P, NQ, 2 * P]) for s in S2]
        m_ab, xt, x, z, a_t, b_t, k_t, v_t, mkv, pt, sa, tn = (
            [sb(f"{n}{s}", [P, NQ, P]) for s in S2]
            for n in ("m_ab", "xt", "x", "z", "a_t", "b_t", "k_t", "v_t", "mkv", "pt", "sa", "tn"))
        m_lvl = [[sb(f"m_lvl{s}{i}", [P, NQ, P]) for i in range(2)] for s in S2]
        seg = sb("seg", [P, NQ * CH])
        tri = [sb(f"tri{s}", [P, 2 * P]) for s in S2]
        same = sb("same", [P, LEVELS + 2, P])
        lvl = sb("lvl", [P, LEVELS + 1, P])
        landed = [[sem(f"in_landed{s}{h}") for h in H2] for s in S2]
        v_landed = [[sem(f"v_landed{s}{h}") for h in H2] for s in S2]
        prep_chain = [sem(f"prep_chain{s}") for s in S2]
        exp_in, exp_done, prep_ready = ([sem(f"{n}{s}") for s in S2] for n in ("exp_in", "exp_done", "prep_ready"))
        pe_done = [sem(f"scan_made{s}") for s in S2]
        taken_by = {e: [sem(f"taken_{e}{s}") for s in S2] for e in ("dve", "act")}
        pool_done = [sem(f"pool_done{s}") for s in S2]
        y_stored = [[sem(f"y_stored{s}{h}") for h in H2] for s in S2]
        tn_added = [sem(f"tn_added{s}") for s in S2]
        consts, zeroed = sem("scan_consts"), sem("scan_zeroed")
        N_POOL = 2 + LEVELS

        def chunk_start(s, i):
            return i * CH if s == 0 else i * (-CH) + (SEQ - CH)

        def wait_taken(eng, s, it, *names):
            need = {}
            for n in names:
                e, c = taken(n)
                need[e] = max(need.get(e, 0), c)
            for e, c in need.items():
                eng.wait_ge(taken_by[e][s], it * N_EV[e] + c)

        with nc.Block() as block:
            @block.gpsimd
            def _(pool):
                pool.memset(seg[:, :], 1.0).then_inc(consts, 1)
                for s in S2:
                    pool.memset(tri[s][:, :], 1.0).then_inc(consts, 1)
                pool.memset(same[:, :, :], 1.0).then_inc(consts, 1)
                for s in S2:
                    for h in H2:
                        for t in (v_bd, ar_bd, b_bd, k_bd, state):
                            pool.memset(t[s][h][:, :, :], 0.0).then_inc(zeroed, 1)
                pool.wait_ge(consts, 4)
                sv = seg[:, :].rearrange("p (q c) -> p q c", c=CH)
                pool.affine_select(out=sv, in_=sv, compare_op=ALU.not_equal, fill=0.0, base=0,
                                   pattern=[[0, NQ], [1, CH]], channel_multiplier=0).then_inc(consts, 1)
                for s in S2:
                    sign = 1 if s == 0 else -1
                    for j, op in enumerate((ALU.is_gt, ALU.is_ge)):
                        v = tri[s][:, j * P:(j + 1) * P]
                        pool.affine_select(out=v, in_=v, compare_op=op, fill=0.0, base=0,
                                           pattern=[[sign, P]], channel_multiplier=-sign).then_inc(consts, 1)
                for l in range(LEVELS + 2):
                    b = 1 << l
                    v = same[:, l, :].rearrange("p (n b) -> p n b", b=b)
                    pool.affine_select(out=v, in_=v, compare_op=ALU.is_ge, fill=0.0, base=0,
                                       pattern=[[-b, P // b], [0, b]], channel_multiplier=1).then_inc(consts, 1)
                pool.wait_ge(consts, 9 + LEVELS + 2)
                for l in range(LEVELS + 2):
                    b = 1 << l
                    v = same[:, l, :].rearrange("p (n b) -> p n b", b=b)
                    pool.affine_select(out=v, in_=v, compare_op=ALU.is_ge, fill=0.0, base=b - 1,
                                       pattern=[[b, P // b], [0, b]], channel_multiplier=-1).then_inc(consts, 1)
                pool.wait_ge(consts, 9 + 2 * (LEVELS + 2))
                pool.tensor_tensor(lvl[:, :, :], same[:, 1:LEVELS + 2, :], same[:, 0:LEVELS + 1, :],
                                   ALU.subtract).then_inc(consts, 1)
                pool.wait_ge(consts, 10 + 2 * (LEVELS + 2))

                def lmask(l):
                    return lvl[:, l:l + 1, :].broadcast_to([P, NQ, P])
                eye = g.ident[:, :].unsqueeze(1).broadcast_to([P, NQ, P])
                with pool.Fori(0, NCH) as i:
                    for h in H2:
                        it = i * 2 + h
                        for s in S2:
                            wait_taken(pool, s, it, "ab1")
                            pool.tensor_tensor(xt[s][:, :, :], ab[s][:, :, 0:P], lmask(0), ALU.mult).then_inc(pool_done[s], 1)
                            wait_taken(pool, s, it, "mab")
                            pool.tensor_tensor(x[s][:, :, :], m_ab[s][:, :, :], lmask(0), ALU.mult).then_inc(pool_done[s], 1)
                            pool.wait_ge(pool_done[s], it * (N_POOL + 2) + 2)
                            pool.tensor_tensor(xt[s][:, :, :], xt[s][:, :, :], eye, ALU.add).then_inc(pool_done[s], 1)
                            pool.tensor_tensor(x[s][:, :, :], x[s][:, :, :], eye, ALU.add).then_inc(pool_done[s], 1)
                        for l in range(1, LEVELS + 1):
                            for s in S2:
                                if l > 2:
                                    pool.wait_ge(pe_done[s], it * N_PE + made(f"z{l - 2}"))
                                pool.tensor_tensor(m_lvl[s][l % 2][:, :, :], m_ab[s][:, :, :], lmask(l),
                                                   ALU.mult).then_inc(pool_done[s], 1)

            @block.sync
            def _(sp):
                sp.wait_ge(zeroed, 20)

                def load(s, h, at):
                    rows = lambda base: zt[base + h * (NQ * P):base + (h + 1) * (NQ * P), bass.ds(at, CH)].rearrange("(q p) c -> p q c", p=P)
                    for dst, base in ((r_in, ROW_RKV), (k_in, ROW_RKV + RW), (kk_in, ROW_KK),
                                      (sw_in, ROW_SW + s * RW), (ic_in, ROW_IC + s * RW)):
                        sp.dma_start(dst[s][h][:, :, :], rows(base)).then_inc(landed[s][h], 16)
                    v = rows(ROW_RKV + 2 * RW)
                    for e in range(2):
                        sp.dma_start(v_bd[s][h][64 * e:64 * e + 64, :, 64 * e:64 * e + 64],
                                     v[64 * e:64 * e + 64]).then_inc(v_landed[s][h], 16)

                def store(s, h, i, at):
                    sp.wait_ge(taken_by["act"][s], i * (2 * N_EV["act"]) + (h * N_EV["act"] + taken("y")[1]))
                    sp.dma_start(yt[s, h * NQ * P:(h + 1) * NQ * P, bass.ds(at, CH)].rearrange("(q p) c -> p q c", p=P),
                                 y_sb[s][h][:, :, :]).then_inc(y_stored[s][h], 16)
                for h in H2:
                    for s in S2:
                        load(s, h, chunk_start(s, 0))
                with sp.Fori(0, NCH - 1) as i:
                    now = [sp.snap(chunk_start(s, i)) for s in S2]
                    ahead = [sp.snap(chunk_start(s, i + 1)) for s in S2]
                    for h in H2:
                        for s in S2:
                            sp.wait_ge(pe_done[s], i * (2 * N_PE) + (h * N_PE + made("tv")))
                            load(s, h, ahead[s])
                        for s in S2:
                            store(s, h, i, now[s])
                for h in H2:
                    for s in S2:
                        store(s, h, NCH - 1, chunk_start(s, NCH - 1))
                for s in S2:
                    for h in H2:
                        sp.wait_ge(y_stored[s][h], 16 * NCH)

            @block.scalar
            def _(act):
                with act.Fori(0, NCH) as i:
                    for h in H2:
                        it = i * 2 + h
                        for s in S2:
                            act.wait_ge(exp_in[s], it + 1)
                            act.activation(e_in[s][:, :, :], cum[s][:, :, :], ACT.Exp)
                            act.activation(e_inv[s][:, :, :], cum[s][:, :, :], ACT.Exp, scale=-1.0)
                            act.activation(e_ex[s][:, :, :], ex[s][:, :, :], ACT.Exp)
                            last = CH - 1 if s == 0 else 0
                            act.activation(g_end[s][h][:, :], cum[s][:, :, last], ACT.Exp).then_inc(exp_done[s], 1)
                        for name, b, e in SCAN_STAGES:
                            if e != "act":
                                continue
                            for s in S2:
                                act.wait_ge(pe_done[s], it * N_PE + made(name))
                                src = bank[s][b]
                                if name == "y":
                                    act.wait_ge(y_stored[s][h], i * 16)
                                    act.copy(y_sb[s][h][0:64, :, :], src[0:64, :, 0:64])
                                    act.copy(y_sb[s][h][64:128, :, :], src[64:128, :, 64:128]).then_inc(taken_by["act"][s], 1)
                                else:
                                    dst = {"ta": a_t, "tb": b_t, "tk": k_t, "tv": v_t, "mkv": mkv, "pt": pt}.get(name)
                                    dst = dst or (z if name[0] == "z" else x)
                                    act.copy(dst[s][:, :, :], src[:, :, :]).then_inc(taken_by["act"][s], 1)

            @block.vector
            def _(dve):
                dve.wait_ge(consts, 10 + 2 * (LEVELS + 2))
                dve.wait_ge(zeroed, 20)
                with dve.Fori(0, NCH) as i:
                    for h in H2:
                        it = i * 2 + h
                        for s in S2:
                            PC = 5 + s
                            pc = lambda c: it * PC + c
                            W = lambda t: t[:, :, :]
                            dve.wait_ge(landed[s][h], i * 80 + 80)
                            dve.tensor_scalar(W(lw[s]), W(sw_in[s][h]), -DECAY_SCALE, None, ALU.mult).then_inc(prep_chain[s], 1)
                            ka = param(g, "k_a", h * NQ, NQ).unsqueeze(2).broadcast_to([P, NQ, CH])
                            dve.scalar_tensor_tensor(out=W(kd[s]), in0=W(ic_in[s][h]), scalar=-1.0, in1=ka,
                                                     op0=ALU.add, op1=ALU.mult).then_inc(prep_chain[s], 1)
                            dve.wait_ge(prep_chain[s], pc(1))
                            dve.tensor_tensor_scan(cum[s][:, :, :].rearrange("p q c -> p (q c)"), seg[:, :],
                                                   lw[s][:, :, :].rearrange("p q c -> p (q c)"), 0.0,
                                                   ALU.mult, ALU.add).then_inc(prep_chain[s], 1)
                            dve.tensor_tensor(W(b0[s]), W(kk_in[s][h]), W(ic_in[s][h]), ALU.mult).then_inc(prep_chain[s], 1)
                            dve.wait_ge(prep_chain[s], pc(3))
                            if s == 0:
                                dve.tensor_tensor(W(ex[s]), W(cum[s]), W(lw[s]), ALU.subtract).then_inc(exp_in[s], 1)
                            else:
                                total = cum[s][:, :, CH - 1:CH].broadcast_to([P, NQ, CH])
                                dve.tensor_tensor(W(ex[s]), total, W(cum[s]), ALU.subtract).then_inc(prep_chain[s], 1)
                                dve.wait_ge(prep_chain[s], pc(5))
                                dve.tensor_tensor(W(cum[s]), W(ex[s]), W(lw[s]), ALU.add).then_inc(exp_in[s], 1)
                            dve.scalar_tensor_tensor(out=W(kd[s]), in0=W(kd[s]), scalar=1.0, in1=W(k_in[s][h]),
                                                     op0=ALU.add, op1=ALU.mult).then_inc(prep_chain[s], 1)
                        for s in S2:
                            dve.wait_ge(exp_done[s], it + 1)
                            dve.wait_ge(prep_chain[s], it * (5 + s) + (5 + s))
                            ar, bb, kb = ar_bd[s][h], b_bd[s][h], k_bd[s][h]
                            for e in range(2):
                                r, c = slice(64 * e, 64 * e + 64), slice(64 * e, 64 * e + 64)
                                c2 = slice(P + 64 * e, P + 64 * e + 64)
                                dve.scalar_tensor_tensor(out=ar[r, :, c], in0=kk_in[s][h][r], scalar=-1.0, in1=e_ex[s][r],
                                                         op0=ALU.mult, op1=ALU.mult)
                                dve.tensor_tensor(ar[r, :, c2], r_in[s][h][r], e_in[s][r], ALU.mult)
                                dve.tensor_tensor(bb[r, :, c], b0[s][r], e_inv[s][r], ALU.mult)
                                ins = dve.tensor_tensor(kb[r, :, c], kd[s][r], e_inv[s][r], ALU.mult)
                            ins.then_inc(prep_ready[s], 1)
                        for name, b, e in SCAN_STAGES:
                            if e != "dve":
                                continue
                            for s in S2:
                                src = bank[s][b]
                                dve.wait_ge(pe_done[s], it * N_PE + made(name))
                                if name in ("ab0", "ab1", "ak0", "ak1"):
                                    dst, q = (ab if name[1] == "b" else ak)[s], 2 * int(name[2])
                                    dve.tensor_tensor(dst[:, q:q + 2, :], src[:, :, :].rearrange("p (a b) c -> p a (b c)", b=2),
                                                      tri[s][:, :].unsqueeze(1).broadcast_to([P, 2, 2 * P]), ALU.mult).then_inc(taken_by["dve"][s], 1)
                                elif name == "mab":
                                    dve.tensor_tensor(m_ab[s][:, :, :], src[:, :, :],
                                                      tri[1 - s][:, 0:P].unsqueeze(1).broadcast_to([P, NQ, P]), ALU.mult).then_inc(taken_by["dve"][s], 1)
                                elif name[0] == "u":
                                    dve.wait_ge(pool_done[s], it * (N_POOL + 2) + 4)
                                    dve.tensor_tensor(xt[s][:, :, :], xt[s][:, :, :], src[:, :, :], ALU.add).then_inc(taken_by["dve"][s], 1)
                                elif name == "sa":
                                    dve.tensor_copy(sa[s][:, :, :], src[:, :, :]).then_inc(taken_by["dve"][s], 1)
                                else:
                                    st = state[s][h]
                                    dve.tensor_tensor(tn[s][:, :, :], st[:, :, :], src[:, :, :], ALU.add).then_inc(tn_added[s], 1)
                                    dve.wait_ge(tn_added[s], it + 1)
                                    dve.tensor_tensor(st[:, :, :], tn[s][:, :, :], g_end[s][h][:, :].unsqueeze(2).broadcast_to([P, NQ, P]),
                                                      ALU.mult).then_inc(taken_by["dve"][s], 1)

            @block.tensor
            def _(pe):
                with pe.Fori(0, NCH) as i:
                    for h in H2:
                        it = i * 2 + h
                        for s in S2:
                            pe.wait_ge(taken_by["dve"][s], it * N_EV["dve"])
                            pe.wait_ge(taken_by["act"][s], it * N_EV["act"])
                        for name, b, _ in SCAN_STAGES:
                            for s in S2:
                                ar, bb, kb, vb, st = ar_bd[s][h], b_bd[s][h], k_bd[s][h], v_bd[s][h], state[s][h]
                                o = bank[s][b]
                                if bank_before(name):
                                    wait_taken(pe, s, it, bank_before(name))
                                mm = lambda q, lhs, rhs, start=True, stop=True: pe.matmul(o[:, q, :], lhs, rhs, start=start, stop=stop)
                                Q = range(NQ)
                                if name in ("ab0", "ab1", "ak0", "ak1"):
                                    pe.wait_ge(prep_ready[s], it + 1)
                                    w = bb if name[1] == "b" else kb
                                    for j in range(2):
                                        q = 2 * int(name[2]) + j
                                        ins = pe.matmul(o[:, 2 * j:2 * j + 2, :].rearrange("p a b -> p (a b)"), w[:, q, :], ar[:, q, :], start=True, stop=True)
                                elif name == "mab":
                                    for q in Q:
                                        ins = mm(q, ar[:, q, 0:P], bb[:, q, :])
                                elif name in ("ta", "tb", "tk", "tv"):
                                    if name == "tv":
                                        pe.wait_ge(v_landed[s][h], i * 32 + 32)
                                    src = {"ta": ar[:, :, 0:P], "tb": bb[:, :, :], "tk": kb[:, :, :], "tv": vb[:, :, :]}[name]
                                    for q in Q:
                                        ins = pe.transpose(o[:, q, :], src[:, q, :], g.ident[:, :])
                                elif name == "mkv":
                                    wait_taken(pe, s, it, "ak1", "tv")
                                    for q in Q:
                                        ins = mm(q, ak[s][:, q, 0:P], v_t[s][:, q, :])
                                elif name[0] == "z":
                                    l = int(name[1])
                                    pe.wait_ge(pool_done[s], it * (N_POOL + 2) + (4 + l))
                                    if l > 1:
                                        wait_taken(pe, s, it, f"u{l - 1}")
                                    for q in Q:
                                        ins = mm(q, m_lvl[s][l % 2][:, q, :], xt[s][:, q, :])
                                elif name[0] == "u":
                                    l = int(name[1])
                                    wait_taken(pe, s, it, f"z{l}", *([f"x{l - 1}"] if l > 1 else []))
                                    for q in Q:
                                        ins = mm(q, x[s][:, q, :], z[s][:, q, :])
                                elif name[0] == "x":
                                    wait_taken(pe, s, it, f"u{name[1]}")
                                    for q in Q:
                                        ins = pe.transpose(o[:, q, :], xt[s][:, q, :], g.ident[:, :])
                                elif name == "pt":
                                    wait_taken(pe, s, it, "ta", f"u{LEVELS}")
                                    for q in Q:
                                        ins = mm(q, a_t[s][:, q, :], xt[s][:, q, :])
                                elif name == "sa":
                                    wait_taken(pe, s, it, "mkv", "pt")
                                    for q in Q:
                                        mm(q, xt[s][:, q, :], mkv[s][:, q, :], True, False)
                                        ins = mm(q, pt[s][:, q, :], st[:, q, :], False, True)
                                elif name == "y":
                                    wait_taken(pe, s, it, "sa")
                                    for q in Q:
                                        mm(q, st[:, q, :], ar[:, q, P:2 * P], True, False)
                                        mm(q, v_t[s][:, q, :], ak[s][:, q, P:2 * P], False, False)
                                        ins = mm(q, sa[s][:, q, :], ab[s][:, q, P:2 * P], False, True)
                                else:
                                    for q in Q:
                                        mm(q, k_t[s][:, q, :], v_t[s][:, q, :], True, False)
                                        ins = mm(q, b_t[s][:, q, :], sa[s][:, q, :], False, True)
                                ins.then_inc(pe_done[s], 1)



def rsqrt_newton(eng_wait, dve, y, t, s):
    eng_wait(dve.reciprocal(y, y))
    eng_wait(dve.tensor_tensor(t, y, y, ALU.mult))
    eng_wait(dve.tensor_tensor(t, t, s, ALU.mult))
    eng_wait(dve.tensor_scalar(t, t, -0.5, 1.5, ALU.mult, ALU.add))


def phase_norms(nc, g, zt):
    loops = ((12, ROW_ATTN, ROW_ATTN, "qn"), (12, ROW_ATTN + ATTN_WIDTH, ROW_ATTN + ATTN_WIDTH, "kn"),
             (NPAIR, ROW_RKV + RW, ROW_KK, "k_k"))
    UN = 2
    with ExitStack() as ctx:
        sem = nc.alloc_semaphore
        R = range(UN)
        tin, sq, s_sb, y, t, o = ([ctx.enter_context(nc.sbuf_tensor(f"n_{n}{j}", [P, SEQ], F32)) for j in R]
                                  for n in ("tin", "sq", "s_sb", "y", "t", "o"))
        bank = [ctx.enter_context(nc.psum_tensor(f"n_bank{j}", [P, SEQ], F32)) for j in R]
        landed = [sem(f"n_landed{j}") for j in R]
        stored = [sem(f"n_stored{j}") for j in R]
        sq_ready, summed, s_ready, root, chain, done, wq = (sem(n) for n in (
            "n_sq_ready", "n_summed", "n_s_ready", "n_root", "n_chain", "n_done", "n_wq"))
        with nc.Block() as block:
            @block.sync
            def _(sp):
                base = 0
                for n, src, dst, _ in loops:
                    with sp.Fori(0, n // UN) as i:
                        for j in R:
                            c = base // UN
                            if base == 0:
                                sp.wait_ge(done, i * UN)
                            else:
                                sp.wait_ge(done, i * UN + base)
                            sp.dma_start(tin[j][:, :], zt[bass.ds(i * (UN * P) + (src + j * P), P), :]).then_inc(landed[j], 16)
                        for j in R:
                            sp.wait_ge(done, i * UN + (base + j + 1))
                            sp.dma_start(zt[bass.ds(i * (UN * P) + (dst + j * P), P), :], o[j][:, :]).then_inc(stored[j], 16)
                    base += n
                for j in R:
                    sp.wait_ge(stored[j], 16 * (base // UN))

            @block.scalar
            def _(act):
                base = 0
                for n, _, _, w in loops:
                    with act.Fori(0, n // UN) as i:
                        for j in R:
                            act.wait_ge(landed[j], i * 16 + (base // UN + 1) * 16)
                            scale = g.params[:, bass.ds(i * UN + (PARAMS["k_k"][0] + j), 1)] if w == "k_k" else 1.0
                            act.activation(sq[j][:, :], tin[j][:, :], ACT.Square, scale=scale).then_inc(sq_ready, 1)
                        for j in R:
                            act.wait_ge(s_ready, i * UN + (base + j + 1))
                            act.activation(y[j][:, :], s_sb[j][:, :], ACT.Sqrt).then_inc(root, 1)
                    base += n

            @block.tensor
            def _(pe):
                base = 0
                for n, _, _, _ in loops:
                    with pe.Fori(0, n // UN) as i:
                        for j in R:
                            pe.wait_ge(sq_ready, i * UN + (base + j + 1))
                            pe.matmul(bank[j][:, :], g.head_ones[:, :], sq[j][:, :], start=True, stop=True).then_inc(summed, 1)
                    base += n

            @block.vector
            def _(dve):
                dve.tensor_scalar(param(g, "qn"), param(g, "qn"), HEAD_DIM ** -0.5, None, ALU.mult).then_inc(wq, 1)
                dve.wait_ge(wq, 1)
                base = 0
                K = 5
                for n, _, _, w in loops:
                    with dve.Fori(0, n // UN) as i:
                        for j in R:
                            dve.wait_ge(summed, i * UN + (base + j + 1))
                            if w == "k_k":
                                dve.tensor_scalar(s_sb[j][:, :], bank[j][:, :], L2_EPS * L2_EPS, None, ALU.max).then_inc(s_ready, 1)
                            else:
                                dve.tensor_scalar(s_sb[j][:, :], bank[j][:, :], 1.0 / HEAD_DIM, RMS_EPS, ALU.mult, ALU.add).then_inc(s_ready, 1)
                        for j in R:
                            count = [0]

                            def link(ins):
                                ins.then_inc(chain, 1)
                                count[0] += 1
                                dve.wait_ge(chain, i * (UN * K) + ((base + j) * K + count[0]))
                            dve.wait_ge(root, i * UN + (base + j + 1))
                            rsqrt_newton(link, dve, y[j][:, :], t[j][:, :], s_sb[j][:, :])
                            link(dve.tensor_tensor(y[j][:, :], y[j][:, :], t[j][:, :], ALU.mult))
                            wt = g.params[:, bass.ds(i * UN + (PARAMS["k_k"][0] + j), 1)] if w == "k_k" else param(g, w)
                            if base // UN:
                                dve.wait_ge(stored[j], i * 16 + base // UN * 16)
                            else:
                                dve.wait_ge(stored[j], i * 16)
                            dve.scalar_tensor_tensor(out=o[j][:, :], in0=tin[j][:, :], scalar=wt, in1=y[j][:, :],
                                                     op0=ALU.mult, op1=ALU.mult).then_inc(done, 1)
                    base += n


def windows(t):
    return min(max(P * t - 64, 0), SEQ - 2 * P)


def phase_attention(nc, g, zt):
    U = [(gr, e) for gr in range(3) for e in range(2)]
    NU = len(U)
    NP = ATTN_HPG // 2
    with ExitStack() as ctx:
        sb = lambda n, s, d=F32: ctx.enter_context(nc.sbuf_tensor(n, s, d))
        sem = nc.alloc_semaphore
        q_sb, k_sb, v_sb = ([sb(f"{n}{i}", [P, SEQ]) for i in range(3)] for n in ("q_sb", "k_sb", "v_sb"))
        q_r, k_r, v_r = (sb(n, [P, SEQ]) for n in ("q_r", "k_r", "v_r"))
        v_tok = [sb(f"v_tok{i}", [P, 7 if i == 0 else 4, P]) for i in range(3)]
        dist = sb("dist", [P, 5, 2 * P])
        slope = sb("slope", [P, 3, ATTN_HPG])
        s_sb = [sb(f"s_sb{i}", [P, 4, 2 * P]) for i in range(2)]
        p_sb = [sb(f"p_sb{i}", [P, 4, 2 * P]) for i in range(2)]
        p_t = [sb(f"p_t{i}", [P, 8, P]) for i in range(2)]
        negmax = [sb(f"negmax{i}", [P, 4]) for i in range(2)]
        den = [sb(f"den{i}", [P, 4]) for i in range(2)]
        mx_all, dn_all = ([sb(f"{n}{i}", [P, ATTN_HPG, 4]) for i in range(3)] for n in ("mx_all", "dn_all"))
        u_all = [sb(f"u_all{i}", [P, NP, SEQ]) for i in range(3)]
        sel = sb("sel", [ATTN_HPG, ATTN_HPG, HEAD_DIM])
        sc_ps = [ctx.enter_context(nc.psum_tensor(f"sc_ps{i}", [P, 4, 2 * P], F32)) for i in range(2)]
        pt_ps = ctx.enter_context(nc.psum_tensor("pt_ps", [P, 8, P], F32))
        pv_ps = ctx.enter_context(nc.psum_tensor("pv_ps", [P, SEQ], F32))
        vt_ps = ctx.enter_context(nc.psum_tensor("vt_ps", [P, 4, P], F32))
        consts, dist_c, landed, vt_done, vt_taken, sc_done, biased, max_ready, neg_ready, exp_done, den_c, pt_done, pt_taken, pv_done, pv_taken, slopes_c, by_res = (
            sem(n) for n in ("a_consts", "a_dist", "a_landed", "vt_done", "vt_taken", "sc_done", "biased", "max_ready", "neg_ready",
                             "exp_done", "den_copied", "pt_done", "pt_taken", "pv_done", "pv_taken", "slopes_c", "by_residue"))

        def tokens(t, gr, i):
            if gr == 0:
                return t[:, i * P:(i + 1) * P]
            if gr == 1:
                return t.rearrange("p (m r) -> p r m", r=4)[:, i, :]
            return t[:, i * P:(i + 1) * P]

        def vstarts(gr):
            return [0, 64, 128, 192, 256, 320, 384] if gr == 0 else [P * i for i in range(4)]
        VT = [(gr, c) for gr in range(3) for c in range(2 if gr == 0 else 1)]
        with nc.Block() as block:
            @block.gpsimd
            def _(pool):
                for gr in range(3):
                    for h in range(ATTN_HPG):
                        v = -2.0 ** (-8.0 * (gr * ATTN_HPG + h + 1) / ATTN_HEADS)
                        pool.memset(slope[:, gr, h:h + 1], v).then_inc(slopes_c, 1)
                pool.memset(sel[:, :, :], 0.0).then_inc(consts, 1)
                pool.wait_ge(consts, 1)
                pool.affine_select(out=sel[:, :, :], in_=sel[:, :, :], compare_op=ALU.not_equal, fill=1.0, base=0,
                                   pattern=[[-1, ATTN_HPG], [0, HEAD_DIM]], channel_multiplier=1).then_inc(consts, 1)
                for j, (off, dil) in enumerate(((0, 1), (-64, 1), (-P, 1), (0, 4))):
                    n = 2 * P if j < 3 else P
                    pool.iota(dist[:, j, 0:n], base=off * dil, pattern=[[dil, n]], channel_multiplier=-dil,
                              allow_small_or_imprecise_dtypes=True).then_inc(consts, 1)
                pool.iota(dist[:, 4, 0:P], base=0, pattern=[[16, P]], channel_multiplier=-16,
                          allow_small_or_imprecise_dtypes=True).then_inc(consts, 1)
                pool.wait_ge(consts, 7)
                pool.wait_ge(dist_c, 2)
                FAR = 1e33
                for j, off in enumerate((0, -64, -P, 0)):
                    n = 2 * P if j < 3 else P
                    v = dist[:, j, 0:n]
                    for k, sg in enumerate((1, -1)):
                        pool.affine_select(out=v, in_=v, compare_op=ALU.is_ge, fill=FAR, base=64 + sg * off,
                                           pattern=[[sg, n]], channel_multiplier=-sg).then_inc(consts, 1)
                        pool.wait_ge(consts, 7 + 2 * j + k + 1)
                v = dist[:, 4, 0:P].rearrange("p (n b) -> p n b", b=32)
                pool.affine_select(out=v, in_=v, compare_op=ALU.is_ge, fill=FAR, base=0,
                                   pattern=[[-32, 4], [0, 32]], channel_multiplier=1).then_inc(consts, 1)
                pool.wait_ge(consts, 16)
                pool.affine_select(out=v, in_=v, compare_op=ALU.is_ge, fill=FAR, base=31,
                                   pattern=[[32, 4], [0, 32]], channel_multiplier=-1).then_inc(consts, 1)

            @block.sync
            def _(sp):
                with sp.Fori(0, NP) as j:
                    sp.wait_ge(sc_done, j * NU)
                    for gr in range(3):
                        for dst, base in ((q_sb, 0), (k_sb, ATTN_WIDTH), (v_sb, 2 * ATTN_WIDTH)):
                            row = j * P + (ROW_ATTN + base + gr * ATTN_HPG * HEAD_DIM)
                            sp.dma_start(dst[gr][:, :], zt[bass.ds(row, P), :]).then_inc(landed, 16)

            @block.tensor
            def _(pe):
                pe.wait_ge(consts, 17)
                with pe.Fori(0, NP) as j:
                    pe.wait_ge(landed, j * 144 + 144)
                    pe.wait_ge(by_res, j * 3 + 3)
                    for n, (gr, c) in enumerate(VT):
                        pe.wait_ge(vt_taken, j * len(VT) + n)
                        starts = vstarts(gr)[4 * c:4 * c + 4]
                        for b, st in enumerate(starts):
                            src = v_sb[gr][:, st:st + P] if gr == 0 else tokens((v_sb[1], v_r)[gr - 1][:, :], gr, st // P)
                            ins = pe.transpose(vt_ps[:, b, :], src, g.ident[:, :])
                        ins.then_inc(vt_done, 1)

                    def scores(u):
                        gr, e = U[u]
                        r = slice(64 * e, 64 * e + 64)
                        if u >= 2:
                            pe.wait_ge(biased, j * NU + (u - 1))
                        for t in range(4):
                            if gr == 0:
                                w = windows(t)
                                ins = pe.matmul(sc_ps[u % 2][:, t, :], q_sb[0][r, t * P:(t + 1) * P],
                                                k_sb[0][r, w:w + 2 * P], start=True, stop=True)
                            else:
                                ins = pe.matmul(sc_ps[u % 2][:, t, 0:P], tokens((q_sb[1], q_r)[gr - 1][r, :], gr, t),
                                                tokens((k_sb[1], k_r)[gr - 1][r, :], gr, t), start=True, stop=True)
                        ins.then_inc(sc_done, 1)

                    def weighted(u):
                        gr, e = U[u]
                        nb = 2 if gr == 0 else 1
                        pe.wait_ge(exp_done, j * NU + (u + 1))
                        pe.wait_ge(pt_taken, j * NU + u)
                        for t in range(4):
                            for b in range(nb):
                                ins = pe.transpose(pt_ps[:, t * nb + b, :], p_sb[u % 2][:, t, b * P:(b + 1) * P], g.ident[:, :])
                        ins.then_inc(pt_done, 1)
                        pe.wait_ge(pt_taken, j * NU + (u + 1))
                        pe.wait_ge(pv_taken, j * NU + u)
                        pe.wait_ge(vt_taken, j * len(VT) + len(VT))
                        for t in range(4):
                            for b in range(nb):
                                vi = vstarts(0).index(windows(t) + b * P) if gr == 0 else t
                                ins = pe.matmul(pv_ps[64 * e:64 * e + 64, t * P:(t + 1) * P], v_tok[gr][:, vi, 64 * e:64 * e + 64],
                                                p_t[u % 2][:, t * nb + b, :], start=b == 0, stop=b == nb - 1, skip_group_check=True)
                        ins.then_inc(pv_done, 1)
                    pe.wait_ge(biased, j * NU)
                    scores(0)
                    for u in range(NU):
                        if u + 1 < NU:
                            scores(u + 1)
                        weighted(u)

            @block.scalar
            def _(act):
                with act.Fori(0, NP) as j:
                    act.wait_ge(landed, j * 144 + 144)
                    act.wait_ge(sc_done, j * NU)
                    for src, dst in ((q_sb, q_r), (k_sb, k_r), (v_sb, v_r)):
                        act.copy(dst[:, :].rearrange("p (r m) -> p r m", r=16),
                                 src[2][:, :].rearrange("p (m r) -> p r m", r=16)).then_inc(by_res, 1)
                    for n, (gr, c) in enumerate(VT):
                        act.wait_ge(vt_done, j * len(VT) + (n + 1))
                        k = len(vstarts(gr)[4 * c:4 * c + 4])
                        if n == 0:
                            act.wait_ge(pv_done, j * NU)
                        act.copy(v_tok[gr][:, 4 * c:4 * c + k, :], vt_ps[:, 0:k, :]).then_inc(vt_taken, 1)
                    for u, (gr, e) in enumerate(U):
                        nk = 2 * P if gr == 0 else P
                        act.wait_ge(neg_ready, j * NU + (u + 1))
                        act.wait_ge(pt_done, j * NU + max(u - 1, 0))
                        act.wait_ge(den_c, j * NU + max(u - 1, 0))
                        for t in range(4):
                            ins = act.activation(p_sb[u % 2][:, t, 0:nk], s_sb[u % 2][:, t, 0:nk], ACT.Exp,
                                                 bias=negmax[u % 2][:, t:t + 1], accum_out=den[u % 2][:, t:t + 1])
                        ins.then_inc(exp_done, 1)
                        act.wait_ge(pt_done, j * NU + (u + 1))
                        act.wait_ge(pv_done, j * NU + max(u - 1, 0))
                        nb = 8 if gr == 0 else 4
                        act.copy(p_t[u % 2][:, 0:nb, :], pt_ps[:, 0:nb, :]).then_inc(pt_taken, 1)

            @block.vector
            def _(dve):
                dve.wait_ge(consts, 7)
                for n, v in enumerate((dist[:, 0:3, :], dist[:, 3:5, 0:P])):
                    dve.scalar_tensor_tensor(out=v, in0=v, scalar=-1.0, in1=v, op0=ALU.mult, op1=ALU.max).then_inc(dist_c, 1)
                dve.wait_ge(consts, 17)
                dve.wait_ge(slopes_c, 24)
                with dve.Fori(0, NP) as j:
                    def soft(u):
                        gr, e = U[u]
                        nk = 2 * P if gr == 0 else P
                        dve.wait_ge(sc_done, j * NU + (u + 1))
                        dve.wait_ge(exp_done, j * NU + max(u - 1, 0))
                        sl = slope[:, gr, bass.ds(j * 2 + e, 1)]
                        parts = ([(0, 1, 0), (1, 3, 1), (3, 4, 2)] if gr == 0 else [(0, 4, 2 + gr)])
                        for a0, a1, dj in parts:
                            ins = dve.scalar_tensor_tensor(out=s_sb[u % 2][:, a0:a1, 0:nk],
                                                           in0=dist[:, dj:dj + 1, 0:nk].broadcast_to([P, a1 - a0, nk]), scalar=sl,
                                                           in1=sc_ps[u % 2][:, a0:a1, 0:nk], op0=ALU.mult, op1=ALU.add)
                        ins.then_inc(biased, 1)
                        dve.wait_ge(biased, j * NU + (u + 1))
                        m = mx_all[gr][:, bass.ds(j * 2 + e, 1), :]
                        dve.tensor_reduce(m.rearrange("p a t -> p (a t)"), s_sb[u % 2][:, :, 0:nk], AX.X, ALU.max).then_inc(max_ready, 1)
                        dve.wait_ge(max_ready, j * NU + (u + 1))
                        dve.tensor_scalar(negmax[u % 2][:, :], m.rearrange("p a t -> p (a t)"), -1.0, None, ALU.mult).then_inc(neg_ready, 1)

                    def file(u):
                        gr, e = U[u]
                        dve.wait_ge(exp_done, j * NU + (u + 1))
                        dve.tensor_copy(dn_all[gr][:, bass.ds(j * 2 + e, 1), :].rearrange("p a t -> p (a t)"), den[u % 2][:, :]).then_inc(den_c, 1)
                        dve.wait_ge(pv_done, j * NU + (u + 1))
                        r = slice(64 * e, 64 * e + 64)
                        o = u_all[gr][r, bass.ds(j, 1), :].rearrange("p a n -> p (a n)")
                        if gr == 0:
                            dve.tensor_copy(o, pv_ps[r, :]).then_inc(pv_taken, 1)
                        else:
                            res = 4 if gr == 1 else 16
                            dve.tensor_copy(o.rearrange("p (m r) -> p r m", r=res),
                                            pv_ps[r, :].rearrange("p (r m) -> p r m", r=res)).then_inc(pv_taken, 1)
                    soft(0)
                    for u in range(NU):
                        if u + 1 < NU:
                            soft(u + 1)
                        file(u)
        phase_combine(nc, ctx, g, mx_all, dn_all, u_all, sel, sc_ps, pt_ps, pv_ps, vt_ps)


def phase_combine(nc, ctx, g, mx_all, dn_all, u_all, sel, sc_ps, pt_ps, pv_ps, vt_ps):
    H = ATTN_HPG
    sb = lambda n, s, d=F32: ctx.enter_context(nc.sbuf_tensor(n, s, d))
    sem = nc.alloc_semaphore
    m_row = [sb(f"m_row{i}", [H, SEQ]) for i in range(3)]
    d_row = [sb(f"d_row{i}", [H, SEQ]) for i in range(3)]
    m_top = sb("m_top", [H, SEQ])
    total = sb("total", [H, SEQ])
    oa_f = sb("oa_f", [P, H // 2, SEQ])
    turned, rows_ready, m_sub, exped, w_ready, bc, chain, o_ready, oh_ready, ol_ready = (sem(n) for n in (
        "turned", "rows_ready", "m_sub", "m_exped", "w_ready", "w_bc", "c_chain", "o_ready", "oh_ready", "ol_ready"))
    flat = [sc_ps[0][:, :, :].rearrange("p a b -> p (a b)"), sc_ps[1][:, :, :].rearrange("p a b -> p (a b)"),
            pt_ps[:, :, :].rearrange("p a b -> p (a b)")]

    def natural(v, gr):
        if gr == 0:
            return v.rearrange("p (t m) -> p t m", t=4)
        if gr == 1:
            return v.rearrange("p (m t) -> p t m", t=4)
        return v.rearrange("p (m t r) -> p t r m", t=4, r=4)
    with nc.Block() as block:
        @block.tensor
        def _(pe):
            for gr in range(3):
                for k, src in enumerate((mx_all, dn_all)):
                    for t in range(4):
                        ins = pe.transpose(flat[gr][0:H, k * SEQ + t * P:k * SEQ + (t + 1) * P], src[gr][:, :, t], g.ident[:, :])
                ins.then_inc(turned, 1)
            pe.wait_ge(w_ready, 3)
            n = 0
            for j in range(H // 2):
                for gr in range(3):
                    if n >= 2:
                        pe.wait_ge(chain, 8 + n - 1)
                    pe.matmul((pv_ps[:, :], vt_ps[:, :, :].rearrange("p a b -> p (a b)"))[n % 2],
                              sel[:, 2 * j:2 * j + 2, :].rearrange("h a b -> h (a b)"), m_row[gr][:, :], start=True, stop=True).then_inc(bc, 1)
                    n += 1

        @block.scalar
        def _(act):
            for gr in range(3):
                act.wait_ge(m_sub, gr + 1)
                act.activation(m_row[gr][:, :], m_row[gr][:, :], ACT.Exp).then_inc(exped, 1)
            for j in range(H // 2):
                act.wait_ge(o_ready, j + 1)
                act.copy(g.oa_hi[:, j, :], oa_f[:, j, :]).then_inc(oh_ready, 1)

        @block.gpsimd
        def _(pool):
            for j in range(H // 2):
                pool.wait_ge(oh_ready, j + 1)
                pool.tensor_tensor(g.oa_lo[:, j, :], oa_f[:, j, :], g.oa_hi[:, j, :].bitcast(F32), ALU.subtract).then_inc(ol_ready, 1)

        @block.vector
        def _(dve):
            n = [0]

            def link(ins):
                ins.then_inc(chain, 1)
                n[0] += 1
                dve.wait_ge(chain, n[0])
            for gr in range(3):
                dve.wait_ge(turned, gr + 1)
                for k, dst in enumerate((m_row, d_row)):
                    v = flat[gr][0:H, k * SEQ:(k + 1) * SEQ]
                    v = v.rearrange("p (t m) -> p t m", t=4) if gr < 2 else v.rearrange("p (t r m) -> p t r m", t=4, r=4)
                    dve.tensor_copy(natural(dst[gr][:, :], gr), v).then_inc(rows_ready, 1)
            dve.wait_ge(rows_ready, 6)
            link(dve.tensor_tensor(m_top[:, :], m_row[0][:, :], m_row[1][:, :], ALU.max))
            link(dve.tensor_tensor(m_top[:, :], m_top[:, :], m_row[2][:, :], ALU.max))
            for gr in range(3):
                dve.tensor_tensor(m_row[gr][:, :], m_row[gr][:, :], m_top[:, :], ALU.subtract).then_inc(m_sub, 1)
            dve.wait_ge(exped, 3)
            for gr in range(3):
                link(dve.tensor_tensor(d_row[gr][:, :], d_row[gr][:, :], m_row[gr][:, :], ALU.mult))
            link(dve.tensor_tensor(total[:, :], d_row[0][:, :], d_row[1][:, :], ALU.add))
            link(dve.tensor_tensor(total[:, :], total[:, :], d_row[2][:, :], ALU.add))
            link(dve.reciprocal(total[:, :], total[:, :]))
            dve.tensor_tensor(m_row[0][:, :], m_row[0][:, :], total[:, :], ALU.mult).then_inc(w_ready, 1)
            dve.tensor_tensor(m_row[1][:, :], m_row[1][:, :], total[:, :], ALU.mult).then_inc(w_ready, 1)
            dve.tensor_tensor(m_row[2][:, :], m_row[2][:, :], total[:, :], ALU.mult).then_inc(w_ready, 1)
            c = 0
            for j in range(H // 2):
                for gr in range(3):
                    dve.wait_ge(bc, c + 1)
                    w = (pv_ps[:, :], vt_ps[:, :, :].rearrange("p a b -> p (a b)"))[c % 2]
                    link(dve.tensor_tensor(u_all[gr][:, j, :], u_all[gr][:, j, :], w, ALU.mult))
                    c += 1
            for j in range(H // 2):
                dve.tensor_tensor(u_all[0][:, j, :], u_all[0][:, j, :], u_all[1][:, j, :], ALU.add).then_inc(rows_ready, 1)
                dve.wait_ge(rows_ready, 6 + j + 1)
                dve.tensor_tensor(oa_f[:, j, :], u_all[0][:, j, :], u_all[2][:, j, :], ALU.add).then_inc(o_ready, 1)


def phase_rwkv_out(nc, g, zt, yt):
    UN = 2
    R = range(UN)
    SRC = ("y0", "y1", "r", "k", "v", "ic0", "ic1", "gate")
    KD_ = 8
    with ExitStack() as ctx:
        sb = lambda n, s, d=F32: ctx.enter_context(nc.sbuf_tensor(n, s, d))
        sem = nc.alloc_semaphore
        tin = [sb(f"r_in{j}", [P, len(SRC), SEQ]) for j in R]
        w, dv, sq, s_sb, y, t, rr, o = ([sb(f"r_{n}{j}", [P, SEQ]) for j in R]
                                        for n in ("w", "d", "sq", "s", "y", "t", "rr", "o"))
        bank = [ctx.enter_context(nc.psum_tensor(f"r_bank{j}", [P, 3, SEQ], F32)) for j in R]
        landed = [sem(f"r_landed{j}") for j in R]
        w_ready, mean_made, d_ready, sq_ready, var_made, s_ready, root, ic_sum, rr_ready, rr_made, chain, o_ready, oh_ready, ol_ready = (
            sem("r_" + n) for n in ("w_ready", "mean_made", "d_ready", "sq_ready", "var_made", "s_ready", "root", "ic_sum",
                                    "rr_ready", "rr_made", "chain", "o_ready", "oh_ready", "ol_ready"))
        gn_chain = sem("r_gn_chain")
        X = {n: k for k, n in enumerate(SRC)}
        rows = {"r": ROW_RKV, "k": ROW_RKV + RW, "v": ROW_RKV + 2 * RW, "ic0": ROW_IC, "ic1": ROW_IC + RW, "gate": ROW_GATE}

        def load(sp, j, base):
            for n, k in X.items():
                if n in rows:
                    src = zt[bass.ds(base + rows[n], P), :]
                else:
                    src = yt[int(n[1]), bass.ds(base, P), :]
                sp.dma_start(tin[j][:, k, :], src).then_inc(landed[j], 16)
        with nc.Block() as block:
            @block.sync
            def _(sp):
                for j in R:
                    load(sp, j, j * P)
                with sp.Fori(0, NPAIR // UN - 1) as i:
                    for j in R:
                        sp.wait_ge(ol_ready, i * UN + (j + 1))
                        load(sp, j, i * (UN * P) + (UN + j) * P)

            @block.tensor
            def _(pe):
                with pe.Fori(0, NPAIR // UN) as i:
                    for src, ready, k, made in ((rr, rr_ready, 2, rr_made), (w, w_ready, 0, mean_made), (sq, sq_ready, 1, var_made)):
                        for j in R:
                            pe.wait_ge(ready, i * UN + (j + 1))
                            if k == 2:
                                pe.wait_ge(o_ready, i * UN)
                            pe.matmul(bank[j][:, k, :], g.head_ones[:, :], src[j][:, :], start=True, stop=True).then_inc(made, 1)

            @block.gpsimd
            def _(pool):
                with pool.Fori(0, NPAIR // UN) as i:
                    for j in R:
                        pool.wait_ge(landed[j], i * (16 * len(SRC)) + 16 * len(SRC))
                        pool.tensor_tensor(tin[j][:, X["ic0"], :], tin[j][:, X["ic0"], :], tin[j][:, X["ic1"], :], ALU.add).then_inc(ic_sum, 1)
                    for j in R:
                        pool.wait_ge(oh_ready, i * UN + (j + 1))
                        pool.tensor_tensor(g.or_lo[:, bass.ds(i * UN + j, 1), :].rearrange("p a n -> p (a n)"), o[j][:, :],
                                           g.or_hi[:, bass.ds(i * UN + j, 1), :].bitcast(F32).rearrange("p a n -> p (a n)"),
                                           ALU.subtract).then_inc(ol_ready, 1)

            @block.scalar
            def _(act):
                with act.Fori(0, NPAIR // UN) as i:
                    for j in R:
                        act.wait_ge(d_ready, i * UN + (j + 1))
                        act.activation(sq[j][:, :], dv[j][:, :], ACT.Square).then_inc(sq_ready, 1)
                    for j in R:
                        act.wait_ge(s_ready, i * UN + (j + 1))
                        act.activation(y[j][:, :], s_sb[j][:, :], ACT.Sqrt).then_inc(root, 1)
                    for j in R:
                        act.wait_ge(o_ready, i * UN + (j + 1))
                        act.copy(g.or_hi[:, bass.ds(i * UN + j, 1), :].rearrange("p a n -> p (a n)"), o[j][:, :]).then_inc(oh_ready, 1)

            @block.vector
            def _(dve):
                with dve.Fori(0, NPAIR // UN) as i:
                    links = [0]

                    def link(ins):
                        ins.then_inc(chain, 1)
                        links[0] += 1
                        dve.wait_ge(chain, i * (KD_ * UN) + links[0])

                    def par(name, j):
                        return g.params[:, bass.ds(i * UN + (PARAMS[name][0] + j), 1)]
                    for j in R:
                        I = lambda n: tin[j][:, X[n], :]
                        dve.wait_ge(landed[j], i * (16 * len(SRC)) + 16 * len(SRC))
                        dve.tensor_tensor(w[j][:, :], I("y0"), I("y1"), ALU.add).then_inc(w_ready, 1)
                        dve.wait_ge(ic_sum, i * UN + (j + 1))
                        link(dve.tensor_scalar(t[j][:, :], I("ic0"), -2.0, par("k_a", j), ALU.add, ALU.mult))
                        link(dve.scalar_tensor_tensor(out=t[j][:, :], in0=t[j][:, :], scalar=2.0, in1=I("k"), op0=ALU.add, op1=ALU.mult))
                        dve.scalar_tensor_tensor(out=rr[j][:, :], in0=I("r"), scalar=par("r_k", j), in1=t[j][:, :],
                                                 op0=ALU.mult, op1=ALU.mult).then_inc(rr_ready, 1)
                    for j in R:
                        dve.wait_ge(mean_made, i * UN + (j + 1))
                        dve.scalar_tensor_tensor(out=dv[j][:, :], in0=bank[j][:, 0, :], scalar=-1.0 / HEAD_DIM, in1=w[j][:, :],
                                                 op0=ALU.mult, op1=ALU.add).then_inc(d_ready, 1)
                    for j in R:
                        dve.wait_ge(var_made, i * UN + (j + 1))
                        dve.tensor_scalar(s_sb[j][:, :], bank[j][:, 1, :], 1.0 / HEAD_DIM, GN_EPS, ALU.mult, ALU.add).then_inc(s_ready, 1)
                    for j in R:
                        I = lambda n: tin[j][:, X[n], :]
                        dve.wait_ge(root, i * UN + (j + 1))
                        rsqrt_newton(link, dve, y[j][:, :], t[j][:, :], s_sb[j][:, :])
                        dve.tensor_tensor(y[j][:, :], y[j][:, :], t[j][:, :], ALU.mult).then_inc(chain, 1)
                        dve.wait_ge(rr_made, i * UN + (j + 1))
                        dve.tensor_tensor(I("v"), I("v"), bank[j][:, 2, :], ALU.mult).then_inc(chain, 1)
                        links[0] += 2
                        dve.wait_ge(chain, i * (KD_ * UN) + links[0])
                        dve.wait_ge(d_ready, i * UN + UN)
                        dve.scalar_tensor_tensor(out=dv[j][:, :], in0=dv[j][:, :], scalar=par("lnw", j), in1=y[j][:, :],
                                                 op0=ALU.mult, op1=ALU.mult).then_inc(gn_chain, 1)
                        dve.wait_ge(gn_chain, i * (2 * UN) + (2 * j + 1))
                        dve.scalar_tensor_tensor(out=dv[j][:, :], in0=dv[j][:, :], scalar=par("lnb", j), in1=I("v"),
                                                 op0=ALU.add, op1=ALU.add).then_inc(gn_chain, 1)
                        dve.wait_ge(gn_chain, i * (2 * UN) + (2 * j + 2))
                        dve.wait_ge(ol_ready, i * UN)
                        dve.tensor_tensor(o[j][:, :], dv[j][:, :], I("gate"), ALU.mult).then_inc(o_ready, 1)


def phase_output(nc, g, a, zt, xt, out):
    w_a = a["w_branch_attn"].rearrange("l (k p) n -> (l p) k n", p=P)
    w_b = a["w_branch_rwkv"].rearrange("l (k p) n -> (l p) k n", p=P)
    w_o = a["w_out"].rearrange("l (k p) n -> (l p) k n", p=P)
    w_g = a["w_ffn_gate"].rearrange("l (k p) n -> (l p) k n", p=P)
    w_u = a["w_ffn_up"].rearrange("l (k p) n -> (l p) k n", p=P)
    w_d = a["w_ffn_down"].rearrange("l (k p) n -> (l p) k n", p=P)
    KA, KB = ATTN_HPG * HEAD_DIM // P, RW // P
    NBLK = 4
    HB = KF // NBLK
    SO, SF, PER = KD, 2 * KD, 2 * HB + KD
    XL = KD // 2
    with ExitStack() as ctx:
        sem = nc.alloc_semaphore
        bank = [ctx.enter_context(nc.psum_tensor(f"f_bank{i}", [P, SEQ], F32)) for i in range(8)]
        hid, plain = two_faced(nc, ctx, "hid", [P, 2 * HB, SEQ])
        hid_hi, hid_lo = hid[:, 0:HB, :], hid[:, HB:2 * HB, :]
        mix = [plain[:, 2 * i:2 * i + 2, :] for i in range(2)]
        part = [plain[:, 4 + i, :] for i in range(2)]
        merged = [plain[:, 6 + i, :] for i in range(2)]
        xin = [plain[:, 8 + i, :] for i in range(2)]
        sq_sum, s_sb, y, t_sb = (g.after_oa[:, i, :] for i in range(4))
        sq = [g.after_oa[:, 4 + i, :] for i in range(2)]
        h2f = [g.after_oa[:, 6 + i, :] for i in range(2)]
        sig, act_f = sq
        x2 = g.x2
        act_hi, act_lo = g.act_hi, g.act_lo
        (merged_ready, mhi_ready, mlo_ready, part_ready, gated, mix_used, x2_ready, sq_ready, sq_added, sq_summed, s_ready, root, chain,
         h2_ready, h2hi_ready, h2lo_ready, sig_ready, gs_ready, hid_ready, hhi_ready, hlo_ready, turned, staged) = (sem("f_" + n) for n in (
             "merged_ready", "mhi_ready", "mlo_ready", "part_ready", "gated", "mix_used", "x2_ready", "sq_ready", "sq_added", "sq_summed",
             "s_ready", "root", "chain", "h2_ready", "h2hi_ready", "h2lo_ready", "sig_ready", "gs_ready", "hid_ready",
             "hhi_ready", "hlo_ready", "turned", "staged"))
        mix_landed = [sem(f"f_mix_landed{i}") for i in range(2)]
        xin_landed = [sem(f"f_xin_landed{i}") for i in range(2)]
        out_stored = sem("f_out_stored")

        def branch(i, j):
            return Step(j, i, 2)

        def outp(i, j):
            return Step(SO + j, i, 2, loads=XL)

        def gate_up(b, i, j):
            return Step(SF + j, i, 2, b, PER, loads=XL)

        def down(b, i, j):
            return Step(SF + 2 * HB + j, i, 2, b, PER, loads=XL)

        def one(v):
            return v.rearrange("p a n -> p (a n)")

        with nc.Block() as block:
            @block.sync
            def _(sp):
                for j in range(2):
                    load_slab(sp, g, branch(0, j), [(KA, w_a[:, :, j * P:(j + 1) * P]), (KB, w_b[:, :, j * P:(j + 1) * P])])

                def mix_loads(j, m):
                    for br in range(2):
                        sp.dma_start(mix[j][:, br, :], zt[bass.ds(m * P + (ROW_MIX + br * D_MODEL), P), :]).then_inc(mix_landed[j], 16)
                for j in range(2):
                    mix_loads(j, j)
                with sp.Fori(0, KD // 2 - 1) as i:
                    for j in range(2):
                        c = bass.ds(i * (2 * P) + (2 + j) * P, P)
                        sp.wait_ge(g.w_lo_ready, i * 2 + (j + 1))
                        sp.dma_start(g.w_raw[j][:, 0:KA, :], w_a[:, :, c]).then_inc(g.w_landed[j], 16)
                        sp.dma_start(g.w_raw[j][:, KA:KA + KB, :], w_b[:, :, c]).then_inc(g.w_landed[j], 16)
                        sp.wait_ge(merged_ready, i * 2 + (j + 1))
                        mix_loads(j, i * 2 + (2 + j))
                with sp.Fori(0, KD // 2) as i:
                    for j in range(2):
                        load_slab(sp, g, outp(i, j), [(KD, w_o[:, :, bass.ds(i * (2 * P) + j * P, P)])])
                        sp.wait_ge(x2_ready, i * 2)
                        sp.dma_start(xin[j], xt[bass.ds(i * (2 * P) + j * P, P), :]).then_inc(xin_landed[j], 16)
                with sp.Fori(0, NBLK) as b:
                    with sp.Fori(0, HB) as i:
                        for j, w in enumerate((w_g, w_u)):
                            load_slab(sp, g, gate_up(b, i, j), [(KD, w[:, :, bass.ds(b * (HB * P) + i * P, P)])])
                    with sp.Fori(0, KD // 2) as i:
                        for j in range(2):
                            load_slab(sp, g, down(b, i, j), [(HB, w_d[:, bass.ds(b * HB, HB), bass.ds(i * (2 * P) + j * P, P)])])
                for n in range(KD):
                    t, q = n % TT, n // TT
                    sp.wait_ge(staged, n + 1)
                    sp.dma_start(out[0, t * P:(t + 1) * P, q * SEQ:(q + 1) * SEQ], plain[:, n, :]).then_inc(out_stored, 16)
                sp.wait_ge(out_stored, 16 * KD)

            @block.tensor
            def _(pe):
                with pe.Fori(0, KD // 2) as i:
                    for j in range(2):
                        st = branch(i, j)
                        pe.wait_ge(g.w_lo_ready, st.count())
                        pe.wait_ge(merged_ready, i * 2)
                        products(pe, g, st, [(k, k) for k in range(KA)], bank[j][:, :], g.oa_hi, g.oa_lo)
                        products(pe, g, st, [(KA + k, k) for k in range(KB)], bank[2 + j][:, :], g.or_hi, g.or_lo).then_inc(g.w_used, 1)
                pe.wait_ge(mlo_ready, KD)
                with pe.Fori(0, KD // 2) as i:
                    for j in range(2):
                        st = outp(i, j)
                        pe.wait_ge(g.w_lo_ready, st.count())
                        pe.wait_ge(x2_ready, i * 2)
                        products(pe, g, st, [(k, k) for k in range(KD)], bank[4 + j][:, :], act_hi, act_lo).then_inc(g.w_used, 1)
                pe.wait_ge(sq_added, KD)
                pe.matmul(bank[2][:, :], g.all_ones[:, :], sq_sum, start=True, stop=True).then_inc(sq_summed, 1)
                pe.wait_ge(h2lo_ready, KD)
                with pe.Fori(0, NBLK) as b:
                    with pe.Fori(0, HB) as i:
                        for j in range(2):
                            st = gate_up(b, i, j)
                            pe.wait_ge(g.w_lo_ready, st.count())
                            pe.wait_ge(hid_ready if j else gs_ready, b * HB + i)
                            products(pe, g, st, [(k, k) for k in range(KD)], bank[6 + j][:, :], act_hi, act_lo).then_inc(g.w_used, 1)
                    with pe.Fori(0, KD // 2) as i:
                        for j in range(2):
                            st = down(b, i, j)
                            pe.wait_ge(g.w_lo_ready, st.count())
                            pe.wait_ge(hlo_ready, b * HB + HB)
                            pe.wait_ge(x2_ready, b * KD + i * 2 + KD)
                            products(pe, g, st, [(k, k) for k in range(HB)], bank[j][:, :], hid_hi, hid_lo).then_inc(g.w_used, 1)
                for n in range(KD):
                    t, q = n % TT, n // TT
                    pe.wait_ge(x2_ready, KD + (NBLK - 1) * KD + 4 * q + 4)
                    if n >= 2:
                        pe.wait_ge(staged, n - 1)
                    for m in range(4):
                        ins = pe.transpose(bank[2 + n % 2][:, m * P:(m + 1) * P], x2[:, 4 * q + m, t * P:(t + 1) * P], g.ident[:, :])
                    ins.then_inc(turned, 1)

            @block.scalar
            def _(act):
                K12 = KA + KB

                def high_merged(m, j):
                    act.wait_ge(merged_ready, m + 1)
                    act.copy(one(act_hi[:, bass.ds(m, 1), :]), merged[j]).then_inc(mhi_ready, 1)
                split_hi(act, g, branch(0, 0), K12, 32)
                with act.Fori(0, KD // 2 - 1) as i:
                    split_hi(act, g, branch(i, 1), K12, i * 32 + 32)
                    high_merged(i * 2, 0)
                    split_hi(act, g, branch(i, 2), K12, i * 32 + 64)
                    high_merged(i * 2 + 1, 1)
                split_hi(act, g, branch(0, KD - 1), K12, 16 * KD)
                high_merged(KD - 2, 0)
                split_hi(act, g, outp(0, 0), KD)
                high_merged(KD - 1, 1)

                with act.Fori(0, KD // 2 - 1) as i:
                    for j in range(2):
                        split_hi(act, g, outp(i, j + 1), KD)
                        act.wait_ge(x2_ready, i * 2 + (j + 1))
                        act.wait_ge(sq_added, i * 2)
                        act.activation(sq[j], one(x2[:, bass.ds(i * 2 + j, 1), :]), ACT.Square).then_inc(sq_ready, 1)
                split_hi(act, g, outp(0, KD - 1), KD)
                for j in range(2):
                    act.wait_ge(x2_ready, KD - 1 + j)
                    act.wait_ge(sq_added, KD - 2)
                    act.activation(sq[j], x2[:, KD - 2 + j, :], ACT.Square).then_inc(sq_ready, 1)
                act.wait_ge(s_ready, 1)
                act.activation(y, s_sb, ACT.Sqrt).then_inc(root, 1)
                for k in range(KD):
                    act.wait_ge(h2_ready, k + 1)
                    act.copy(act_hi[:, k, :], h2f[k % 2]).then_inc(h2hi_ready, 1)
                with act.Fori(0, NBLK) as b:
                    def sigmoid(i):
                        act.wait_ge(g.w_used, gate_up(b, i, 0).count())
                        act.wait_ge(gs_ready, b * HB + i)
                        act.activation(sig, bank[6][:, :], ACT.Sigmoid).then_inc(sig_ready, 1)

                    def high_hidden(i):
                        act.wait_ge(hid_ready, b * HB + i + 1)
                        act.copy(one(hid_hi[:, bass.ds(i, 1), :]), act_f).then_inc(hhi_ready, 1)
                    for j in range(2):
                        split_hi(act, g, gate_up(b, 0, j), KD)
                    with act.Fori(0, HB - 1) as i:
                        sigmoid(i)
                        for j in range(2):
                            split_hi(act, g, gate_up(b, i, j + 2), KD)
                        high_hidden(i)
                    sigmoid(HB - 1)
                    for j in range(2):
                        split_hi(act, g, down(b, 0, j), HB)
                    high_hidden(HB - 1)
                    with act.Fori(0, KD // 2 - 1) as i:
                        for j in range(2):
                            split_hi(act, g, down(b, i, j + 2), HB)

            @block.gpsimd
            def _(pool):
                split_lo(pool, g, branch(0, 0), KA + KB)

                def low_merged(m, j):
                    pool.wait_ge(mhi_ready, m + 1)
                    pool.tensor_tensor(one(act_lo[:, bass.ds(m, 1), :]), merged[j], one(act_hi[:, bass.ds(m, 1), :].bitcast(F32)),
                                       ALU.subtract).then_inc(mlo_ready, 1)
                with pool.Fori(0, KD // 2 - 1) as i:
                    for j in range(2):
                        split_lo(pool, g, branch(i, j + 1), KA + KB)
                        low_merged(i * 2 + j, j)
                split_lo(pool, g, branch(0, KD - 1), KA + KB)
                low_merged(KD - 2, 0)
                low_merged(KD - 1, 1)
                with pool.Fori(0, KD // 2) as i:
                    for j in range(2):
                        split_lo(pool, g, outp(i, j), KD)
                with pool.Fori(0, NBLK) as b:
                    with pool.Fori(0, HB) as i:
                        for j in range(2):
                            split_lo(pool, g, gate_up(b, i, j), KD)
                    with pool.Fori(0, KD // 2) as i:
                        for j in range(2):
                            split_lo(pool, g, down(b, i, j), HB)

            @block.vector
            def _(dve):
                with dve.Fori(0, KD // 2) as i:
                    for j in range(2):
                        dve.wait_ge(g.w_used, branch(i, j).count())
                        dve.wait_ge(mix_landed[j], i * 32 + 32)
                        dve.tensor_tensor(part[j], mix[j][:, 0, :], bank[j][:, :], ALU.mult).then_inc(part_ready, 1)
                        dve.tensor_tensor(mix[j][:, 1, :], mix[j][:, 1, :], bank[2 + j][:, :], ALU.mult).then_inc(part_ready, 1)
                        dve.wait_ge(part_ready, i * 4 + (2 * j + 2))
                        dve.wait_ge(mlo_ready, i * 2)
                        dve.tensor_tensor(merged[j], part[j], mix[j][:, 1, :], ALU.add).then_inc(merged_ready, 1)
                dve.memset(sq_sum, 0.0).then_inc(chain, 1)
                dve.wait_ge(chain, 1)
                with dve.Fori(0, KD // 2) as i:
                    for j in range(2):
                        dve.wait_ge(g.w_used, outp(i, j).count())
                        dve.wait_ge(xin_landed[j], i * 16 + 16)
                        dve.tensor_tensor(one(x2[:, bass.ds(i * 2 + j, 1), :]), bank[4 + j][:, :], xin[j], ALU.add).then_inc(x2_ready, 1)
                        dve.wait_ge(sq_ready, i * 2 + (j + 1))
                        dve.wait_ge(sq_added, i * 2 + j)
                        dve.tensor_tensor(sq_sum, sq_sum, sq[j], ALU.add).then_inc(sq_added, 1)
                links = [1]

                def link(ins):
                    ins.then_inc(chain, 1)
                    links[0] += 1
                    dve.wait_ge(chain, links[0])
                dve.wait_ge(sq_summed, 1)
                dve.tensor_scalar(s_sb, bank[2][:, :], 1.0 / D_MODEL, RMS_EPS, ALU.mult, ALU.add).then_inc(s_ready, 1)
                dve.wait_ge(root, 1)
                rsqrt_newton(link, dve, y, t_sb, s_sb)
                link(dve.tensor_tensor(y, y, t_sb, ALU.mult))

                def normed(k):
                    if k >= 2:
                        dve.wait_ge(h2lo_ready, k - 1)
                    dve.scalar_tensor_tensor(out=h2f[k % 2], in0=x2[:, k, :], scalar=param(g, "norm2", k), in1=y,
                                             op0=ALU.mult, op1=ALU.mult).then_inc(h2_ready, 1)
                normed(0)
                for k in range(KD):
                    if k + 1 < KD:
                        normed(k + 1)
                    dve.wait_ge(h2hi_ready, k + 1)
                    dve.tensor_tensor(act_lo[:, k, :], h2f[k % 2], act_hi[:, k, :].bitcast(F32), ALU.subtract).then_inc(h2lo_ready, 1)
                with dve.Fori(0, NBLK) as b:
                    with dve.Fori(0, HB) as i:
                        dve.wait_ge(sig_ready, b * HB + i + 1)
                        dve.tensor_tensor(t_sb, sig, bank[6][:, :], ALU.mult).then_inc(gs_ready, 1)
                        dve.wait_ge(g.w_used, gate_up(b, i, 1).count())
                        dve.wait_ge(gs_ready, b * HB + i + 1)
                        dve.tensor_tensor(act_f, t_sb, bank[7][:, :], ALU.mult).then_inc(hid_ready, 1)
                        dve.wait_ge(hhi_ready, b * HB + i + 1)
                        dve.tensor_tensor(one(hid_lo[:, bass.ds(i, 1), :]), act_f, one(hid_hi[:, bass.ds(i, 1), :].bitcast(F32)),
                                          ALU.subtract).then_inc(hlo_ready, 1)
                    with dve.Fori(0, KD // 2) as i:
                        for j in range(2):
                            dve.wait_ge(g.w_used, down(b, i, j).count())
                            x = one(x2[:, bass.ds(i * 2 + j, 1), :])
                            dve.tensor_tensor(x, x, bank[j][:, :], ALU.add).then_inc(x2_ready, 1)
                for n in range(KD):
                    dve.wait_ge(turned, n + 1)
                    dve.tensor_copy(plain[:, n, :], bank[2 + n % 2][:, :]).then_inc(staged, 1)


def build(nc, a, out):
    g = Shared()
    with ExitStack() as ctx:
        zt = nc.dram_tensor("zt", [ROW_END, SEQ], F32, kind="Internal").ap()
        yt = nc.dram_tensor("yt", [2, RW, SEQ], F32, kind="Internal").ap()
        xt = nc.dram_tensor("xt", [D_MODEL, SEQ], F32, kind="Internal").ap()
        sb = lambda n, s, d=F32: ctx.enter_context(nc.sbuf_tensor(n, s, d))
        g.ident = sb("ident", [P, P])
        g.head_ones = sb("head_ones", [P, P])
        g.all_ones = sb("all_ones", [P, P])
        g.params = sb("params", [P, N_PARAM])
        with nc.cleanup_on_exit(), ExitStack() as c1:
            weight_stream(nc, c1, g)
            g.h_hi = c1.enter_context(nc.sbuf_tensor("h_hi", [P, KD, SEQ], F32R))
            g.h_lo = c1.enter_context(nc.sbuf_tensor("h_lo", [P, KD, SEQ], F32R))
            phase_setup(nc, g, a, xt)
            phase_project(nc, g, a, zt)
        n_oa = ATTN_HPG * HEAD_DIM // P
        oa, g.after_oa = two_faced(nc, ctx, "oa", [P, 2 * n_oa, SEQ])
        g.oa_hi, g.oa_lo = oa[:, 0:n_oa, :], oa[:, n_oa:2 * n_oa, :]
        with nc.cleanup_on_exit():
            phase_norms(nc, g, zt)
        with nc.cleanup_on_exit():
            phase_attention(nc, g, zt)
        with nc.cleanup_on_exit():
            phase_scan(nc, g, zt, yt)
        orw, g.x2 = two_faced(nc, ctx, "orw", [P, KD, SEQ])
        g.or_hi, g.or_lo = orw[:, 0:NPAIR, :], orw[:, NPAIR:KD, :]
        with nc.cleanup_on_exit():
            phase_rwkv_out(nc, g, zt, yt)
        weight_stream(nc, ctx, g, "_b")
        g.act_hi = sb("act_hi", [P, KD, SEQ], F32R)
        g.act_lo = sb("act_lo", [P, KD, SEQ], F32R)
        phase_output(nc, g, a, zt, xt, out)


NAMES = ("x", "norm1_w", "w_in", "b_gate", "q_norm_w", "k_norm_w", "shift_mu_prev", "shift_mu_next", "decay_w0", "decay_w2",
         "iclr_a0", "iclr_a2", "gate_g2", "k_k", "k_a", "r_k", "ln_x_w", "ln_x_b", "w_branch_attn", "w_branch_rwkv", "w_out",
         "norm2_w", "w_ffn_gate", "w_ffn_up", "w_ffn_down")


def kernel(**inputs):
    import numpy as _np
    import concourse.bacc as _bacc
    from concourse import mybir as _mybir
    from concourse.bass_utils import run_bass_kernel_spmd as _run

    nc = _bacc.Bacc("TRN2", target_bir_lowering=False, num_devices=1)
    arrays, a = {}, {}
    for name in NAMES:
        v = _np.ascontiguousarray(inputs[name])
        arrays[f"in_{name}_dram"] = v
        a[name] = nc.dram_tensor(f"in_{name}_dram", v.shape, _mybir.dt.from_np(v.dtype), kind="ExternalInput").ap()
    out = nc.dram_tensor("out_0_dram", (1, SEQ, D_MODEL), _mybir.dt.float32, kind="ExternalOutput").ap()
    build(nc, a, out)
    r = _run(nc, [arrays], core_ids=[0])
    return r.results[0]["out_0_dram"]
```

```python
from contextlib import ExitStack

import numpy as np

import concourse.bass as bass
from concourse import mybir

F32 = mybir.dt.float32
F32R = mybir.dt.float32r
ALU = mybir.AluOpType
ACT = mybir.ActivationFunctionType
AX = mybir.AxisListType

P = 128
SEQ, D_MODEL = 512, 2048
TT = SEQ // P
KD = D_MODEL // P
HEAD_DIM = 64
ATTN_GROUPS = ((128, 1), (512, 4), (2048, 16))
ATTN_HPG = 8
ATTN_HEADS = 24
ATTN_WIDTH = ATTN_HEADS * HEAD_DIM
RW = 1024
NPAIR = RW // P
DECAY_LORA = ICLR_LORA = 64
GATE_LORA = 160
FFN = 5632
KF = FFN // P
RMS_EPS, GN_EPS, L2_EPS = 1e-6, 64e-5, 1e-12
COL_RKV = 3 * ATTN_WIDTH
COL_LORA = COL_RKV + 3 * RW
COL_G = COL_LORA + DECAY_LORA + ICLR_LORA
COL_GATES = COL_G + GATE_LORA
LORA_COLUMNS = (COL_LORA, COL_G, COL_G + P)
ROW_ATTN, ROW_RKV = 0, 3 * ATTN_WIDTH
ROW_SW = ROW_RKV + 3 * RW
ROW_IC = ROW_SW + 2 * RW
ROW_GATE = ROW_IC + 2 * RW
ROW_MIX = ROW_GATE + RW
ROW_KK = ROW_MIX + 2 * D_MODEL
ROW_BONUS = ROW_KK + RW
ROW_END = ROW_BONUS + RW

PARAMS = {}
_at = 0
for _name, _n in (("norm1", 16), ("norm2", 16), ("b_gate", 32), ("mu_prev", 27), ("mu_next", 27),
                  ("qn", 1), ("kn", 1),
                  ("w0", 16), ("a0", 16), ("k_k", 8), ("k_a", 8), ("r_k", 8), ("lnw", 8), ("lnb", 8),
                  ("c_self", 27)):
    PARAMS[_name] = (_at, _n)
    _at += _n
N_PARAM = _at
N_PARAM_A = PARAMS["w0"][0]
N_PARAM_B = PARAMS["c_self"][0] - N_PARAM_A


class Shared:
    pass


def two_faced(nc, ctx, name, shape):
    with nc.sbuf_tensor(name + "_rounded", shape, F32R) as rounded:
        pass
    return rounded, ctx.enter_context(nc.sbuf_tensor(name + "_plain", shape, F32))


def weight_stream(nc, ctx, g, tag=""):
    g.w_raw = [ctx.enter_context(nc.sbuf_tensor(f"w_raw{s}{tag}", [P, KD, P], F32)) for s in range(2)]
    g.w_hi = [ctx.enter_context(nc.sbuf_tensor(f"w_hi{s}{tag}", [P, KD, P], F32R)) for s in range(2)]
    g.w_lo = [ctx.enter_context(nc.sbuf_tensor(f"w_lo{s}{tag}", [P, KD, P], F32R)) for s in range(2)]
    g.w_landed = [nc.alloc_semaphore(f"w_landed{s}{tag}") for s in range(2)]
    g.w_hi_ready = nc.alloc_semaphore(f"w_hi_ready{tag}")
    g.w_lo_ready = nc.alloc_semaphore(f"w_lo_ready{tag}")
    g.w_used = nc.alloc_semaphore(f"w_used{tag}")
    g.out_ready = nc.alloc_semaphore(f"out_ready{tag}")
    g.out_stored = [nc.alloc_semaphore(f"out_stored{s}{tag}") for s in range(2)]


class Step:

    def __init__(self, c, it=0, per=0, outer=0, outer_per=0, loads=0):
        self.c, self.it, self.per, self.outer, self.outer_per = c, it, per, outer, outer_per
        self.slot, self.loads = c % 2, loads

    def count(self, back=0):
        return self.outer * self.outer_per + self.it * self.per + (self.c - back + 1)

    def slot_count(self, back=0):
        return (self.outer * (8 * self.outer_per) + self.it * (8 * self.per)
                + 16 * ((self.c - back) // 2 + 1 + self.loads))


def load_slab(sp, g, n, parts):
    if n.c >= 2:
        sp.wait_ge(g.w_lo_ready, n.count(2))
    at = 0
    for i, (k, view) in enumerate(parts):
        ins = sp.dma_start(g.w_raw[n.slot][:, at:at + k, :], view)
        ins.then_inc(g.w_landed[n.slot], 16)
        at += k


def split_hi(act, g, n, k, dmas=None):
    act.wait_ge(g.w_landed[n.slot], n.slot_count() if dmas is None else dmas)
    if n.c >= 2:
        act.wait_ge(g.w_used, n.count(2))
    act.copy(g.w_hi[n.slot][:, 0:k, :], g.w_raw[n.slot][:, 0:k, :]).then_inc(g.w_hi_ready, 1)


def split_lo(pool, g, n, k):
    pool.wait_ge(g.w_hi_ready, n.count())
    if n.c >= 2:
        pool.wait_ge(g.w_used, n.count(2))
    pool.tensor_tensor(g.w_lo[n.slot][:, 0:k, :], g.w_raw[n.slot][:, 0:k, :],
                       g.w_hi[n.slot][:, 0:k, :].bitcast(F32), ALU.subtract).then_inc(g.w_lo_ready, 1)


def products(pe, g, n, ks, bank, hi, lo, start=True, stop=True):
    ins = None
    for j, (kw, ka) in enumerate(ks):
        wh, wl = g.w_hi[n.slot][:, kw, :], g.w_lo[n.slot][:, kw, :]
        pe.matmul(bank, wl, hi[:, ka, :], start=start and j == 0, stop=False)
        pe.matmul(bank, wh, lo[:, ka, :], start=False, stop=False)
        ins = pe.matmul(bank, wh, hi[:, ka, :], start=False, stop=stop and j == len(ks) - 1)
    return ins


def param(g, name, i=0, n=1):
    at = PARAMS[name][0] + i
    return g.params[:, at:at + n]


def phase_setup(nc, g, a, xt):
    with ExitStack() as ctx:
        sb = lambda n, s, d=F32: ctx.enter_context(nc.sbuf_tensor(n, s, d))
        ps = lambda n, s: ctx.enter_context(nc.psum_tensor(n, s, F32))
        sem = nc.alloc_semaphore
        x_tok = sb("x_tok", [P, TT, D_MODEL])
        sq = sb("sq", [P, D_MODEL])
        x_t = sb("x_t", [P, 4, SEQ])
        diag = sb("diag", [P, TT, P])
        rstd_all = sb("rstd_all", [P, SEQ])
        h_f32 = sb("h_f32", [P, 2, SEQ])
        rows_a = sb("rows_a", [P, P])
        rows_b = sb("rows_b", [P, P])
        ssq = sb("ssq", [P, TT])
        ms = sb("ms", [P, TT])
        neg_half = sb("neg_half", [P, TT])
        rstd = sb("rstd", [P, TT])
        ps_t = [ps(f"ps_t{i}", [P, SEQ]) for i in range(2)]
        ps_p = ps("ps_p", [P, SEQ])
        ps_r = ps("ps_r", [P, SEQ])
        x_landed, rows_landed = [sem(f"x_landed{t}") for t in range(TT)], sem("rows_landed")
        zeroed, const_ready, ssq_ready, ms_ready = sem("zeroed"), sem("const_ready"), sem("ssq_ready"), sem("ms_ready")
        rstd_ready, xn_ready, tr_done, hf_ready, hh_ready, hl_ready = (sem(n) for n in (
            "rstd_ready", "xn_ready", "tr_done", "hf_ready", "hh_ready", "hl_ready"))
        par_t, par_ready, xt_ready, spread, rstd_kept = (sem(n) for n in ("par_t", "par_ready", "xt_ready", "spread", "rstd_kept"))
        xt_stored = [sem(f"xt_stored{i}") for i in range(4)]
        ra, rb = PARAMS, N_PARAM_A
        row_loads = []

        def rows(name, src, n, lo_row=0):
            at = PARAMS[name][0] + lo_row
            t, at = (rows_a, at) if at < N_PARAM_A else (rows_b, at - N_PARAM_A)
            row_loads.append((t[at:at + n, :], src))

        rows("norm1", a["norm1_w"].rearrange("l (k p) -> (l k) p", p=P), 16)
        rows("norm2", a["norm2_w"].rearrange("l (k p) -> (l k) p", p=P), 16)
        rows("b_gate", a["b_gate"].rearrange("l b (k p) -> (l b k) p", p=P), 32)
        for nm, key in (("mu_prev", "shift_mu_prev"), ("mu_next", "shift_mu_next")):
            rows(nm, a[key][:, 0:26 * P].rearrange("l (k p) -> (l k) p", p=P), 26)
            at = PARAMS[nm][0] + 26
            row_loads.append((rows_a[at:at + 1, 0:32], a[key][:, 26 * P:26 * P + 32]))
        for nm, key in (("qn", "q_norm_w"), ("kn", "k_norm_w")):
            at = PARAMS[nm][0]
            for h in range(2):
                row_loads.append((rows_a[at:at + 1, 64 * h:64 * h + 64], a[key]))
        rows("w0", a["decay_w0"].rearrange("l z (k p) -> (l z k) p", p=P), 16)
        rows("a0", a["iclr_a0"].rearrange("l z (k p) -> (l z k) p", p=P), 16)
        for nm, key in (("k_k", "k_k"), ("k_a", "k_a"), ("lnw", "ln_x_w"), ("lnb", "ln_x_b")):
            rows(nm, a[key].rearrange("l (k p) -> (l k) p", p=P), 8)
        rows("r_k", a["r_k"].rearrange("l (k a) e -> (l k) (a e)", a=2), 8)
        nrow = len(row_loads)

        with nc.Block() as block:
            @block.sync
            def _(sp):
                for t in range(TT):
                    sp.dma_start(x_tok[:, t, :], a["x"][0, t * P:(t + 1) * P, :]).then_inc(x_landed[t], 16)
                w_in = a["w_in"].rearrange("l (k p) n -> (l p) k n", p=P)
                for c, c0 in enumerate(LORA_COLUMNS[:2]):
                    load_slab(sp, g, Step(c), [(KD, w_in[:, :, c0:c0 + P])])
                sp.wait_ge(zeroed, 2)
                for dst, src in row_loads:
                    sp.dma_start(dst, src).then_inc(rows_landed, 16)
                for k in range(KD):
                    sp.wait_ge(xt_ready, k + 1)
                    sp.dma_start(xt[k * P:(k + 1) * P, :], x_t[:, k % 4, :]).then_inc(xt_stored[k % 4], 16)
                for i in range(4):
                    sp.wait_ge(xt_stored[i], 16 * (KD // 4))

            @block.gpsimd
            def _(pool):
                pool.memset(g.ident[:, :], 0.0).then_inc(const_ready, 1)
                pool.memset(g.head_ones[:, :], 1.0).then_inc(const_ready, 1)
                pool.memset(neg_half[:, :], -0.5).then_inc(const_ready, 1)
                pool.memset(g.all_ones[:, :], 1.0).then_inc(const_ready, 1)
                pool.wait_ge(const_ready, 4)
                pool.affine_select(out=g.ident[:, :], in_=g.ident[:, :], compare_op=ALU.not_equal, fill=1.0,
                                   base=0, pattern=[[-1, P]], channel_multiplier=1).then_inc(const_ready, 1)
                pool.affine_select(out=g.head_ones[:, 0:64], in_=g.head_ones[:, 0:64], compare_op=ALU.is_ge,
                                   fill=0.0, base=63, pattern=[[0, 64]], channel_multiplier=-1).then_inc(const_ready, 1)
                pool.affine_select(out=g.head_ones[:, 64:128], in_=g.head_ones[:, 64:128], compare_op=ALU.is_ge,
                                   fill=0.0, base=-64, pattern=[[0, 64]], channel_multiplier=1).then_inc(const_ready, 1)
                pool.wait_ge(ms_ready, 1)
                pool.tensor_tensor(rstd[:, :], ms[:, :], neg_half[:, :], ALU.pow).then_inc(rstd_ready, 1)
                for c in range(2):
                    split_lo(pool, g, Step(c), KD)

            @block.scalar
            def _(act):
                for t in range(TT):
                    act.wait_ge(x_landed[t], 16)
                    act.activation(sq[:, :], x_tok[:, t, :], ACT.Square, accum_out=ssq[:, t:t + 1]).then_inc(ssq_ready, 1)
                    act.wait_ge(ssq_ready, t + 1)

                def keep(k):
                    act.wait_ge(tr_done, k + 1)
                    if k >= 4:
                        act.wait_ge(xt_stored[k % 4], 16 * (k // 4))
                        act.wait_ge(hf_ready, k - 3)
                    act.copy(x_t[:, k % 4, :], ps_t[k % 2][:, :]).then_inc(xt_ready, 1)
                keep(0)
                keep(1)
                for c in range(2):
                    split_hi(act, g, Step(c), KD)
                for k in range(KD):
                    if k + 2 < KD:
                        keep(k + 2)
                    act.wait_ge(hf_ready, k + 1)
                    act.copy(g.h_hi[:, k, :], h_f32[:, k % 2, :]).then_inc(hh_ready, 1)

            @block.tensor
            def _(pe):
                pe.wait_ge(const_ready, 5)
                for t in range(TT):
                    pe.wait_ge(x_landed[t], 16)
                for k in range(KD):
                    if k == 2:
                        pe.wait_ge(rows_landed, 16 * nrow)
                        pe.transpose(ps_p[:, 0:P], rows_a[:, :], g.ident[:, :])
                        pe.transpose(ps_p[:, P:2 * P], rows_b[:, :], g.ident[:, :]).then_inc(par_t, 1)
                        pe.wait_ge(xn_ready, TT)
                        for t in range(TT):
                            ins = pe.matmul(ps_r[:, t * P:(t + 1) * P], g.all_ones[:, :], diag[:, t, :], start=True, stop=True)
                        ins.then_inc(spread, 1)
                    if k >= 2:
                        pe.wait_ge(xt_ready, k - 1)
                    for t in range(TT):
                        ins = pe.transpose(ps_t[k % 2][:, t * P:(t + 1) * P], x_tok[:, t, k * P:(k + 1) * P], g.ident[:, :])
                    ins.then_inc(tr_done, 1)

            @block.vector
            def _(dve):
                dve.memset(rows_a[:, :], 0.0).then_inc(zeroed, 1)
                dve.memset(rows_b[:, :], 0.0).then_inc(zeroed, 1)
                dve.wait_ge(ssq_ready, TT)
                dve.tensor_scalar(ms[:, :], ssq[:, :], 1.0 / D_MODEL, RMS_EPS, ALU.mult, ALU.add).then_inc(ms_ready, 1)
                dve.wait_ge(rstd_ready, 1)
                dve.wait_ge(const_ready, 5)
                for t in range(TT):
                    dve.tensor_scalar(diag[:, t, :], g.ident[:, :], rstd[:, t:t + 1], None, ALU.mult).then_inc(xn_ready, 1)
                dve.wait_ge(par_t, 1)
                dve.tensor_copy(g.params[:, 0:N_PARAM_A], ps_p[:, 0:N_PARAM_A]).then_inc(par_ready, 1)
                dve.tensor_copy(g.params[:, N_PARAM_A:N_PARAM_A + N_PARAM_B], ps_p[:, P:P + N_PARAM_B]).then_inc(par_ready, 1)
                dve.wait_ge(par_ready, 2)
                dve.tensor_tensor(param(g, "c_self", 0, 27), param(g, "mu_prev", 0, 27), param(g, "mu_next", 0, 27),
                                  ALU.add).then_inc(par_ready, 1)
                dve.wait_ge(par_ready, 3)
                dve.tensor_scalar(param(g, "c_self", 0, 27), param(g, "c_self", 0, 27), -1.0, 1.0, ALU.mult,
                                  ALU.add).then_inc(par_ready, 1)
                dve.wait_ge(spread, 1)
                dve.tensor_copy(rstd_all[:, :], ps_r[:, :]).then_inc(rstd_kept, 1)
                dve.wait_ge(rstd_kept, 1)
                def normed(k):
                    dve.wait_ge(xt_ready, k + 1)
                    if k >= 2:
                        dve.wait_ge(hl_ready, k - 1)
                    dve.scalar_tensor_tensor(out=h_f32[:, k % 2, :], in0=x_t[:, k % 4, :], scalar=param(g, "norm1", k),
                                             in1=rstd_all[:, :], op0=ALU.mult, op1=ALU.mult).then_inc(hf_ready, 1)
                normed(0)
                for k in range(KD):
                    if k + 1 < KD:
                        normed(k + 1)
                    dve.wait_ge(hh_ready, k + 1)
                    dve.tensor_tensor(g.h_lo[:, k, :], h_f32[:, k % 2, :], g.h_hi[:, k, :].bitcast(F32),
                                      ALU.subtract).then_inc(hl_ready, 1)


def phase_project(nc, g, a, zt):
    w_in = a["w_in"].rearrange("l (k p) n -> (l p) k n", p=P)
    C0 = 3
    NA, NB, ND = 36, 24, 32
    SA0, SB0, SD0, SEND = C0, C0 + NA, C0 + NA + NB, C0 + NA + NB + ND
    UN = 4
    W = ATTN_WIDTH
    SECTIONS = ((SA0, 12, "norm", 0, ROW_ATTN, 0, "qn", None),
                (SA0 + 12, 12, "norm", W, ROW_ATTN + W, 12, "kn", None),
                (SA0 + 24, 12, "plain", 2 * W, ROW_ATTN + 2 * W, 24, None, None),
                (SB0, 8, "shift", COL_RKV, ROW_RKV, 24, None, 0),
                (SB0 + 8, 8, "shift norm", COL_RKV + RW, ROW_RKV + RW, 24, "k_k", 8),
                (SB0 + 16, 8, "shift", COL_RKV + 2 * RW, ROW_RKV + 2 * RW, 32, None, 16))
    with ExitStack() as ctx:
        sb = lambda n, s, d=F32: ctx.enter_context(nc.sbuf_tensor(n, s, d))
        ps = lambda n, s: ctx.enter_context(nc.psum_tensor(n, s, F32))
        sem = nc.alloc_semaphore
        bank = [ps(f"bank{i}", [P, SEQ]) for i in range(2)]
        lbank = [ps(f"lbank{i}", [P, SEQ]) for i in range(2)]
        out = [sb(f"out{i}", [P, SEQ]) for i in range(2)]
        NL = 4
        lout = [sb(f"lout{i}", [P, SEQ]) for i in range(NL)]
        raw = [sb(f"raw{i}", [P, SEQ]) for i in range(2)]
        kk_out = [sb(f"kk_out{i}", [P, SEQ]) for i in range(2)]
        sq = [sb(f"n_sq{i}", [P, SEQ]) for i in range(2)]
        s_sb, y, t_sb = (sb(n, [P, SEQ]) for n in ("n_s", "n_y", "n_t"))
        nbank = [ps(f"nbank{i}", [P, SEQ]) for i in range(2)]
        b_in = sb("b_in", [P, 5, SEQ])
        b_t, rr, bonus = (sb(n, [P, SEQ]) for n in ("b_t", "rr", "bonus"))
        b_landed, ic_sum, b_chain, rr_ready, b_summed, b_ready, b_stored = (sem(n) for n in (
            "b_landed", "ic_sum", "b_chain", "rr_ready", "b_summed", "b_ready", "b_stored"))
        drained, sq_ready, summed, s_ready, root, chain, normed, wq = (sem(n) for n in (
            "drained", "n_sq_ready", "n_summed", "n_s_ready", "n_root", "n_chain", "normed", "n_wq"))
        kk_stored = [sem(f"kk_stored{i}") for i in range(2)]
        lora = sb("lora", [P, 3, SEQ])
        w2 = sb("w2", [P, 2, RW])
        g2 = sb("g2", [P, 2, RW])
        mix_ready, w2_landed, sem_c, lora_ready, lora_act, l_done, l_ev = (sem(n) for n in (
            "mix_ready", "w2_landed", "shift_chain", "lora_ready", "lora_act", "l_done", "l_ev"))
        l_stored = [sem(f"l_stored{i}") for i in range(NL)]
        shifted = [0]

        def cols(c0):
            return w_in[:, :, c0:c0 + P]

        lora_jobs = []
        for z in range(2):
            for p in range(NPAIR):
                lora_jobs.append((ROW_SW + z * RW + p * P, "w", z, p))
                lora_jobs.append((ROW_IC + z * RW + p * P, "a", z, p))
        for p in range(NPAIR):
            lora_jobs.append((ROW_GATE + p * P, "g", 0, p))

        with nc.Block() as block:
            @block.sync
            def _(sp):
                for z in range(2):
                    sp.dma_start(w2[0:64, z, :], a["decay_w2"][0, z]).then_inc(w2_landed, 16)
                    sp.dma_start(w2[64:128, z, :], a["iclr_a2"][0, z]).then_inc(w2_landed, 16)
                sp.dma_start(g2[:, 0, :], a["gate_g2"][0, 0:P, :]).then_inc(w2_landed, 16)
                sp.dma_start(g2[0:32, 1, :], a["gate_g2"][0, P:GATE_LORA, :]).then_inc(w2_landed, 16)
                load_slab(sp, g, Step(2), [(KD, cols(LORA_COLUMNS[2]))])
                load_slab(sp, g, Step(SA0), [(KD, cols(0))])
                load_slab(sp, g, Step(SA0 + 1), [(KD, cols(P))])
                load_slab(sp, g, Step(SA0 + 2), [(KD, cols(2 * P))])
                for j, (row, _, _, _) in enumerate(lora_jobs):
                    sp.wait_ge(l_ev, j + 1)
                    sp.dma_start(zt[row:row + P, :], lout[j % NL][:, :]).then_inc(l_stored[j % NL], 16)

                def bonus_loads(row, so_far):
                    sp.wait_ge(b_ready, so_far)
                    for k, first in enumerate((ROW_RKV, ROW_RKV + RW, ROW_RKV + 2 * RW, ROW_IC, ROW_IC + RW)):
                        sp.dma_start(b_in[:, k, :], zt[bass.ds(row + first, P), :]).then_inc(b_landed, 16)

                def bonus_store(row, count):
                    sp.wait_ge(b_ready, count)
                    sp.dma_start(zt[bass.ds(row + ROW_BONUS, P), :], bonus[:, :]).then_inc(b_stored, 16)

                def turn(base, i, row0, freed, counted, ahead, kk=False, norms=0, pair=None):
                    def store(j):
                        st = Step(base + j, i, UN)
                        sp.wait_ge(freed, st.count() - counted)
                        sp.dma_start(zt[bass.ds(i * (UN * P) + (row0 + j * P), P), :],
                                     out[st.slot][:, :]).then_inc(g.out_stored[st.slot], 16)
                        if kk:
                            sp.wait_ge(normed, i * UN + (norms - 24 + j + 1))
                            sp.dma_start(zt[bass.ds(i * (UN * P) + (ROW_KK + (norms - 24 + j) * P), P), :],
                                         kk_out[st.slot][:, :]).then_inc(kk_stored[st.slot], 16)
                    for j in range(UN):
                        if ahead[j] is not None:
                            load_slab(sp, g, Step(base + j + 3, i, UN), [(KD, ahead[j])])
                        if j >= 2:
                            store(j - 2)
                        if pair is not None and j == 0:
                            bonus_loads(i * P + pair * P, i + pair)
                    store(UN - 2)
                    store(UN - 1)
                    if pair is not None:
                        bonus_store(i * P + pair * P, i + (pair + 1))

                def section(base, n, col0, row0, freed, counted, then, kk=False, norms=0, pairs=False):
                    with sp.Fori(0, n // UN - 1) as i:
                        turn(base, i, row0, freed, counted,
                             [w_in[:, :, bass.ds(i * (UN * P) + (col0 + (j + 3) * P), P)] for j in range(UN)], kk, norms, 0 if pairs else None)
                    m = n - UN
                    turn(base + m, 0, row0 + m * P, freed, counted,
                         [cols(col0 + (m + 3) * P)] + then, kk, norms + m, m // UN if pairs else None)

                for q, (base, n, kind, col0, row0, norms, _, _) in enumerate(SECTIONS):
                    col1 = SECTIONS[q + 1][3] if q + 1 < len(SECTIONS) else COL_GATES
                    section(base, n, col0, row0, g.out_ready, C0, [cols(col1 + k * P) for k in range(3)], kind == "shift norm", norms)
                for s in range(2):
                    sp.wait_ge(g.out_stored[s], 16 * ((SD0 - C0) // 2))
                for s in range(NL):
                    sp.wait_ge(l_stored[s], 16 * (len(lora_jobs) // NL))
                section(SD0, ND, COL_GATES, ROW_MIX, mix_ready, SD0, [None, None, None], pairs=True)
                sp.wait_ge(b_stored, 16 * NPAIR)
                for s in range(2):
                    sp.wait_ge(g.out_stored[s], 16 * ((SEND - C0) // 2))
                    sp.wait_ge(kk_stored[s], 16 * (NPAIR // 2))

            @block.scalar
            def _(act):
                split_hi(act, g, Step(2), KD)
                act.wait_ge(lora_ready, 3)
                act.activation(lora[0:64, 0, :], lora[0:64, 0, :], ACT.Tanh).then_inc(lora_act, 1)
                act.activation(lora[:, 1, :], lora[:, 1, :], ACT.Sigmoid).then_inc(lora_act, 1)
                act.activation(lora[0:32, 2, :], lora[0:32, 2, :], ACT.Sigmoid).then_inc(lora_act, 1)
                for c in range(2):
                    split_hi(act, g, Step(SA0 + c), KD)
                for j, (row, kind, z, p) in enumerate(lora_jobs):
                    act.wait_ge(l_done, j + 1)
                    if j >= NL:
                        act.wait_ge(l_stored[j % NL], 16 * (j // NL))
                    if kind == "g":
                        ins = act.copy(lout[j % NL][:, :], lbank[j % 2][:, :])
                    else:
                        ins = act.activation(lout[j % NL][:, :], lbank[j % 2][:, :], ACT.Sigmoid,
                                             bias=param(g, "w0" if kind == "w" else "a0", z * 8 + p))
                    ins.then_inc(l_ev, 1)
                for base, n, kind, _, _, norms, w, _ in SECTIONS:
                    with act.Fori(0, n // UN) as i:
                        def square(j):
                            st = Step(base + j, i, UN)
                            if w == "k_k":
                                act.wait_ge(g.out_ready, st.count() - C0)
                                act.activation(sq[j % 2][:, :], out[st.slot][:, :], ACT.Square,
                                               scale=g.params[:, bass.ds(i * UN + (PARAMS["k_k"][0] + j), 1)]).then_inc(sq_ready, 1)
                            else:
                                act.wait_ge(drained, st.count() - C0)
                                act.activation(sq[j % 2][:, :], raw[st.slot][:, :], ACT.Square).then_inc(sq_ready, 1)

                        def root_of(j):
                            act.wait_ge(s_ready, i * UN + (norms + j + 1))
                            act.activation(y[:, :], s_sb[:, :], ACT.Sqrt).then_inc(root, 1)
                        for j in range(UN):
                            if w:
                                square(j)
                            split_hi(act, g, Step(base + j + 2, i, UN), KD)
                            if w and j:
                                root_of(j - 1)
                        if w:
                            root_of(UN - 1)

                def mix(st, row_tile):
                    act.wait_ge(g.w_used, st.count())
                    act.wait_ge(g.out_stored[st.slot], st.slot_count(2) - 16 * (C0 // 2 + (0 if st.slot else 1)))
                    act.activation(out[st.slot][:, :], bank[st.slot][:, :], ACT.Sigmoid, bias=row_tile).then_inc(mix_ready, 1)
                with act.Fori(0, ND // UN - 1) as i:
                    for j in range(UN):
                        mix(Step(SD0 + j, i, UN), g.params[:, bass.ds(i * UN + (PARAMS["b_gate"][0] + j), 1)])
                        split_hi(act, g, Step(SD0 + j + 2, i, UN), KD)
                for j in range(ND - UN, ND):
                    mix(Step(SD0 + j), param(g, "b_gate", j))
                    if j + 2 < ND:
                        split_hi(act, g, Step(SD0 + j + 2), KD)

            @block.gpsimd
            def _(pool):
                split_lo(pool, g, Step(2), KD)
                with pool.Fori(0, (SD0 - C0) // UN) as i:
                    for j in range(UN):
                        split_lo(pool, g, Step(C0 + j, i, UN), KD)
                with pool.Fori(0, ND // UN) as i:
                    for j in range(UN):
                        split_lo(pool, g, Step(SD0 + j, i, UN), KD)
                        if j == 2:
                            pool.wait_ge(b_landed, i * 80 + 80)
                            pool.tensor_tensor(b_in[:, 3, :], b_in[:, 3, :], b_in[:, 4, :], ALU.add).then_inc(ic_sum, 1)

            @block.tensor
            def _(pe):
                for c in range(C0):
                    pe.wait_ge(g.w_lo_ready, c + 1)
                    if c >= 2:
                        pe.wait_ge(lora_ready, c - 1)
                    products(pe, g, Step(c), [(k, k) for k in range(KD)], bank[c % 2][:, :], g.h_hi, g.h_lo).then_inc(g.w_used, 1)
                pe.wait_ge(w2_landed, 16 * 6)
                pe.wait_ge(lora_act, 3)
                for j, (row, kind, z, p) in enumerate(lora_jobs):
                    if j >= 2:
                        pe.wait_ge(l_ev, j - 1)
                    o, c = lbank[j % 2][:, :], slice(p * P, (p + 1) * P)
                    if kind == "g":
                        pe.matmul(o, g2[:, 0, c], lora[:, 1, :], start=True, stop=False)
                        ins = pe.matmul(o, g2[0:32, 1, c], lora[0:32, 2, :], start=False, stop=True)
                    else:
                        r = slice(0, 64) if kind == "w" else slice(64, 128)
                        ins = pe.matmul(o, w2[r, z, c], lora[r, 0, :], start=True, stop=True)
                    ins.then_inc(l_done, 1)

                def one(st, freed, base):
                    pe.wait_ge(g.w_lo_ready, st.count())
                    if freed is not None:
                        pe.wait_ge(freed, st.count(2) - base)
                    products(pe, g, st, [(k, k) for k in range(KD)], bank[st.slot][:, :], g.h_hi, g.h_lo).then_inc(g.w_used, 1)
                pe.wait_ge(lora_ready, 3)

                def head_sums(i, j, norms):
                    pe.wait_ge(sq_ready, i * UN + (norms + j + 1))
                    pe.wait_ge(s_ready, i * UN + (norms + max(j - 1, 0)))
                    pe.matmul(nbank[j % 2][:, :], g.head_ones[:, :], sq[j % 2][:, :], start=True, stop=True).then_inc(summed, 1)

                def slabs(base, i, w, norms, first=False):
                    for j in range(UN):
                        one(Step(base + j, i, UN), None if first and j < 2 else drained, C0)
                        if w and j:
                            head_sums(i, j - 1, norms)
                    if w:
                        head_sums(i, UN - 1, norms)
                for base, n, _, _, _, norms, w, _ in SECTIONS:
                    skip = 1 if base == C0 else 0
                    if skip:
                        slabs(base, 0, w, norms, first=True)
                    with pe.Fori(0, n // UN - skip) as i:
                        slabs(base + skip * UN, i, w, norms + skip * UN)

                def bonus_sums(i, pair):
                    pe.wait_ge(rr_ready, i + (pair + 1))
                    pe.matmul(nbank[0][:, :], g.head_ones[:, :], rr[:, :], start=True, stop=True).then_inc(b_summed, 1)
                for j in range(UN):
                    one(Step(SD0 + j), *((drained, C0) if j < 2 else (mix_ready, SD0)))
                bonus_sums(0, 0)
                with pe.Fori(0, ND // UN - 1) as i:
                    for j in range(UN):
                        one(Step(SD0 + UN + j, i, UN), mix_ready, SD0)
                    bonus_sums(i, 1)

            @block.vector
            def _(dve):
                def shift(src, dst, ti, rows=P, it=None):
                    def pr(name):
                        if it is None:
                            return param(g, name, ti)[0:rows, :]
                        return g.params[0:rows, bass.ds(it * UN + (PARAMS[name][0] + ti), 1)]
                    base = shifted[0]
                    s = src[0:rows, :]
                    dve.tensor_scalar(dst[0:rows, :], s, pr("c_self"), None, ALU.mult).then_inc(sem_c, 1)
                    cnt = (lambda k: base + k) if it is None else (lambda k: it * (2 * UN) + (base + k))
                    dve.wait_ge(sem_c, cnt(1))
                    dve.scalar_tensor_tensor(out=dst[0:rows, 1:SEQ], in0=src[0:rows, 0:SEQ - 1], scalar=pr("mu_prev"),
                                             in1=dst[0:rows, 1:SEQ], op0=ALU.mult, op1=ALU.add).then_inc(sem_c, 1)
                    dve.wait_ge(sem_c, cnt(2))
                    shifted[0] += 2
                    return dve.scalar_tensor_tensor(out=dst[0:rows, 0:SEQ - 1], in0=src[0:rows, 1:SEQ], scalar=pr("mu_next"),
                                                    in1=dst[0:rows, 0:SEQ - 1], op0=ALU.mult, op1=ALU.add)

                for c, rows in enumerate((P, P, 32)):
                    dve.wait_ge(g.w_used, c + 1)
                    shift(bank[c % 2], lora[:, c, :], 24 + c, rows).then_inc(lora_ready, 1)

                def slot_free(st):
                    dve.wait_ge(g.out_stored[st.slot], st.slot_count(2) - 16 * (C0 // 2 + (0 if st.slot else 1)))

                K = 5

                def drain(st, first):
                    dve.wait_ge(g.w_used, st.count())
                    if not first:
                        dve.wait_ge(g.out_ready, st.count(2) - C0)
                    dve.tensor_copy(raw[st.slot][:, :], bank[st.slot][:, :]).then_inc(drained, 1)

                def norm(base, i, j, norms, w, first):
                    st = Step(base + j, i, UN)
                    links = [0]

                    def link(ins):
                        ins.then_inc(chain, 1)
                        links[0] += 1
                        dve.wait_ge(chain, i * (UN * K) + ((norms + j) * K + links[0]))
                    dve.wait_ge(summed, i * UN + (norms + j + 1))
                    if w == "k_k":
                        dve.tensor_scalar(s_sb[:, :], nbank[j % 2][:, :], L2_EPS * L2_EPS, None, ALU.max).then_inc(s_ready, 1)
                    else:
                        dve.tensor_scalar(s_sb[:, :], nbank[j % 2][:, :], 1.0 / HEAD_DIM, RMS_EPS, ALU.mult, ALU.add).then_inc(s_ready, 1)
                    dve.wait_ge(root, i * UN + (norms + j + 1))
                    rsqrt_newton(link, dve, y[:, :], t_sb[:, :], s_sb[:, :])
                    link(dve.tensor_tensor(y[:, :], y[:, :], t_sb[:, :], ALU.mult))
                    if w == "k_k":
                        if not first:
                            dve.wait_ge(kk_stored[st.slot], i * (8 * UN) + 16 * ((norms - 24 + j) // 2))
                        dve.scalar_tensor_tensor(out=kk_out[st.slot][:, :], in0=out[st.slot][:, :],
                                                 scalar=g.params[:, bass.ds(i * UN + (PARAMS["k_k"][0] + (norms - 24) + j), 1)],
                                                 in1=y[:, :], op0=ALU.mult, op1=ALU.mult).then_inc(normed, 1)
                    else:
                        if not first:
                            slot_free(st)
                        dve.scalar_tensor_tensor(out=out[st.slot][:, :], in0=raw[st.slot][:, :], scalar=param(g, w),
                                                 in1=y[:, :], op0=ALU.mult, op1=ALU.mult).then_inc(g.out_ready, 1)

                def turn(base, i, kind, norms, w, tile, first=False):
                    for j in range(UN):
                        st = Step(base + j, i, UN)
                        drain(st, first and j < 2)
                        if kind != "norm":
                            if kind == "shift norm":
                                dve.wait_ge(normed, i * UN + (norms - 24 + max(j - 1, 0)))
                            elif tile == 16:
                                dve.wait_ge(normed, NPAIR)
                            slot_free(st)
                            dve.wait_ge(drained, st.count() - C0)
                            if kind == "plain":
                                dve.tensor_copy(out[st.slot][:, :], raw[st.slot][:, :]).then_inc(g.out_ready, 1)
                            else:
                                shift(raw[st.slot], out[st.slot], tile + j, it=i).then_inc(g.out_ready, 1)
                        if w and j:
                            norm(base, i, j - 1, norms, w, first and j - 1 < 2)
                    if w:
                        norm(base, i, UN - 1, norms, w, False)
                dve.tensor_scalar(param(g, "qn"), param(g, "qn"), HEAD_DIM ** -0.5, None, ALU.mult).then_inc(wq, 1)
                dve.wait_ge(wq, 1)
                for base, n, kind, _, _, norms, w, tile in SECTIONS:
                    skip = 1 if base == C0 else 0
                    if skip:
                        turn(base, 0, kind, norms, w, tile, first=True)
                    with dve.Fori(0, n // UN - skip) as i:
                        turn(base + skip * UN, i, kind, norms + skip * UN, w, tile)
                    if tile is not None:
                        shifted[0] += 2 * (n - UN)
                with dve.Fori(0, NPAIR) as i:
                    def par(name):
                        return g.params[:, bass.ds(i + PARAMS[name][0], 1)]
                    dve.wait_ge(ic_sum, i + 1)
                    dve.tensor_scalar(b_t[:, :], b_in[:, 3, :], -2.0, par("k_a"), ALU.add, ALU.mult).then_inc(b_chain, 1)
                    dve.wait_ge(b_chain, i * 2 + 1)
                    dve.scalar_tensor_tensor(out=b_t[:, :], in0=b_t[:, :], scalar=2.0, in1=b_in[:, 1, :],
                                             op0=ALU.add, op1=ALU.mult).then_inc(b_chain, 1)
                    dve.wait_ge(b_chain, i * 2 + 2)
                    dve.scalar_tensor_tensor(out=rr[:, :], in0=b_in[:, 0, :], scalar=par("r_k"), in1=b_t[:, :],
                                             op0=ALU.mult, op1=ALU.mult).then_inc(rr_ready, 1)
                    dve.wait_ge(b_summed, i + 1)
                    dve.wait_ge(b_stored, i * 16)
                    dve.tensor_tensor(bonus[:, :], b_in[:, 2, :], nbank[0][:, :], ALU.mult).then_inc(b_ready, 1)
    g.next_step = SEND



CH = 64
NCH = SEQ // CH
NQ = 4
LEVELS = 5
DECAY_SCALE = float(np.exp(np.float64(-0.5)))

SCAN_STAGES = ([("ab0", 0, "dve"), ("ab1", 1, "dve"), ("ak0", 2, "dve"), ("ak1", 3, "dve"), ("mab", 0, "dve"),
                ("tb", 2, "act"), ("tk", 3, "act"), ("tv", 1, "act"), ("w", 2, "act")]
               + [s for l in range(1, LEVELS) for s in
                  [(f"z{l}", 0, "act"), (f"u{l}", 3, "dve")] + ([(f"x{l}", 1, "act")] if l < LEVELS - 1 else [])]
               + [("v", 1, "act"), ("m", 2, "dve"), ("sa", 0, "dve"), ("y", 3, "act"), ("tn", 1, "dve")])
SCAN_NAMES = [s[0] for s in SCAN_STAGES]
AHEAD_DECAYS, AHEAD_EXPONENTS, AHEAD_OPERANDS = "z2", "z3", "z4"
N_PE = len(SCAN_STAGES)
N_EV = {e: sum(s[2] == e for s in SCAN_STAGES) for e in ("dve", "act")}


def made(name):
    return SCAN_NAMES.index(name) + 1


def taken(name):
    e = SCAN_STAGES[SCAN_NAMES.index(name)][2]
    return e, sum(s[2] == e for s in SCAN_STAGES[:SCAN_NAMES.index(name) + 1])


def bank_before(name):
    i = SCAN_NAMES.index(name)
    prev = [s[0] for s in SCAN_STAGES[:i] if s[1] == SCAN_STAGES[i][1]]
    return prev[-1] if prev else None


def scan_masks(pool, g, made_masks):
    c = [0]

    def count(ins):
        ins.then_inc(made_masks, 1)
        c[0] += 1
    count(pool.memset(g.seg[:, :], 1.0))
    for s in range(2):
        count(pool.memset(g.tri[s][:, :], 1.0))
    count(pool.memset(g.same[:, :, :], 1.0))
    pool.wait_ge(made_masks, c[0])
    sv = g.seg[:, :].rearrange("p (q c) -> p q c", c=CH)
    count(pool.affine_select(out=sv, in_=sv, compare_op=ALU.not_equal, fill=0.0, base=0,
                             pattern=[[0, NQ], [1, CH]], channel_multiplier=0))
    for s in range(2):
        sign = 1 if s == 0 else -1
        for j, op in enumerate((ALU.is_gt, ALU.is_ge)):
            v = g.tri[s][:, j * P:(j + 1) * P]
            count(pool.affine_select(out=v, in_=v, compare_op=op, fill=0.0, base=0,
                                     pattern=[[sign, P]], channel_multiplier=-sign))
    for l in range(LEVELS + 2):
        b = 1 << l
        v = g.same[:, l, :].rearrange("p (n b) -> p n b", b=b)
        count(pool.affine_select(out=v, in_=v, compare_op=ALU.is_ge, fill=0.0, base=0,
                                 pattern=[[-b, P // b], [0, b]], channel_multiplier=1))
    pool.wait_ge(made_masks, c[0])
    for l in range(LEVELS + 2):
        b = 1 << l
        v = g.same[:, l, :].rearrange("p (n b) -> p n b", b=b)
        count(pool.affine_select(out=v, in_=v, compare_op=ALU.is_ge, fill=0.0, base=b - 1,
                                 pattern=[[b, P // b], [0, b]], channel_multiplier=-1))
    pool.wait_ge(made_masks, c[0])
    count(pool.tensor_tensor(g.lvl[:, :, :], g.same[:, 1:LEVELS + 2, :], g.same[:, 0:LEVELS + 1, :], ALU.subtract))


def phase_scan(nc, g, zt, yt):
    with ExitStack() as ctx:
        sb = lambda n, s, d=F32: ctx.enter_context(nc.sbuf_tensor(n, s, d))
        sem = nc.alloc_semaphore
        S2, H2 = range(2), range(2)
        bank = [[ctx.enter_context(nc.psum_tensor(f"sbank{s}{b}", [P, NQ, P], F32)) for b in range(4)] for s in S2]
        r_in, k_in, kk_in, sw_in, ic_in = ([[sb(f"{n}{s}{h}", [P, NQ, CH]) for h in H2] for s in S2]
                                           for n in ("r_in", "k_in", "kk_in", "sw_in", "ic_in"))
        v_bd = [[sb(f"v_bd{s}{h}", [P, NQ, P]) for h in H2] for s in S2]
        ar_bd = [[sb(f"ar_bd{s}{h}", [P, NQ, 2 * P]) for h in H2] for s in S2]
        b_bd = [[sb(f"b_bd{s}{h}", [P, NQ, P]) for h in H2] for s in S2]
        k_bd = [[sb(f"k_bd{s}{h}", [P, NQ, P]) for h in H2] for s in S2]
        g_end = [[sb(f"g_end{s}{h}", [P, NQ]) for h in H2] for s in S2]
        state = [[sb(f"state{s}{h}", [P, NQ, P]) for h in H2] for s in S2]
        y_sb = [[sb(f"y_sb{s}{h}", [P, NQ, CH]) for h in H2] for s in S2]
        lw, cum, ex, e_in, e_inv, e_ex, kd, b0 = ([sb(f"{n}{s}", [P, NQ, CH]) for s in S2]
                                                  for n in ("lw", "cum", "ex", "e_in", "e_inv", "e_ex", "kd", "b0"))
        ab = [sb(f"ab{s}", [P, NQ, 2 * P]) for s in S2]
        ak = [sb(f"ak{s}", [P, NQ, 2 * P]) for s in S2]
        m_ab, xt, x, z, b_t, k_t, v_t, w_sb, xw, w2, sa, tn = (
            [sb(f"{n}{s}", [P, NQ, P]) for s in S2]
            for n in ("m_ab", "xt", "x", "z", "b_t", "k_t", "v_t", "w_sb", "xw", "w2", "sa", "tn"))
        m_lvl = [[sb(f"m_lvl{s}{i}", [P, NQ, P]) for i in range(2)] for s in S2]
        seg, tri, lvl = g.seg, g.tri, g.lvl
        landed = [[sem(f"in_landed{s}{h}") for h in H2] for s in S2]
        v_landed = [[sem(f"v_landed{s}{h}") for h in H2] for s in S2]
        prep_chain = [sem(f"prep_chain{s}") for s in S2]
        exp_in, exp_done, prep_ready = ([sem(f"{n}{s}") for s in S2] for n in ("exp_in", "exp_done", "prep_ready"))
        pe_done = [sem(f"scan_made{s}") for s in S2]
        taken_by = {e: [sem(f"taken_{e}{s}") for s in S2] for e in ("dve", "act")}
        pool_done = [sem(f"pool_done{s}") for s in S2]
        y_stored = [[sem(f"y_stored{s}{h}") for h in H2] for s in S2]
        tn_added = [sem(f"tn_added{s}") for s in S2]
        v_zeroed, zeroed = sem("v_zeroed"), sem("scan_zeroed")
        N_POOL = 2 + LEVELS

        def chunk_start(s, i):
            return i * CH if s == 0 else i * (-CH) + (SEQ - CH)

        def wait_taken(eng, s, it, *names):
            need = {}
            for n in names:
                e, c = taken(n)
                need[e] = max(need.get(e, 0), c)
            for e, c in need.items():
                eng.wait_ge(taken_by[e][s], it * N_EV[e] + c)

        with nc.Block() as block:
            @block.gpsimd
            def _(pool):
                for s in S2:
                    for h in H2:
                        pool.memset(v_bd[s][h][:, :, :], 0.0).then_inc(v_zeroed, 1)

                def lmask(l):
                    return lvl[:, l:l + 1, :].broadcast_to([P, NQ, P])
                eye = g.ident[:, :].unsqueeze(1).broadcast_to([P, NQ, P])
                with pool.Fori(0, NCH) as i:
                    for h in H2:
                        it = i * 2 + h
                        for s in S2:
                            wait_taken(pool, s, it, "ab1")
                            pool.tensor_tensor(xt[s][:, :, :], ab[s][:, :, 0:P], lmask(0), ALU.mult).then_inc(pool_done[s], 1)
                            wait_taken(pool, s, it, "mab")
                            pool.tensor_tensor(x[s][:, :, :], m_ab[s][:, :, :], lmask(0), ALU.mult).then_inc(pool_done[s], 1)
                            pool.wait_ge(pool_done[s], it * (N_POOL + 2) + 2)
                            pool.tensor_tensor(xt[s][:, :, :], xt[s][:, :, :], eye, ALU.add).then_inc(pool_done[s], 1)
                            pool.tensor_tensor(x[s][:, :, :], x[s][:, :, :], eye, ALU.add).then_inc(pool_done[s], 1)
                        for l in range(1, LEVELS + 1):
                            for s in S2:
                                if l > 2:
                                    pool.wait_ge(pe_done[s], it * N_PE + made(f"z{l - 2}"))
                                src = m_ab[s][:, :, :] if l < LEVELS else ab[s][:, :, 0:P]
                                pool.tensor_tensor(m_lvl[s][l % 2][:, :, :], src, lmask(l),
                                                   ALU.mult).then_inc(pool_done[s], 1)

            @block.sync
            def _(sp):
                def load(s, h, at, first=False):
                    rows = lambda base: zt[base + h * (NQ * P):base + (h + 1) * (NQ * P), bass.ds(at, CH)].rearrange("(q p) c -> p q c", p=P)
                    for dst, base in ((r_in, ROW_RKV), (k_in, ROW_RKV + RW), (kk_in, ROW_KK),
                                      (sw_in, ROW_SW + s * RW), (ic_in, ROW_IC + s * RW)):
                        sp.dma_start(dst[s][h][:, :, :], rows(base)).then_inc(landed[s][h], 16)
                    if first:
                        sp.wait_ge(v_zeroed, 4)
                    v = rows(ROW_RKV + 2 * RW)
                    for e in range(2):
                        sp.dma_start(v_bd[s][h][64 * e:64 * e + 64, :, 64 * e:64 * e + 64],
                                     v[64 * e:64 * e + 64]).then_inc(v_landed[s][h], 16)

                def store(s, h, i, at):
                    sp.wait_ge(taken_by["act"][s], i * (2 * N_EV["act"]) + (h * N_EV["act"] + taken("y")[1]))
                    sp.dma_start(yt[s, h * NQ * P:(h + 1) * NQ * P, bass.ds(at, CH)].rearrange("(q p) c -> p q c", p=P),
                                 y_sb[s][h][:, :, :]).then_inc(y_stored[s][h], 16)
                for h in H2:
                    for s in S2:
                        load(s, h, chunk_start(s, 0), first=True)
                with sp.Fori(0, NCH - 1) as i:
                    now = [sp.snap(chunk_start(s, i)) for s in S2]
                    ahead = [sp.snap(chunk_start(s, i + 1)) for s in S2]
                    for h in H2:
                        for s in S2:
                            sp.wait_ge(pe_done[s], i * (2 * N_PE) + (h * N_PE + made("tv")))
                            load(s, h, ahead[s])
                        for s in S2:
                            store(s, h, i, now[s])
                for h in H2:
                    for s in S2:
                        store(s, h, NCH - 1, chunk_start(s, NCH - 1))
                for s in S2:
                    for h in H2:
                        sp.wait_ge(y_stored[s][h], 16 * NCH)

            @block.scalar
            def _(act):
                def exponents(i, h):
                    it = i * 2 + h
                    for s in S2:
                        act.wait_ge(exp_in[s], it + 1)
                        act.activation(e_in[s][:, :, :], cum[s][:, :, :], ACT.Exp)
                        act.activation(e_inv[s][:, :, :], cum[s][:, :, :], ACT.Exp, scale=-1.0)
                        act.activation(e_ex[s][:, :, :], ex[s][:, :, :], ACT.Exp)
                        last = CH - 1 if s == 0 else 0
                        act.activation(g_end[s][h][:, :], cum[s][:, :, last], ACT.Exp).then_inc(exp_done[s], 1)

                def stages(i, h, ahead):
                    it = i * 2 + h
                    for name, b, e in SCAN_STAGES:
                        if ahead and name == AHEAD_EXPONENTS:
                            exponents(*ahead)
                        if e != "act":
                            continue
                        for s in S2:
                            act.wait_ge(pe_done[s], it * N_PE + made(name))
                            src = bank[s][b]
                            if name == "y":
                                act.wait_ge(y_stored[s][h], i * 16)
                                act.copy(y_sb[s][h][0:64, :, :], src[0:64, :, 0:64])
                                act.copy(y_sb[s][h][64:128, :, :], src[64:128, :, 64:128]).then_inc(taken_by["act"][s], 1)
                            else:
                                dst = {"tb": b_t, "tk": k_t, "tv": v_t, "w": w_sb, "v": xw}.get(name)
                                dst = dst or (z if name[0] == "z" else x)
                                act.copy(dst[s][:, :, :], src[:, :, :]).then_inc(taken_by["act"][s], 1)

                def turn(i, last):
                    stages(i, 0, (i, 1))
                    stages(i, 1, None if last else (i + 1, 0))
                exponents(0, 0)
                with act.Fori(0, NCH - 1) as i:
                    turn(i, False)
                turn(NCH - 1, True)

            @block.vector
            def _(dve):
                for h in H2:
                    for s in S2:
                        for t in (ar_bd, b_bd, k_bd, state):
                            dve.memset(t[s][h][:, :, :], 0.0).then_inc(zeroed, 1)
                dve.wait_ge(zeroed, 16)
                def decays(i, h):
                    it = i * 2 + h
                    for s in S2:
                        PC = 5 + s
                        pc = lambda c: it * PC + c
                        W = lambda t: t[:, :, :]
                        dve.wait_ge(landed[s][h], i * 80 + 80)
                        dve.tensor_scalar(W(lw[s]), W(sw_in[s][h]), -DECAY_SCALE, None, ALU.mult).then_inc(prep_chain[s], 1)
                        ka = param(g, "k_a", h * NQ, NQ).unsqueeze(2).broadcast_to([P, NQ, CH])
                        dve.scalar_tensor_tensor(out=W(kd[s]), in0=W(ic_in[s][h]), scalar=-1.0, in1=ka,
                                                 op0=ALU.add, op1=ALU.mult).then_inc(prep_chain[s], 1)
                        dve.wait_ge(prep_chain[s], pc(1))
                        dve.tensor_tensor_scan(cum[s][:, :, :].rearrange("p q c -> p (q c)"), seg[:, :],
                                               lw[s][:, :, :].rearrange("p q c -> p (q c)"), 0.0,
                                               ALU.mult, ALU.add).then_inc(prep_chain[s], 1)
                        dve.tensor_tensor(W(b0[s]), W(kk_in[s][h]), W(ic_in[s][h]), ALU.mult).then_inc(prep_chain[s], 1)
                        dve.wait_ge(prep_chain[s], pc(3))
                        if s == 0:
                            dve.tensor_tensor(W(ex[s]), W(cum[s]), W(lw[s]), ALU.subtract).then_inc(exp_in[s], 1)
                        else:
                            total = cum[s][:, :, CH - 1:CH].broadcast_to([P, NQ, CH])
                            dve.tensor_tensor(W(ex[s]), total, W(cum[s]), ALU.subtract).then_inc(prep_chain[s], 1)
                            dve.wait_ge(prep_chain[s], pc(5))
                            dve.tensor_tensor(W(cum[s]), W(ex[s]), W(lw[s]), ALU.add).then_inc(exp_in[s], 1)
                        dve.scalar_tensor_tensor(out=W(kd[s]), in0=W(kd[s]), scalar=1.0, in1=W(k_in[s][h]),
                                                 op0=ALU.add, op1=ALU.mult).then_inc(prep_chain[s], 1)
                def operands(i, h):
                    it = i * 2 + h
                    for s in S2:
                        dve.wait_ge(exp_done[s], it + 1)
                        dve.wait_ge(prep_chain[s], it * (5 + s) + (5 + s))
                        ar, bb, kb = ar_bd[s][h], b_bd[s][h], k_bd[s][h]
                        for e in range(2):
                            r, c = slice(64 * e, 64 * e + 64), slice(64 * e, 64 * e + 64)
                            c2 = slice(P + 64 * e, P + 64 * e + 64)
                            dve.scalar_tensor_tensor(out=ar[r, :, c], in0=kk_in[s][h][r], scalar=-1.0, in1=e_ex[s][r],
                                                     op0=ALU.mult, op1=ALU.mult)
                            dve.tensor_tensor(ar[r, :, c2], r_in[s][h][r], e_in[s][r], ALU.mult)
                            dve.tensor_tensor(bb[r, :, c], b0[s][r], e_inv[s][r], ALU.mult)
                            ins = dve.tensor_tensor(kb[r, :, c], kd[s][r], e_inv[s][r], ALU.mult)
                        ins.then_inc(prep_ready[s], 1)
                def stages(i, h, ahead):
                    it = i * 2 + h
                    for name, b, e in SCAN_STAGES:
                        if ahead and name == AHEAD_DECAYS:
                            decays(*ahead)
                        if ahead and name == AHEAD_OPERANDS:
                            operands(*ahead)
                        if e != "dve":
                            continue
                        for s in S2:
                            src = bank[s][b]
                            dve.wait_ge(pe_done[s], it * N_PE + made(name))
                            if name in ("ab0", "ab1", "ak0", "ak1"):
                                dst, q = (ab if name[1] == "b" else ak)[s], 2 * int(name[2])
                                dve.tensor_tensor(dst[:, q:q + 2, :], src[:, :, :].rearrange("p (a b) c -> p a (b c)", b=2),
                                                  tri[s][:, :].unsqueeze(1).broadcast_to([P, 2, 2 * P]), ALU.mult).then_inc(taken_by["dve"][s], 1)
                            elif name == "mab":
                                dve.tensor_tensor(m_ab[s][:, :, :], src[:, :, :],
                                                  tri[1 - s][:, 0:P].unsqueeze(1).broadcast_to([P, NQ, P]), ALU.mult).then_inc(taken_by["dve"][s], 1)
                            elif name[0] == "u":
                                dve.wait_ge(pool_done[s], it * (N_POOL + 2) + 4)
                                dve.tensor_tensor(xt[s][:, :, :], xt[s][:, :, :], src[:, :, :], ALU.add).then_inc(taken_by["dve"][s], 1)
                            elif name == "m":
                                wait_taken(dve, s, it, "w")
                                dve.tensor_tensor(w2[s][:, :, :], w_sb[s][:, :, :], src[:, :, :], ALU.add).then_inc(taken_by["dve"][s], 1)
                            elif name == "sa":
                                dve.tensor_copy(sa[s][:, :, :], src[:, :, :]).then_inc(taken_by["dve"][s], 1)
                            else:
                                st = state[s][h]
                                dve.tensor_tensor(tn[s][:, :, :], st[:, :, :], src[:, :, :], ALU.add).then_inc(tn_added[s], 1)
                                dve.wait_ge(tn_added[s], it + 1)
                                dve.tensor_tensor(st[:, :, :], tn[s][:, :, :], g_end[s][h][:, :].unsqueeze(2).broadcast_to([P, NQ, P]),
                                                  ALU.mult).then_inc(taken_by["dve"][s], 1)

                def turn(i, last):
                    stages(i, 0, (i, 1))
                    stages(i, 1, None if last else (i + 1, 0))
                decays(0, 0)
                operands(0, 0)
                with dve.Fori(0, NCH - 1) as i:
                    turn(i, False)
                turn(NCH - 1, True)

            @block.tensor
            def _(pe):
                with pe.Fori(0, NCH) as i:
                    for h in H2:
                        it = i * 2 + h
                        for s in S2:
                            pe.wait_ge(taken_by["dve"][s], it * N_EV["dve"])
                            pe.wait_ge(taken_by["act"][s], it * N_EV["act"])
                        for name, b, _ in SCAN_STAGES:
                            for s in S2:
                                ar, bb, kb, vb, st = ar_bd[s][h], b_bd[s][h], k_bd[s][h], v_bd[s][h], state[s][h]
                                o = bank[s][b]
                                if bank_before(name):
                                    wait_taken(pe, s, it, bank_before(name))
                                mm = lambda q, lhs, rhs, start=True, stop=True: pe.matmul(o[:, q, :], lhs, rhs, start=start, stop=stop)
                                Q = range(NQ)
                                if name in ("ab0", "ab1", "ak0", "ak1"):
                                    pe.wait_ge(prep_ready[s], it + 1)
                                    w = bb if name[1] == "b" else kb
                                    for j in range(2):
                                        q = 2 * int(name[2]) + j
                                        ins = pe.matmul(o[:, 2 * j:2 * j + 2, :].rearrange("p a b -> p (a b)"), w[:, q, :], ar[:, q, :], start=True, stop=True)
                                elif name == "mab":
                                    for q in Q:
                                        ins = mm(q, ar[:, q, 0:P], bb[:, q, :])
                                elif name in ("tb", "tk", "tv"):
                                    if name == "tv":
                                        pe.wait_ge(v_landed[s][h], i * 32 + 32)
                                    src = {"tb": bb[:, :, :], "tk": kb[:, :, :], "tv": vb[:, :, :]}[name]
                                    for q in Q:
                                        ins = pe.transpose(o[:, q, :], src[:, q, :], g.ident[:, :])
                                elif name == "w":
                                    wait_taken(pe, s, it, "ak1", "tv")
                                    for q in Q:
                                        mm(q, ar[:, q, 0:P], st[:, q, :], True, False)
                                        ins = mm(q, ak[s][:, q, 0:P], v_t[s][:, q, :], False, True)
                                elif name[0] == "z":
                                    l = int(name[1])
                                    pe.wait_ge(pool_done[s], it * (N_POOL + 2) + (4 + l))
                                    if l > 1:
                                        wait_taken(pe, s, it, f"u{l - 1}")
                                    for q in Q:
                                        ins = mm(q, m_lvl[s][l % 2][:, q, :], xt[s][:, q, :])
                                elif name[0] == "u":
                                    l = int(name[1])
                                    wait_taken(pe, s, it, f"z{l}", *([f"x{l - 1}"] if l > 1 else []))
                                    for q in Q:
                                        ins = mm(q, x[s][:, q, :], z[s][:, q, :])
                                elif name[0] == "x":
                                    wait_taken(pe, s, it, f"u{name[1]}")
                                    for q in Q:
                                        ins = pe.transpose(o[:, q, :], xt[s][:, q, :], g.ident[:, :])
                                elif name in ("v", "sa"):
                                    wait_taken(pe, s, it, *((f"u{LEVELS - 1}", "w") if name == "v" else ("m",)))
                                    for q in Q:
                                        ins = mm(q, xt[s][:, q, :], (w_sb if name == "v" else w2)[s][:, q, :])
                                elif name == "m":
                                    wait_taken(pe, s, it, "v")
                                    pe.wait_ge(pool_done[s], it * (N_POOL + 2) + (4 + LEVELS))
                                    for q in Q:
                                        ins = mm(q, m_lvl[s][LEVELS % 2][:, q, :], xw[s][:, q, :])
                                elif name == "y":
                                    wait_taken(pe, s, it, "sa")
                                    for q in Q:
                                        mm(q, st[:, q, :], ar[:, q, P:2 * P], True, False)
                                        mm(q, v_t[s][:, q, :], ak[s][:, q, P:2 * P], False, False)
                                        ins = mm(q, sa[s][:, q, :], ab[s][:, q, P:2 * P], False, True)
                                else:
                                    for q in Q:
                                        mm(q, k_t[s][:, q, :], v_t[s][:, q, :], True, False)
                                        ins = mm(q, b_t[s][:, q, :], sa[s][:, q, :], False, True)
                                ins.then_inc(pe_done[s], 1)



def rsqrt_newton(eng_wait, dve, y, t, s):
    eng_wait(dve.reciprocal(y, y))
    eng_wait(dve.tensor_tensor(t, y, y, ALU.mult))
    eng_wait(dve.tensor_tensor(t, t, s, ALU.mult))
    eng_wait(dve.tensor_scalar(t, t, -0.5, 1.5, ALU.mult, ALU.add))


def windows(t):
    return min(max(P * t - 64, 0), SEQ - 2 * P)


def phase_attention(nc, g, zt):
    U = [(gr, e) for gr in range(3) for e in range(2)]
    NU = len(U)
    NP = ATTN_HPG // 2
    with ExitStack() as ctx:
        sb = lambda n, s, d=F32: ctx.enter_context(nc.sbuf_tensor(n, s, d))
        sem = nc.alloc_semaphore
        q_sb, k_sb, v_sb = ([sb(f"{n}{i}", [P, SEQ]) for i in range(3)] for n in ("q_sb", "k_sb", "v_sb"))
        q_r, k_r, v_r = (sb(n, [P, SEQ]) for n in ("q_r", "k_r", "v_r"))
        v_tok = [sb(f"v_tok{i}", [P, 7 if i == 0 else 4, P]) for i in range(3)]
        made_masks = sem("made_masks")
        dist = sb("dist", [P, 5, 2 * P])
        slope = sb("slope", [P, 3, ATTN_HPG])
        s_sb = [sb(f"s_sb{i}", [P, 4, 2 * P]) for i in range(2)]
        p_sb = [sb(f"p_sb{i}", [P, 4, 2 * P]) for i in range(2)]
        p_t = [sb(f"p_t{i}", [P, 8, P]) for i in range(2)]
        negmax = [sb(f"negmax{i}", [P, 4]) for i in range(2)]
        den = [sb(f"den{i}", [P, 4]) for i in range(2)]
        mx_all, dn_all = ([sb(f"{n}{i}", [P, ATTN_HPG, 4]) for i in range(3)] for n in ("mx_all", "dn_all"))
        u_all = [sb(f"u_all{i}", [P, NP, SEQ]) for i in range(3)]
        sel = sb("sel", [ATTN_HPG, ATTN_HPG, HEAD_DIM])
        sc_ps = [ctx.enter_context(nc.psum_tensor(f"sc_ps{i}", [P, 4, 2 * P], F32)) for i in range(2)]
        pt_ps = ctx.enter_context(nc.psum_tensor("pt_ps", [P, 8, P], F32))
        pv_ps = ctx.enter_context(nc.psum_tensor("pv_ps", [P, SEQ], F32))
        vt_ps = ctx.enter_context(nc.psum_tensor("vt_ps", [P, 4, P], F32))
        consts, dist_c, landed, vt_done, vt_taken, sc_done, biased, max_ready, neg_ready, exp_done, den_c, pt_done, pt_taken, pv_done, pv_taken, slopes_c, by_res = (
            sem(n) for n in ("a_consts", "a_dist", "a_landed", "vt_done", "vt_taken", "sc_done", "biased", "max_ready", "neg_ready",
                             "exp_done", "den_copied", "pt_done", "pt_taken", "pv_done", "pv_taken", "slopes_c", "by_residue"))

        def tokens(t, gr, i):
            if gr == 0:
                return t[:, i * P:(i + 1) * P]
            if gr == 1:
                return t.rearrange("p (m r) -> p r m", r=4)[:, i, :]
            return t[:, i * P:(i + 1) * P]

        def vstarts(gr):
            return [0, 64, 128, 192, 256, 320, 384] if gr == 0 else [P * i for i in range(4)]
        VT = [(gr, c) for gr in range(3) for c in range(2 if gr == 0 else 1)]
        with nc.Block() as block:
            @block.gpsimd
            def _(pool):
                for gr in range(3):
                    for h in range(ATTN_HPG):
                        v = -2.0 ** (-8.0 * (gr * ATTN_HPG + h + 1) / ATTN_HEADS)
                        pool.memset(slope[:, gr, h:h + 1], v).then_inc(slopes_c, 1)
                pool.memset(sel[:, :, :], 0.0).then_inc(consts, 1)
                pool.wait_ge(consts, 1)
                pool.affine_select(out=sel[:, :, :], in_=sel[:, :, :], compare_op=ALU.not_equal, fill=1.0, base=0,
                                   pattern=[[-1, ATTN_HPG], [0, HEAD_DIM]], channel_multiplier=1).then_inc(consts, 1)
                for j, (off, dil) in enumerate(((0, 1), (-64, 1), (-P, 1), (0, 4))):
                    n = 2 * P if j < 3 else P
                    pool.iota(dist[:, j, 0:n], base=off * dil, pattern=[[dil, n]], channel_multiplier=-dil,
                              allow_small_or_imprecise_dtypes=True).then_inc(consts, 1)
                pool.iota(dist[:, 4, 0:P], base=0, pattern=[[16, P]], channel_multiplier=-16,
                          allow_small_or_imprecise_dtypes=True).then_inc(consts, 1)
                pool.wait_ge(consts, 7)
                pool.wait_ge(dist_c, 2)
                FAR = 1e33
                for j, off in enumerate((0, -64, -P, 0)):
                    n = 2 * P if j < 3 else P
                    v = dist[:, j, 0:n]
                    for k, sg in enumerate((1, -1)):
                        pool.affine_select(out=v, in_=v, compare_op=ALU.is_ge, fill=FAR, base=64 + sg * off,
                                           pattern=[[sg, n]], channel_multiplier=-sg).then_inc(consts, 1)
                        pool.wait_ge(consts, 7 + 2 * j + k + 1)
                v = dist[:, 4, 0:P].rearrange("p (n b) -> p n b", b=32)
                pool.affine_select(out=v, in_=v, compare_op=ALU.is_ge, fill=FAR, base=0,
                                   pattern=[[-32, 4], [0, 32]], channel_multiplier=1).then_inc(consts, 1)
                pool.wait_ge(consts, 16)
                pool.affine_select(out=v, in_=v, compare_op=ALU.is_ge, fill=FAR, base=31,
                                   pattern=[[32, 4], [0, 32]], channel_multiplier=-1).then_inc(consts, 1)
                scan_masks(pool, g, made_masks)

            @block.sync
            def _(sp):
                with sp.Fori(0, NP) as j:
                    sp.wait_ge(sc_done, j * NU)
                    for gr in range(3):
                        for dst, base in ((q_sb, 0), (k_sb, ATTN_WIDTH), (v_sb, 2 * ATTN_WIDTH)):
                            row = j * P + (ROW_ATTN + base + gr * ATTN_HPG * HEAD_DIM)
                            sp.dma_start(dst[gr][:, :], zt[bass.ds(row, P), :]).then_inc(landed, 16)

            @block.tensor
            def _(pe):
                pe.wait_ge(consts, 17)
                with pe.Fori(0, NP) as j:
                    pe.wait_ge(landed, j * 144 + 144)
                    pe.wait_ge(by_res, j * 3 + 3)
                    for n, (gr, c) in enumerate(VT):
                        pe.wait_ge(vt_taken, j * len(VT) + n)
                        starts = vstarts(gr)[4 * c:4 * c + 4]
                        for b, st in enumerate(starts):
                            src = v_sb[gr][:, st:st + P] if gr == 0 else tokens((v_sb[1], v_r)[gr - 1][:, :], gr, st // P)
                            ins = pe.transpose(vt_ps[:, b, :], src, g.ident[:, :])
                        ins.then_inc(vt_done, 1)

                    def scores(u):
                        gr, e = U[u]
                        r = slice(64 * e, 64 * e + 64)
                        if u >= 2:
                            pe.wait_ge(biased, j * NU + (u - 1))
                        for t in range(4):
                            if gr == 0:
                                w = windows(t)
                                ins = pe.matmul(sc_ps[u % 2][:, t, :], q_sb[0][r, t * P:(t + 1) * P],
                                                k_sb[0][r, w:w + 2 * P], start=True, stop=True)
                            else:
                                ins = pe.matmul(sc_ps[u % 2][:, t, 0:P], tokens((q_sb[1], q_r)[gr - 1][r, :], gr, t),
                                                tokens((k_sb[1], k_r)[gr - 1][r, :], gr, t), start=True, stop=True)
                        ins.then_inc(sc_done, 1)

                    def weighted(u):
                        gr, e = U[u]
                        nb = 2 if gr == 0 else 1
                        pe.wait_ge(exp_done, j * NU + (u + 1))
                        pe.wait_ge(pt_taken, j * NU + u)
                        for t in range(4):
                            for b in range(nb):
                                ins = pe.transpose(pt_ps[:, t * nb + b, :], p_sb[u % 2][:, t, b * P:(b + 1) * P], g.ident[:, :])
                        ins.then_inc(pt_done, 1)
                        pe.wait_ge(pt_taken, j * NU + (u + 1))
                        pe.wait_ge(pv_taken, j * NU + u)
                        pe.wait_ge(vt_taken, j * len(VT) + len(VT))
                        for t in range(4):
                            for b in range(nb):
                                vi = vstarts(0).index(windows(t) + b * P) if gr == 0 else t
                                ins = pe.matmul(pv_ps[64 * e:64 * e + 64, t * P:(t + 1) * P], v_tok[gr][:, vi, 64 * e:64 * e + 64],
                                                p_t[u % 2][:, t * nb + b, :], start=b == 0, stop=b == nb - 1, skip_group_check=True)
                        ins.then_inc(pv_done, 1)
                    pe.wait_ge(biased, j * NU)
                    scores(0)
                    for u in range(NU):
                        if u + 1 < NU:
                            scores(u + 1)
                        weighted(u)

            @block.scalar
            def _(act):
                with act.Fori(0, NP) as j:
                    act.wait_ge(landed, j * 144 + 144)
                    act.wait_ge(sc_done, j * NU)
                    for src, dst in ((q_sb, q_r), (k_sb, k_r), (v_sb, v_r)):
                        act.copy(dst[:, :].rearrange("p (r m) -> p r m", r=16),
                                 src[2][:, :].rearrange("p (m r) -> p r m", r=16)).then_inc(by_res, 1)
                    for n, (gr, c) in enumerate(VT):
                        act.wait_ge(vt_done, j * len(VT) + (n + 1))
                        k = len(vstarts(gr)[4 * c:4 * c + 4])
                        if n == 0:
                            act.wait_ge(pv_done, j * NU)
                        act.copy(v_tok[gr][:, 4 * c:4 * c + k, :], vt_ps[:, 0:k, :]).then_inc(vt_taken, 1)
                    for u, (gr, e) in enumerate(U):
                        nk = 2 * P if gr == 0 else P
                        act.wait_ge(neg_ready, j * NU + (u + 1))
                        act.wait_ge(pt_done, j * NU + max(u - 1, 0))
                        act.wait_ge(den_c, j * NU + max(u - 1, 0))
                        for t in range(4):
                            ins = act.activation(p_sb[u % 2][:, t, 0:nk], s_sb[u % 2][:, t, 0:nk], ACT.Exp,
                                                 bias=negmax[u % 2][:, t:t + 1], accum_out=den[u % 2][:, t:t + 1])
                        ins.then_inc(exp_done, 1)
                        act.wait_ge(pt_done, j * NU + (u + 1))
                        act.wait_ge(pv_done, j * NU + max(u - 1, 0))
                        nb = 8 if gr == 0 else 4
                        act.copy(p_t[u % 2][:, 0:nb, :], pt_ps[:, 0:nb, :]).then_inc(pt_taken, 1)

            @block.vector
            def _(dve):
                dve.wait_ge(consts, 7)
                for n, v in enumerate((dist[:, 0:3, :], dist[:, 3:5, 0:P])):
                    dve.scalar_tensor_tensor(out=v, in0=v, scalar=-1.0, in1=v, op0=ALU.mult, op1=ALU.max).then_inc(dist_c, 1)
                dve.wait_ge(consts, 17)
                dve.wait_ge(slopes_c, 24)
                with dve.Fori(0, NP) as j:
                    def soft(u):
                        gr, e = U[u]
                        nk = 2 * P if gr == 0 else P
                        dve.wait_ge(sc_done, j * NU + (u + 1))
                        dve.wait_ge(exp_done, j * NU + max(u - 1, 0))
                        sl = slope[:, gr, bass.ds(j * 2 + e, 1)]
                        parts = ([(0, 1, 0), (1, 3, 1), (3, 4, 2)] if gr == 0 else [(0, 4, 2 + gr)])
                        for a0, a1, dj in parts:
                            ins = dve.scalar_tensor_tensor(out=s_sb[u % 2][:, a0:a1, 0:nk],
                                                           in0=dist[:, dj:dj + 1, 0:nk].broadcast_to([P, a1 - a0, nk]), scalar=sl,
                                                           in1=sc_ps[u % 2][:, a0:a1, 0:nk], op0=ALU.mult, op1=ALU.add)
                        ins.then_inc(biased, 1)
                        dve.wait_ge(biased, j * NU + (u + 1))
                        m = mx_all[gr][:, bass.ds(j * 2 + e, 1), :]
                        dve.tensor_reduce(m.rearrange("p a t -> p (a t)"), s_sb[u % 2][:, :, 0:nk], AX.X, ALU.max).then_inc(max_ready, 1)
                        dve.wait_ge(max_ready, j * NU + (u + 1))
                        dve.tensor_scalar(negmax[u % 2][:, :], m.rearrange("p a t -> p (a t)"), -1.0, None, ALU.mult).then_inc(neg_ready, 1)

                    def file(u):
                        gr, e = U[u]
                        dve.wait_ge(exp_done, j * NU + (u + 1))
                        dve.tensor_copy(dn_all[gr][:, bass.ds(j * 2 + e, 1), :].rearrange("p a t -> p (a t)"), den[u % 2][:, :]).then_inc(den_c, 1)
                        dve.wait_ge(pv_done, j * NU + (u + 1))
                        r = slice(64 * e, 64 * e + 64)
                        o = u_all[gr][r, bass.ds(j, 1), :].rearrange("p a n -> p (a n)")
                        if gr == 0:
                            dve.tensor_copy(o, pv_ps[r, :]).then_inc(pv_taken, 1)
                        else:
                            res = 4 if gr == 1 else 16
                            dve.tensor_copy(o.rearrange("p (m r) -> p r m", r=res),
                                            pv_ps[r, :].rearrange("p (r m) -> p r m", r=res)).then_inc(pv_taken, 1)
                    soft(0)
                    for u in range(NU):
                        if u + 1 < NU:
                            soft(u + 1)
                        file(u)
        phase_combine(nc, ctx, g, mx_all, dn_all, u_all, sel, sc_ps, pt_ps, pv_ps, vt_ps)


def phase_combine(nc, ctx, g, mx_all, dn_all, u_all, sel, sc_ps, pt_ps, pv_ps, vt_ps):
    H = ATTN_HPG
    sb = lambda n, s, d=F32: ctx.enter_context(nc.sbuf_tensor(n, s, d))
    sem = nc.alloc_semaphore
    m_row = [sb(f"m_row{i}", [H, SEQ]) for i in range(3)]
    d_row = [sb(f"d_row{i}", [H, SEQ]) for i in range(3)]
    m_top = sb("m_top", [H, SEQ])
    total = sb("total", [H, SEQ])
    oa_f = sb("oa_f", [P, H // 2, SEQ])
    turned, rows_ready, m_sub, exped, w_ready, bc, chain, o_ready, oh_ready, ol_ready = (sem(n) for n in (
        "turned", "rows_ready", "m_sub", "m_exped", "w_ready", "w_bc", "c_chain", "o_ready", "oh_ready", "ol_ready"))
    flat = [sc_ps[0][:, :, :].rearrange("p a b -> p (a b)"), sc_ps[1][:, :, :].rearrange("p a b -> p (a b)"),
            pt_ps[:, :, :].rearrange("p a b -> p (a b)")]

    def natural(v, gr):
        if gr == 0:
            return v.rearrange("p (t m) -> p t m", t=4)
        if gr == 1:
            return v.rearrange("p (m t) -> p t m", t=4)
        return v.rearrange("p (m t r) -> p t r m", t=4, r=4)
    with nc.Block() as block:
        @block.tensor
        def _(pe):
            for gr in range(3):
                for k, src in enumerate((mx_all, dn_all)):
                    for t in range(4):
                        ins = pe.transpose(flat[gr][0:H, k * SEQ + t * P:k * SEQ + (t + 1) * P], src[gr][:, :, t], g.ident[:, :])
                ins.then_inc(turned, 1)
            pe.wait_ge(w_ready, 3)
            n = 0
            for j in range(H // 2):
                for gr in range(3):
                    if n >= 2:
                        pe.wait_ge(chain, 8 + n - 1)
                    pe.matmul((pv_ps[:, :], vt_ps[:, :, :].rearrange("p a b -> p (a b)"))[n % 2],
                              sel[:, 2 * j:2 * j + 2, :].rearrange("h a b -> h (a b)"), m_row[gr][:, :], start=True, stop=True).then_inc(bc, 1)
                    n += 1

        @block.scalar
        def _(act):
            for gr in range(3):
                act.wait_ge(m_sub, gr + 1)
                act.activation(m_row[gr][:, :], m_row[gr][:, :], ACT.Exp).then_inc(exped, 1)
            for j in range(H // 2):
                act.wait_ge(o_ready, j + 1)
                act.copy(g.oa_hi[:, j, :], oa_f[:, j, :]).then_inc(oh_ready, 1)

        @block.gpsimd
        def _(pool):
            for j in range(H // 2):
                pool.wait_ge(oh_ready, j + 1)
                pool.tensor_tensor(g.oa_lo[:, j, :], oa_f[:, j, :], g.oa_hi[:, j, :].bitcast(F32), ALU.subtract).then_inc(ol_ready, 1)

        @block.vector
        def _(dve):
            n = [0]

            def link(ins):
                ins.then_inc(chain, 1)
                n[0] += 1
                dve.wait_ge(chain, n[0])
            for gr in range(3):
                dve.wait_ge(turned, gr + 1)
                for k, dst in enumerate((m_row, d_row)):
                    v = flat[gr][0:H, k * SEQ:(k + 1) * SEQ]
                    v = v.rearrange("p (t m) -> p t m", t=4) if gr < 2 else v.rearrange("p (t r m) -> p t r m", t=4, r=4)
                    dve.tensor_copy(natural(dst[gr][:, :], gr), v).then_inc(rows_ready, 1)
            dve.wait_ge(rows_ready, 6)
            link(dve.tensor_tensor(m_top[:, :], m_row[0][:, :], m_row[1][:, :], ALU.max))
            link(dve.tensor_tensor(m_top[:, :], m_top[:, :], m_row[2][:, :], ALU.max))
            for gr in range(3):
                dve.tensor_tensor(m_row[gr][:, :], m_row[gr][:, :], m_top[:, :], ALU.subtract).then_inc(m_sub, 1)
            dve.wait_ge(exped, 3)
            for gr in range(3):
                link(dve.tensor_tensor(d_row[gr][:, :], d_row[gr][:, :], m_row[gr][:, :], ALU.mult))
            link(dve.tensor_tensor(total[:, :], d_row[0][:, :], d_row[1][:, :], ALU.add))
            link(dve.tensor_tensor(total[:, :], total[:, :], d_row[2][:, :], ALU.add))
            link(dve.reciprocal(total[:, :], total[:, :]))
            dve.tensor_tensor(m_row[0][:, :], m_row[0][:, :], total[:, :], ALU.mult).then_inc(w_ready, 1)
            dve.tensor_tensor(m_row[1][:, :], m_row[1][:, :], total[:, :], ALU.mult).then_inc(w_ready, 1)
            dve.tensor_tensor(m_row[2][:, :], m_row[2][:, :], total[:, :], ALU.mult).then_inc(w_ready, 1)
            c = 0
            for j in range(H // 2):
                for gr in range(3):
                    dve.wait_ge(bc, c + 1)
                    w = (pv_ps[:, :], vt_ps[:, :, :].rearrange("p a b -> p (a b)"))[c % 2]
                    link(dve.tensor_tensor(u_all[gr][:, j, :], u_all[gr][:, j, :], w, ALU.mult))
                    c += 1
            for j in range(H // 2):
                dve.tensor_tensor(u_all[0][:, j, :], u_all[0][:, j, :], u_all[1][:, j, :], ALU.add).then_inc(rows_ready, 1)
                dve.wait_ge(rows_ready, 6 + j + 1)
                dve.tensor_tensor(oa_f[:, j, :], u_all[0][:, j, :], u_all[2][:, j, :], ALU.add).then_inc(o_ready, 1)


def phase_output(nc, g, a, zt, yt, xt, out):
    w_a = a["w_branch_attn"].rearrange("l (k p) n -> (l p) k n", p=P)
    w_b = a["w_branch_rwkv"].rearrange("l (k p) n -> (l p) k n", p=P)
    w_o = a["w_out"].rearrange("l (k p) n -> (l p) k n", p=P)
    w_g = a["w_ffn_gate"].rearrange("l (k p) n -> (l p) k n", p=P)
    w_u = a["w_ffn_up"].rearrange("l (k p) n -> (l p) k n", p=P)
    w_d = a["w_ffn_down"].rearrange("l (k p) n -> (l p) k n", p=P)
    KA, KB = ATTN_HPG * HEAD_DIM // P, RW // P
    NBLK = 4
    HB = KF // NBLK
    SB, SO, SF = KD, 2 * KD, 3 * KD
    PER = 2 * HB + KD
    with ExitStack() as ctx:
        sem = nc.alloc_semaphore
        bank = [ctx.enter_context(nc.psum_tensor(f"f_bank{i}", [P, SEQ], F32)) for i in range(8)]
        hid, plain = two_faced(nc, ctx, "hid", [P, 2 * HB, SEQ])
        hid_hi, hid_lo = hid[:, 0:HB, :], hid[:, HB:2 * HB, :]
        part = plain[:, 0:KD, :]
        mix = [plain[:, KD + i, :] for i in range(2)]
        merged = [plain[:, KD + 2 + i, :] for i in range(2)]
        xin = [plain[:, KD + 4 + i, :] for i in range(2)]
        NP = NPAIR
        wkv, y_back, bonus, gate = (g.act_plain[:, k * NP:(k + 1) * NP, :] for k in range(4))
        gsq, go = ([y_back[:, k + i, :] for i in range(2)] for k in (0, 2))
        gs, gy, gt = (y_back[0:2 * NP, k, :] for k in (4, 5, 6))
        to_heads = plain[:, KD + 4, 0:2 * NP * NP].rearrange("p (q h) -> p q h", h=2 * NP)
        from_heads = plain[0:2 * NP, KD + 2:KD + 4, :].rearrange("h a n -> h (a n)").rearrange("h (q c) -> h q c", c=P)
        sq_sum, s_sb, y, t_sb = (g.after_oa[:, i, :] for i in range(4))
        sq = [g.after_oa[:, 4 + i, :] for i in range(2)]
        h2f = [g.after_oa[:, 6 + i, :] for i in range(2)]
        sig, act_f = sq
        x2 = g.x2
        act_hi, act_lo = g.act_hi, g.act_lo
        (merged_ready, mhi_ready, mlo_ready, part_ready, gated, mix_used, x2_ready, sq_ready, sq_added, sq_summed, s_ready, root, chain,
         h2_ready, h2hi_ready, h2lo_ready, sig_ready, gs_ready, hid_ready, hhi_ready, hlo_ready, turned, staged) = (sem("f_" + n) for n in (
             "merged_ready", "mhi_ready", "mlo_ready", "part_ready", "gated", "mix_used", "x2_ready", "sq_ready", "sq_added", "sq_summed",
             "s_ready", "root", "chain", "h2_ready", "h2hi_ready", "h2lo_ready", "sig_ready", "gs_ready", "hid_ready",
             "hhi_ready", "hlo_ready", "turned", "staged"))
        mix_landed = [sem(f"f_mix_landed{i}") for i in range(2)]
        xin_landed = [sem(f"f_xin_landed{i}") for i in range(2)]
        out_stored = sem("f_out_stored")

        (w_ready, mean_made, d_ready, gsq_ready, var_made, gs_done, groot, gchain, gy_ready, bc_made, gn_chain, go_ready, ohi_ready,
         olo_ready, sel_ready, part_done) = (sem("g_" + n) for n in (
             "w_ready", "mean_made", "d_ready", "sq_ready", "var_made", "s_ready", "root", "chain", "y_ready", "bc_made", "gn_chain",
             "o_ready", "ohi_ready", "olo_ready", "sel_ready", "part_done"))
        y_landed = [sem(f"y_landed{i}") for i in range(4)]
        rest_landed = sem("bonus_gate_landed")

        def branch(i, j):
            return Step(SB + j, i, 2)

        def outp(i, j):
            return Step(SO + j, i, 2)

        def gate_up(b, i, j):
            return Step(SF + j, i, 2, b, PER)

        def down(b, i, j):
            return Step(SF + 2 * HB + j, i, 2, b, PER)

        def one(v):
            return v.rearrange("p a n -> p (a n)")

        with nc.Block() as block:
            @block.sync
            def _(sp):
                def mix_load(j, br, m):
                    sp.dma_start(mix[j], zt[bass.ds(m * P + (ROW_MIX + br * D_MODEL), P), :]).then_inc(mix_landed[j], 16)

                def attn_slab(m):
                    load_slab(sp, g, Step(m), [(KA, w_a[:, :, m * P:(m + 1) * P])])
                    if m >= 2:
                        sp.wait_ge(part_done, m - 1)
                    mix_load(m % 2, 0, m)
                for q in range(4):
                    for z, dst in enumerate((wkv, y_back)):
                        sp.dma_start(dst[:, 2 * q:2 * q + 2, :], yt[z, 2 * q * P:(2 * q + 2) * P, :].rearrange("(q p) n -> p q n", p=P)
                                     ).then_inc(y_landed[q], 16)
                    if q == 1:
                        attn_slab(0)
                        attn_slab(1)
                for row, dst in ((ROW_BONUS, bonus), (ROW_GATE, gate)):
                    sp.dma_start(dst, zt[row:row + RW, :].rearrange("(q p) n -> p q n", p=P)).then_inc(rest_landed, 16)
                for m in range(2, KD):
                    attn_slab(m)
                with sp.Fori(0, KD // 2) as i:
                    for j in range(2):
                        load_slab(sp, g, branch(i, j), [(KB, w_b[:, :, bass.ds(i * (2 * P) + j * P, P)])])
                    sp.wait_ge(part_done, KD)
                    sp.wait_ge(merged_ready, i * 2)
                    for j in range(2):
                        mix_load(j, 1, i * 2 + j)
                with sp.Fori(0, KD // 2) as i:
                    for j in range(2):
                        load_slab(sp, g, outp(i, j), [(KD, w_o[:, :, bass.ds(i * (2 * P) + j * P, P)])])
                    sp.wait_ge(x2_ready, i * 2)
                    for j in range(2):
                        sp.dma_start(xin[j], xt[bass.ds(i * (2 * P) + j * P, P), :]).then_inc(xin_landed[j], 16)
                with sp.Fori(0, NBLK) as b:
                    with sp.Fori(0, HB) as i:
                        for j, w in enumerate((w_g, w_u)):
                            load_slab(sp, g, gate_up(b, i, j), [(KD, w[:, :, bass.ds(b * (HB * P) + i * P, P)])])
                    with sp.Fori(0, KD // 2) as i:
                        for j in range(2):
                            load_slab(sp, g, down(b, i, j), [(HB, w_d[:, bass.ds(b * HB, HB), bass.ds(i * (2 * P) + j * P, P)])])
                for n in range(KD):
                    t, q = n % TT, n // TT
                    sp.wait_ge(staged, n + 1)
                    sp.dma_start(out[0, t * P:(t + 1) * P, q * SEQ:(q + 1) * SEQ], plain[:, n, :]).then_inc(out_stored, 16)
                sp.wait_ge(out_stored, 16 * KD)

            @block.tensor
            def _(pe):
                def attn_slab(m):
                    pe.wait_ge(g.w_lo_ready, m + 1)
                    if m >= 2:
                        pe.wait_ge(part_done, m - 1)
                    products(pe, g, Step(m), [(k, k) for k in range(KA)], bank[m % 2][:, :], g.oa_hi, g.oa_lo).then_inc(g.w_used, 1)
                for p in range(NP):
                    pe.wait_ge(w_ready, p + 1)
                    if p >= 2:
                        pe.wait_ge(d_ready, p - 1)
                    pe.matmul(bank[4 + p % 2][:, :], g.head_ones[:, :], wkv[:, p, :], start=True, stop=True).then_inc(mean_made, 1)
                for m in range(4):
                    attn_slab(m)
                pe.wait_ge(sel_ready, 6)
                for p in range(NP):
                    pe.wait_ge(gsq_ready, p + 1)
                    ins = pe.matmul(bank[6][0:2 * NP, :], to_heads[:, p, :], gsq[p % 2], start=p == 0, stop=p == NP - 1)
                    ins.then_inc(var_made, 1)
                for m in range(4, 8):
                    attn_slab(m)
                pe.wait_ge(gy_ready, 1)
                for p in range(NP):
                    if p >= 2:
                        pe.wait_ge(gn_chain, p - 1)
                    pe.matmul(bank[4 + p % 2][:, :], from_heads[:, p, :], gy, start=True, stop=True).then_inc(bc_made, 1)
                    attn_slab(8 + p)
                pe.wait_ge(olo_ready, NP)
                def slabs(step, first, freed, i, K, banks, hi, lo):
                    for j in range(2):
                        st = step(i, first + j)
                        pe.wait_ge(g.w_lo_ready, st.count())
                        if first:
                            pe.wait_ge(freed, i * 2 + (j + 1))
                        products(pe, g, st, [(k, k) for k in range(K)], bank[banks + j][:, :], hi, lo).then_inc(g.w_used, 1)
                slabs(branch, 0, None, 0, KB, 2, g.or_hi, g.or_lo)
                with pe.Fori(0, KD // 2 - 1) as i:
                    slabs(branch, 2, merged_ready, i, KB, 2, g.or_hi, g.or_lo)
                pe.wait_ge(mlo_ready, KD)
                slabs(outp, 0, None, 0, KD, 4, act_hi, act_lo)
                with pe.Fori(0, KD // 2 - 1) as i:
                    slabs(outp, 2, x2_ready, i, KD, 4, act_hi, act_lo)
                pe.wait_ge(sq_added, KD)
                pe.matmul(bank[2][:, :], g.all_ones[:, :], sq_sum, start=True, stop=True).then_inc(sq_summed, 1)
                pe.wait_ge(h2lo_ready, KD)
                with pe.Fori(0, NBLK) as b:
                    with pe.Fori(0, HB) as i:
                        for j in range(2):
                            st = gate_up(b, i, j)
                            pe.wait_ge(g.w_lo_ready, st.count())
                            pe.wait_ge(hid_ready if j else gs_ready, b * HB + i)
                            products(pe, g, st, [(k, k) for k in range(KD)], bank[6 + j][:, :], act_hi, act_lo).then_inc(g.w_used, 1)
                    with pe.Fori(0, KD // 2) as i:
                        for j in range(2):
                            st = down(b, i, j)
                            pe.wait_ge(g.w_lo_ready, st.count())
                            pe.wait_ge(hlo_ready, b * HB + HB)
                            pe.wait_ge(x2_ready, b * KD + i * 2 + (KD + j - 1))
                            products(pe, g, st, [(k, k) for k in range(HB)], bank[j][:, :], hid_hi, hid_lo).then_inc(g.w_used, 1)
                for n in range(KD):
                    t, q = n % TT, n // TT
                    pe.wait_ge(x2_ready, KD + (NBLK - 1) * KD + 4 * q + 4)
                    if n >= 2:
                        pe.wait_ge(staged, n - 1)
                    for m in range(4):
                        ins = pe.transpose(bank[2 + n % 2][:, m * P:(m + 1) * P], x2[:, 4 * q + m, t * P:(t + 1) * P], g.ident[:, :])
                    ins.then_inc(turned, 1)

            @block.scalar
            def _(act):
                for m in range(2):
                    split_hi(act, g, Step(m), KA)
                for p in range(NP):
                    act.wait_ge(d_ready, p + 1)
                    if p >= 2:
                        act.wait_ge(var_made, p - 1)
                    act.activation(gsq[p % 2], wkv[:, p, :], ACT.Square).then_inc(gsq_ready, 1)
                    if p < 2:
                        split_hi(act, g, Step(2 + p), KA)
                for m in range(4, 6):
                    split_hi(act, g, Step(m), KA)
                act.wait_ge(gs_done, 1)
                act.activation(gy, gs, ACT.Sqrt).then_inc(groot, 1)
                for m in range(6, 10):
                    split_hi(act, g, Step(m), KA)
                for p in range(NP):
                    act.wait_ge(go_ready, p + 1)
                    act.copy(g.or_hi[:, p, :], go[p % 2]).then_inc(ohi_ready, 1)
                    split_hi(act, g, Step(10 + p), KA if 10 + p < SB else KB)

                def high_merged(m, j):
                    act.wait_ge(merged_ready, m + 1)
                    act.copy(one(act_hi[:, bass.ds(m, 1), :]), merged[j]).then_inc(mhi_ready, 1)
                with act.Fori(0, KD // 2 - 1) as i:
                    for j in range(2):
                        split_hi(act, g, branch(i, j + 2), KB)
                        high_merged(i * 2 + j, j)
                for j in range(2):
                    split_hi(act, g, outp(0, j), KD)
                    high_merged(KD - 2 + j, j)
                with act.Fori(0, KD // 2 - 1) as i:
                    for j in range(2):
                        split_hi(act, g, outp(i, j + 2), KD)
                        act.wait_ge(x2_ready, i * 2 + (j + 1))
                        act.wait_ge(sq_added, i * 2)
                        act.activation(sq[j], one(x2[:, bass.ds(i * 2 + j, 1), :]), ACT.Square).then_inc(sq_ready, 1)
                for j in range(2):
                    act.wait_ge(x2_ready, KD - 1 + j)
                    act.wait_ge(sq_added, KD - 2)
                    act.activation(sq[j], x2[:, KD - 2 + j, :], ACT.Square).then_inc(sq_ready, 1)
                    split_hi(act, g, gate_up(0, 0, j), KD)
                act.wait_ge(s_ready, 1)
                act.activation(y, s_sb, ACT.Sqrt).then_inc(root, 1)
                for k in range(KD):
                    act.wait_ge(h2_ready, k + 1)
                    act.copy(act_hi[:, k, :], h2f[k % 2]).then_inc(h2hi_ready, 1)
                def block_of_hidden(b, last):
                    def sigmoid(i):
                        act.wait_ge(g.w_used, gate_up(b, i, 0).count())
                        act.wait_ge(gs_ready, b * HB + i)
                        act.activation(sig, bank[6][:, :], ACT.Sigmoid).then_inc(sig_ready, 1)

                    def high_hidden(i):
                        act.wait_ge(hid_ready, b * HB + (i + 1))
                        act.copy(one(hid_hi[:, bass.ds(i, 1), :]), act_f).then_inc(hhi_ready, 1)
                    with act.Fori(0, HB - 1) as i:
                        sigmoid(i)
                        for j in range(2):
                            split_hi(act, g, gate_up(b, i, j + 2), KD)
                        high_hidden(i)
                    sigmoid(HB - 1)
                    for j in range(2):
                        split_hi(act, g, down(b, 0, j), HB)
                    high_hidden(HB - 1)
                    with act.Fori(0, KD // 2 - 1) as i:
                        for j in range(2):
                            split_hi(act, g, down(b, i, j + 2), HB)
                    if not last:
                        for j in range(2):
                            split_hi(act, g, gate_up(b, 0, PER + j), KD)
                with act.Fori(0, NBLK - 1) as b:
                    block_of_hidden(b, False)
                block_of_hidden(NBLK - 1, True)

            @block.gpsimd
            def _(pool):
                for v in (to_heads, from_heads):
                    pool.memset(v, 1.0).then_inc(sel_ready, 1)
                pool.wait_ge(sel_ready, 2)
                views = ((to_heads, [[2 * HEAD_DIM, NP], [-HEAD_DIM, 2 * NP]], 1),
                         (from_heads, [[2 * HEAD_DIM, NP], [1, P]], -HEAD_DIM))
                for v, pat, chan in views:
                    pool.affine_select(out=v, in_=v, compare_op=ALU.is_ge, fill=0.0, base=0, pattern=pat,
                                       channel_multiplier=chan).then_inc(sel_ready, 1)
                pool.wait_ge(sel_ready, 4)
                for v, pat, chan in views:
                    pool.affine_select(out=v, in_=v, compare_op=ALU.is_ge, fill=0.0, base=HEAD_DIM - 1,
                                       pattern=[[-st, n] for st, n in pat], channel_multiplier=-chan).then_inc(sel_ready, 1)
                for m in range(10):
                    split_lo(pool, g, Step(m), KA)
                for p in range(NP):
                    pool.wait_ge(ohi_ready, p + 1)
                    pool.tensor_tensor(g.or_lo[:, p, :], go[p % 2], g.or_hi[:, p, :].bitcast(F32), ALU.subtract).then_inc(olo_ready, 1)
                    split_lo(pool, g, Step(10 + p), KA if 10 + p < SB else KB)

                def low_merged(m, j):
                    pool.wait_ge(mhi_ready, m + 1)
                    pool.tensor_tensor(one(act_lo[:, bass.ds(m, 1), :]), merged[j], one(act_hi[:, bass.ds(m, 1), :].bitcast(F32)),
                                       ALU.subtract).then_inc(mlo_ready, 1)
                with pool.Fori(0, KD // 2 - 1) as i:
                    for j in range(2):
                        split_lo(pool, g, branch(i, j + 2), KB)
                        low_merged(i * 2 + j, j)
                for j in range(2):
                    low_merged(KD - 2 + j, j)
                    split_lo(pool, g, outp(0, j), KD)
                with pool.Fori(0, KD // 2 - 1) as i:
                    for j in range(2):
                        split_lo(pool, g, outp(i, j + 2), KD)
                with pool.Fori(0, NBLK) as b:
                    with pool.Fori(0, HB) as i:
                        for j in range(2):
                            split_lo(pool, g, gate_up(b, i, j), KD)
                    with pool.Fori(0, KD // 2) as i:
                        for j in range(2):
                            split_lo(pool, g, down(b, i, j), HB)

            @block.vector
            def _(dve):
                def gate_attn(m):
                    dve.wait_ge(g.w_used, m + 1)
                    dve.wait_ge(mix_landed[m % 2], 16 * (m // 2 + 1))
                    dve.tensor_tensor(part[:, m, :], mix[m % 2], bank[m % 2][:, :], ALU.mult).then_inc(part_done, 1)
                for p in range(NP):
                    if p % 2 == 0:
                        dve.wait_ge(y_landed[p // 2], 32)
                    dve.tensor_tensor(wkv[:, p, :], wkv[:, p, :], y_back[:, p, :], ALU.add).then_inc(w_ready, 1)
                for p in range(NP):
                    dve.wait_ge(mean_made, p + 1)
                    dve.scalar_tensor_tensor(out=wkv[:, p, :], in0=bank[4 + p % 2][:, :], scalar=-1.0 / HEAD_DIM, in1=wkv[:, p, :],
                                             op0=ALU.mult, op1=ALU.add).then_inc(d_ready, 1)
                for m in range(4):
                    gate_attn(m)
                dve.wait_ge(var_made, NP)
                dve.tensor_scalar(gs, bank[6][0:2 * NP, :], 1.0 / HEAD_DIM, GN_EPS, ALU.mult, ALU.add).then_inc(gs_done, 1)
                glinks = [0]

                def glink(ins):
                    ins.then_inc(gchain, 1)
                    glinks[0] += 1
                    dve.wait_ge(gchain, glinks[0])
                dve.wait_ge(groot, 1)
                rsqrt_newton(glink, dve, gy, gt, gs)
                dve.tensor_tensor(gy, gy, gt, ALU.mult).then_inc(gy_ready, 1)
                for m in range(4, 8):
                    gate_attn(m)
                dve.wait_ge(rest_landed, 32)
                for p in range(NP):
                    dve.wait_ge(bc_made, p + 1)
                    dve.scalar_tensor_tensor(out=wkv[:, p, :], in0=wkv[:, p, :], scalar=param(g, "lnw", p), in1=bank[4 + p % 2][:, :],
                                             op0=ALU.mult, op1=ALU.mult).then_inc(gn_chain, 1)
                    dve.wait_ge(gn_chain, p + 1)
                    dve.scalar_tensor_tensor(out=wkv[:, p, :], in0=wkv[:, p, :], scalar=param(g, "lnb", p), in1=bonus[:, p, :],
                                             op0=ALU.add, op1=ALU.add).then_inc(gchain, 1)
                    glinks[0] += 1
                    dve.wait_ge(gchain, glinks[0])
                    if p >= 2:
                        dve.wait_ge(olo_ready, p - 1)
                    dve.tensor_tensor(go[p % 2], wkv[:, p, :], gate[:, p, :], ALU.mult).then_inc(go_ready, 1)
                    gate_attn(8 + p)
                with dve.Fori(0, KD // 2) as i:
                    for j in range(2):
                        dve.wait_ge(g.w_used, branch(i, j).count())
                        dve.wait_ge(mix_landed[j], i * 16 + (16 * (KD // 2) + 16))
                        dve.tensor_tensor(mix[j], mix[j], bank[2 + j][:, :], ALU.mult).then_inc(part_ready, 1)
                        dve.wait_ge(part_ready, i * 2 + (j + 1))
                        dve.wait_ge(mlo_ready, i * 2)
                        dve.tensor_tensor(merged[j], one(part[:, bass.ds(i * 2 + j, 1), :]), mix[j], ALU.add).then_inc(merged_ready, 1)
                dve.memset(sq_sum, 0.0).then_inc(chain, 1)
                dve.wait_ge(chain, 1)
                with dve.Fori(0, KD // 2) as i:
                    for j in range(2):
                        dve.wait_ge(g.w_used, outp(i, j).count())
                        dve.wait_ge(xin_landed[j], i * 16 + 16)
                        dve.tensor_tensor(one(x2[:, bass.ds(i * 2 + j, 1), :]), bank[4 + j][:, :], xin[j], ALU.add).then_inc(x2_ready, 1)
                        dve.wait_ge(sq_ready, i * 2 + (j + 1))
                        dve.wait_ge(sq_added, i * 2 + j)
                        dve.tensor_tensor(sq_sum, sq_sum, sq[j], ALU.add).then_inc(sq_added, 1)
                links = [1]

                def link(ins):
                    ins.then_inc(chain, 1)
                    links[0] += 1
                    dve.wait_ge(chain, links[0])
                dve.wait_ge(sq_summed, 1)
                dve.tensor_scalar(s_sb, bank[2][:, :], 1.0 / D_MODEL, RMS_EPS, ALU.mult, ALU.add).then_inc(s_ready, 1)
                dve.wait_ge(root, 1)
                rsqrt_newton(link, dve, y, t_sb, s_sb)
                link(dve.tensor_tensor(y, y, t_sb, ALU.mult))

                def normed(k):
                    if k >= 2:
                        dve.wait_ge(h2lo_ready, k - 1)
                    dve.scalar_tensor_tensor(out=h2f[k % 2], in0=x2[:, k, :], scalar=param(g, "norm2", k), in1=y,
                                             op0=ALU.mult, op1=ALU.mult).then_inc(h2_ready, 1)
                normed(0)
                for k in range(KD):
                    if k + 1 < KD:
                        normed(k + 1)
                    dve.wait_ge(h2hi_ready, k + 1)
                    dve.tensor_tensor(act_lo[:, k, :], h2f[k % 2], act_hi[:, k, :].bitcast(F32), ALU.subtract).then_inc(h2lo_ready, 1)
                with dve.Fori(0, NBLK) as b:
                    with dve.Fori(0, HB) as i:
                        dve.wait_ge(sig_ready, b * HB + i + 1)
                        dve.tensor_tensor(t_sb, sig, bank[6][:, :], ALU.mult).then_inc(gs_ready, 1)
                        dve.wait_ge(g.w_used, gate_up(b, i, 1).count())
                        dve.wait_ge(gs_ready, b * HB + i + 1)
                        dve.tensor_tensor(act_f, t_sb, bank[7][:, :], ALU.mult).then_inc(hid_ready, 1)
                        dve.wait_ge(hhi_ready, b * HB + i + 1)
                        dve.tensor_tensor(one(hid_lo[:, bass.ds(i, 1), :]), act_f, one(hid_hi[:, bass.ds(i, 1), :].bitcast(F32)),
                                          ALU.subtract).then_inc(hlo_ready, 1)
                    with dve.Fori(0, KD // 2) as i:
                        for j in range(2):
                            dve.wait_ge(g.w_used, down(b, i, j).count())
                            x = one(x2[:, bass.ds(i * 2 + j, 1), :])
                            dve.tensor_tensor(x, x, bank[j][:, :], ALU.add).then_inc(x2_ready, 1)
                for n in range(KD):
                    dve.wait_ge(turned, n + 1)
                    dve.tensor_copy(plain[:, n, :], bank[2 + n % 2][:, :]).then_inc(staged, 1)


def build(nc, a, out):
    g = Shared()
    with ExitStack() as ctx:
        zt = nc.dram_tensor("zt", [ROW_END, SEQ], F32, kind="Internal").ap()
        yt = nc.dram_tensor("yt", [2, RW, SEQ], F32, kind="Internal").ap()
        xt = nc.dram_tensor("xt", [D_MODEL, SEQ], F32, kind="Internal").ap()
        sb = lambda n, s, d=F32: ctx.enter_context(nc.sbuf_tensor(n, s, d))
        g.ident = sb("ident", [P, P])
        g.head_ones = sb("head_ones", [P, P])
        g.all_ones = sb("all_ones", [P, P])
        g.params = sb("params", [P, N_PARAM])
        with nc.cleanup_on_exit(), ExitStack() as c1:
            weight_stream(nc, c1, g)
            g.h_hi = c1.enter_context(nc.sbuf_tensor("h_hi", [P, KD, SEQ], F32R))
            g.h_lo = c1.enter_context(nc.sbuf_tensor("h_lo", [P, KD, SEQ], F32R))
            phase_setup(nc, g, a, xt)
            phase_project(nc, g, a, zt)
        n_oa = ATTN_HPG * HEAD_DIM // P
        oa, g.after_oa = two_faced(nc, ctx, "oa", [P, 2 * n_oa, SEQ])
        g.oa_hi, g.oa_lo = oa[:, 0:n_oa, :], oa[:, n_oa:2 * n_oa, :]
        with ExitStack() as c2:
            g.seg, g.same, g.lvl = (c2.enter_context(nc.sbuf_tensor(n, shape, F32)) for n, shape in (
                ("seg", [P, NQ * CH]), ("same", [P, LEVELS + 2, P]), ("lvl", [P, LEVELS + 1, P])))
            g.tri = [c2.enter_context(nc.sbuf_tensor(f"tri{z}", [P, 2 * P], F32)) for z in range(2)]
            with nc.cleanup_on_exit():
                phase_attention(nc, g, zt)
            with nc.cleanup_on_exit():
                phase_scan(nc, g, zt, yt)
        orw, g.x2 = two_faced(nc, ctx, "orw", [P, KD, SEQ])
        g.or_hi, g.or_lo = orw[:, 0:NPAIR, :], orw[:, NPAIR:KD, :]
        weight_stream(nc, ctx, g, "_b")
        act, g.act_plain = two_faced(nc, ctx, "act", [P, 2 * KD, SEQ])
        g.act_hi, g.act_lo = act[:, 0:KD, :], act[:, KD:2 * KD, :]
        phase_output(nc, g, a, zt, yt, xt, out)


NAMES = ("x", "norm1_w", "w_in", "b_gate", "q_norm_w", "k_norm_w", "shift_mu_prev", "shift_mu_next", "decay_w0", "decay_w2",
         "iclr_a0", "iclr_a2", "gate_g2", "k_k", "k_a", "r_k", "ln_x_w", "ln_x_b", "w_branch_attn", "w_branch_rwkv", "w_out",
         "norm2_w", "w_ffn_gate", "w_ffn_up", "w_ffn_down")


def kernel(**inputs):
    import numpy as _np
    import concourse.bacc as _bacc
    from concourse import mybir as _mybir
    from concourse.bass_utils import run_bass_kernel_spmd as _run

    nc = _bacc.Bacc("TRN2", target_bir_lowering=False, num_devices=1)
    arrays, a = {}, {}
    for name in NAMES:
        v = _np.ascontiguousarray(inputs[name])
        arrays[f"in_{name}_dram"] = v
        a[name] = nc.dram_tensor(f"in_{name}_dram", v.shape, _mybir.dt.from_np(v.dtype), kind="ExternalInput").ap()
    out = nc.dram_tensor("out_0_dram", (1, SEQ, D_MODEL), _mybir.dt.float32, kind="ExternalOutput").ap()
    build(nc, a, out)
    r = _run(nc, [arrays], core_ids=[0])
    return r.results[0]["out_0_dram"]
```
